# Optimizing a Trainium2 kernel written in Bass

```python
import jax, jax.numpy as jnp
from jax import lax
import numpy as np

D_MODEL = 1024
BATCH = 1
SEQ = 1024
DEPTH = 1

N_META = 16
D_CONV = D_MODEL
CONV_WIDTH = 31
HG_HEADS = 8
HG_DK = 128
HG_DV = D_MODEL // HG_HEADS
D_HK = HG_HEADS * HG_DK
D_HV = HG_HEADS * HG_DV
CHUNK = 64
EPS = 1e-6
SPLIT_SIZES = (D_CONV, D_CONV, D_CONV, D_HK, D_HK, D_HV, D_HV, D_MODEL, D_MODEL)
D_IN = D_CONV * 3 + D_HK * 2 + D_HV * 2 + D_MODEL * 2


def rmsnorm(x, g):
    xf = x.astype(jnp.float32)
    y = xf * lax.rsqrt(jnp.mean(xf * xf, axis=-1, keepdims=True) + EPS)
    return (y * g.astype(jnp.float32)).astype(x.dtype)

def layernorm(x, g, b):
    xf = x.astype(jnp.float32)
    mu = jnp.mean(xf, axis=-1, keepdims=True)
    var = jnp.mean(jnp.square(xf - mu), axis=-1, keepdims=True)
    y = (xf - mu) * lax.rsqrt(var + EPS)
    return (y * g.astype(jnp.float32) + b.astype(jnp.float32)).astype(x.dtype)

def conformer_branch(u_a, u_b, z, conv_w, conv_b, ln_g, ln_b, w_out):
    a = u_a * jax.nn.sigmoid(u_b)
    c = lax.conv_general_dilated(
        a, conv_w[:, None, :].astype(a.dtype), window_strides=(1,),
        padding=[(CONV_WIDTH - 1, 0)],
        dimension_numbers=('NWC', 'WIO', 'NWC'),
        feature_group_count=D_CONV) + conv_b
    c = jax.nn.silu(layernorm(c, ln_g, ln_b))
    return (c * jax.nn.silu(z)) @ w_out

def hgrn2_branch(q_raw, f_raw, i_raw, g, lb, gnorm_g, w_out):
    bsz, seqlen, _ = q_raw.shape
    out_dtype = i_raw.dtype
    q = jax.nn.silu(q_raw.astype(jnp.float32))
    f = lb + (1.0 - lb) * jax.nn.sigmoid(f_raw.astype(jnp.float32))
    log_f = jnp.log(f)
    k = 1.0 - f
    v = i_raw.astype(jnp.float32)
    pad = (-seqlen) % CHUNK
    n_chunks = (seqlen + pad) // CHUNK

    def to_chunks(t, d):
        t = jnp.pad(t, ((0, 0), (pad, 0), (0, 0)))
        t = t.reshape(bsz, n_chunks, CHUNK, HG_HEADS, d)
        return jnp.transpose(t, (1, 0, 3, 2, 4))

    qc = to_chunks(q, HG_DK)
    kc = to_chunks(k, HG_DK)
    vc = to_chunks(v, HG_DV)
    bc = jnp.cumsum(to_chunks(log_f, HG_DK), axis=3)
    causal = jnp.tril(jnp.ones((CHUNK, CHUNK), dtype=bool))[None, None, :, :, None]

    def step(S, inp):
        qi, ki, vi, bi = inp
        o_inter = jnp.einsum('bhtk,bhkv->bhtv', qi * jnp.exp(bi), S)
        diff = bi[:, :, :, None, :] - bi[:, :, None, :, :]
        decay = jnp.exp(jnp.where(causal, diff, -jnp.inf))
        attn = jnp.einsum('bhtk,bhsk,bhtsk->bhts', qi, ki, decay)
        o_intra = jnp.einsum('bhts,bhsv->bhtv', attn, vi)
        b_last = bi[:, :, -1:, :]
        S_new = jnp.exp(b_last[:, :, 0, :])[..., None] * S + jnp.einsum(
            'bhsk,bhsv->bhkv', ki * jnp.exp(b_last - bi), vi)
        return S_new, o_inter + o_intra

    S0 = jnp.zeros((bsz, HG_HEADS, HG_DK, HG_DV), jnp.float32)
    _, o = lax.scan(step, S0, (qc, kc, vc, bc))
    o = jnp.transpose(o, (1, 0, 3, 2, 4)).reshape(bsz, n_chunks * CHUNK, HG_HEADS, HG_DV)
    o = o[:, pad:]
    o = o * lax.rsqrt(jnp.mean(o * o, axis=-1, keepdims=True) + EPS)
    o = o * gnorm_g.astype(jnp.float32).reshape(HG_HEADS, HG_DV)
    o = o.reshape(bsz, seqlen, D_HV).astype(out_dtype)
    return (o * jax.nn.silu(g)) @ w_out

def first_inputs(seed: int = 0) -> dict:
    key = jax.random.key(seed)
    ks = jax.random.split(key, 16)
    f32 = jnp.float32
    nrm = lambda k, shape, s: jax.random.normal(k, shape, f32) * s
    return {
        "x": nrm(ks[0], (BATCH, SEQ, D_MODEL), 1.0),
        "meta_tokens": nrm(ks[1], (N_META, D_MODEL), 1.0),
        "norm_g": 1.0 + nrm(ks[2], (DEPTH, D_MODEL), 0.02),
        "w_in": nrm(ks[3], (DEPTH, D_MODEL, D_IN), D_MODEL ** -0.5),
        "conv_w": nrm(ks[4], (DEPTH, CONV_WIDTH, D_CONV), CONV_WIDTH ** -0.5),
        "conv_b": nrm(ks[5], (DEPTH, D_CONV), 0.02),
        "ln_g": 1.0 + nrm(ks[6], (DEPTH, D_CONV), 0.02),
        "ln_b": nrm(ks[7], (DEPTH, D_CONV), 0.02),
        "w_conv_out": nrm(ks[8], (DEPTH, D_CONV, D_MODEL), D_CONV ** -0.5),
        "lb_logits": nrm(ks[9], (DEPTH + 1, D_HK), 0.5),
        "gnorm_g": 1.0 + nrm(ks[10], (DEPTH, D_HV), 0.02),
        "w_rec_out": nrm(ks[11], (DEPTH, D_HV, D_MODEL), D_HV ** -0.5),
        "w_out": nrm(ks[12], (DEPTH, D_MODEL, D_MODEL), D_MODEL ** -0.5),
        "final_g": 1.0 + nrm(ks[13], (D_MODEL,), 0.02),
    }

def first_block(x, meta_tokens, norm_g, w_in, conv_w, conv_b, ln_g, ln_b, w_conv_out,
              lb_logits, gnorm_g, w_rec_out, w_out, final_g):
    bsz = x.shape[0]
    meta = jnp.broadcast_to(meta_tokens.astype(x.dtype)[None], (bsz, N_META, D_MODEL))
    h_res = jnp.concatenate([meta, x], axis=1)
    lb_all = jnp.cumsum(jax.nn.softmax(lb_logits.astype(jnp.float32), axis=0), axis=0)
    split_idx = [int(v) for v in np.cumsum(SPLIT_SIZES)[:-1]]
    for l in range(DEPTH):
        h = rmsnorm(h_res, norm_g[l])
        proj = h @ w_in[l]
        glu_a, glu_b, z_conv, q, f, i, g_rec, m_conv, m_rec = jnp.split(proj, split_idx, axis=-1)
        y_conv = conformer_branch(glu_a, glu_b, z_conv, conv_w[l], conv_b[l],
                                  ln_g[l], ln_b[l], w_conv_out[l])
        y_rec = hgrn2_branch(q, f, i, g_rec, lb_all[l], gnorm_g[l], w_rec_out[l])
        merged = jax.nn.sigmoid(m_conv) * y_conv + jax.nn.sigmoid(m_rec) * y_rec
        h_res = h_res + merged @ w_out[l]
    return rmsnorm(h_res[:, N_META:], final_g)


_first_inputs = first_inputs


def first_inputs(seed=0):
    import zlib

    import numpy as np

    out = dict(_first_inputs(seed))
    spreads = {}
    factors = {'norm_g': 5.198,
     'conv_b': 7.996,
     'ln_g': 8.0,
     'ln_b': 8.0,
     'lb_logits': 3.279,
     'gnorm_g': 8.0,
     'final_g': 2.742}
    for name, (base, spread) in spreads.items():
        noise = np.random.default_rng([zlib.crc32(name.encode()), seed]).standard_normal(out[name].shape)
        drawn = base * np.exp(spread * noise) if base else spread * noise
        out[name] = __import__('jax').numpy.asarray(drawn.astype(out[name].dtype))
    for name, factor in factors.items():
        out[name] = (out[name] * factor).astype(out[name].dtype)
    return out


_narrow_inputs = first_inputs


def first_inputs(seed=0):

    out = dict(_narrow_inputs(seed))
    wider = {'ln_g': 5.31, 'ln_b': 5.58, 'gnorm_g': 4.03, 'final_g': 3.09}
    for name, times in wider.items():
        mean = out[name].mean()
        out[name] = (mean + times * (out[name] - mean)).astype(out[name].dtype)
    return out


LEFT_CHUNKS = 8
BAND = (LEFT_CHUNKS + 1) * CHUNK
ATT_HEAD_DIM = 64
ATT_HEADS = D_MODEL // 128
ATT_WIDTH = ATT_HEADS * ATT_HEAD_DIM
REL_CLIP = 128
CONV_CH = D_MODEL // 4
CONV_K = 3
SG_WIDTH = D_MODEL // 4
SG_GROUPS = 4
SG_GROUP_DIM = SG_WIDTH // SG_GROUPS
SG_BLOCK = 128
GROUP_DIM = 64
MIX_WIDTH = ATT_WIDTH + CONV_CH + SG_WIDTH
N_GROUPS = MIX_WIDTH // GROUP_DIM
IN_WIDTH = 3 * ATT_WIDTH + 3 * CONV_CH + 2 * SG_WIDTH
D_FF = 4 * D_MODEL


def rms_norm(x, g):
    xf = x.astype(jnp.float32)
    y = xf * lax.rsqrt(jnp.mean(xf * xf, axis=-1, keepdims=True) + EPS)
    return (y * g.astype(jnp.float32)).astype(x.dtype)

def layer_norm(x, g, b):
    xf = x.astype(jnp.float32)
    mu = jnp.mean(xf, axis=-1, keepdims=True)
    var = jnp.mean(jnp.square(xf - mu), axis=-1, keepdims=True)
    y = (xf - mu) * lax.rsqrt(var + EPS)
    return (y * g.astype(jnp.float32) + b.astype(jnp.float32)).astype(x.dtype)

def chunked_rel_attention(q, k, v, rel_bias):
    b, s, h, dh = q.shape
    n_c = s // CHUNK
    qc = q.reshape(b, n_c, CHUNK, h, dh)
    pad = ((0, 0), (LEFT_CHUNKS, 0), (0, 0), (0, 0), (0, 0))
    kp = jnp.pad(k.reshape(b, n_c, CHUNK, h, dh), pad)
    vp = jnp.pad(v.reshape(b, n_c, CHUNK, h, dh), pad)
    kb = jnp.stack([kp[:, j:j + n_c] for j in range(LEFT_CHUNKS + 1)], axis=2).reshape(b, n_c, BAND, h, dh)
    vb = jnp.stack([vp[:, j:j + n_c] for j in range(LEFT_CHUNKS + 1)], axis=2).reshape(b, n_c, BAND, h, dh)
    rel = jnp.arange(CHUNK)[:, None] + LEFT_CHUNKS * CHUNK - jnp.arange(BAND)[None, :]
    idx = jnp.clip(rel, -REL_CLIP, REL_CLIP) + REL_CLIP
    bias = rel_bias.astype(jnp.float32)[:, idx]
    key_chunk = jnp.arange(n_c)[:, None] - LEFT_CHUNKS + jnp.arange(BAND)[None, :] // CHUNK
    valid = key_chunk >= 0
    scores = jnp.einsum('bnqhd,bnkhd->bnhqk', qc, kb).astype(jnp.float32) * (dh ** -0.5)
    scores = scores + bias[None, None]
    scores = jnp.where(valid[None, :, None, None, :], scores, jnp.float32(-1e30))
    p = jax.nn.softmax(scores, axis=-1).astype(v.dtype)
    out = jnp.einsum('bnhqk,bnkhd->bnqhd', p, vb)
    return out.reshape(b, s, h * dh)

def gated_short_conv(bg, cg, xh, conv_w):
    z = cg * xh
    s = z.shape[1]
    zp = jnp.pad(z, ((0, 0), (CONV_K - 1, 0), (0, 0)))
    y = sum(zp[:, j:j + s] * conv_w[j] for j in range(CONV_K))
    return bg * y

def spatial_gating(u, v, ln_g, ln_b, sg_w, sg_b):
    b, s, _ = u.shape
    u = jax.nn.gelu(u, approximate=False)
    v = layer_norm(jax.nn.gelu(v, approximate=False), ln_g, ln_b)
    vb = v.reshape(b, s // SG_BLOCK, SG_BLOCK, SG_GROUPS, SG_GROUP_DIM)
    mask = jnp.tril(jnp.ones((SG_BLOCK, SG_BLOCK), dtype=sg_w.dtype))
    ws = sg_w * mask[None]
    mixed = jnp.einsum('gts,bnsgc->bntgc', ws, vb) + sg_b.T[None, None, :, :, None]
    return u * mixed.reshape(b, s, SG_WIDTH)

def second_inputs(seed: int = 0) -> dict:
    key = jax.random.key(seed)
    ks = jax.random.split(key, 16)
    f32 = jnp.float32
    nrm = lambda k, shp, sc: jax.random.normal(k, shp, f32) * sc
    return {
        "x": nrm(ks[0], (BATCH, SEQ, D_MODEL), 1.0),
        "mix_norm_g": 1.0 + nrm(ks[1], (DEPTH, D_MODEL), 0.02),
        "w_in": nrm(ks[2], (DEPTH, D_MODEL, IN_WIDTH), D_MODEL ** -0.5),
        "rel_bias": nrm(ks[3], (DEPTH, ATT_HEADS, 2 * REL_CLIP + 1), 0.1),
        "conv_w": nrm(ks[4], (DEPTH, CONV_K, CONV_CH), CONV_K ** -0.5),
        "sg_ln_g": 1.0 + nrm(ks[5], (DEPTH, SG_WIDTH), 0.02),
        "sg_ln_b": nrm(ks[6], (DEPTH, SG_WIDTH), 0.02),
        "sg_w": nrm(ks[7], (DEPTH, SG_GROUPS, SG_BLOCK, SG_BLOCK), 0.5 * SG_BLOCK ** -0.5),
        "sg_b": 1.0 + nrm(ks[8], (DEPTH, SG_GROUPS, SG_BLOCK), 0.02),
        "group_norm_g": 1.0 + nrm(ks[9], (DEPTH, MIX_WIDTH), 0.02),
        "w_out": nrm(ks[10], (DEPTH, MIX_WIDTH, D_MODEL), 0.5 * MIX_WIDTH ** -0.5),
        "mlp_norm_g": 1.0 + nrm(ks[11], (DEPTH, D_MODEL), 0.02),
        "w_up": nrm(ks[12], (DEPTH, D_MODEL, D_FF), D_MODEL ** -0.5),
        "w_down": nrm(ks[13], (DEPTH, D_FF, D_MODEL), 0.5 * D_FF ** -0.5),
        "final_norm_g": 1.0 + nrm(ks[14], (D_MODEL,), 0.02),
    }

def second_block(x, mix_norm_g, w_in, rel_bias, conv_w, sg_ln_g, sg_ln_b, sg_w, sg_b,
              group_norm_g, w_out, mlp_norm_g, w_up, w_down, final_norm_g):
    b, s, _ = x.shape
    cuts = np.cumsum([ATT_WIDTH, ATT_WIDTH, ATT_WIDTH, CONV_CH, CONV_CH, CONV_CH, SG_WIDTH])
    for l in range(DEPTH):
        n = rms_norm(x, mix_norm_g[l])
        proj = jnp.einsum('bsd,de->bse', n, w_in[l])
        q, k, v, bg, cg, xh, su, sv = jnp.split(proj, cuts, axis=-1)
        shp = (b, s, ATT_HEADS, ATT_HEAD_DIM)
        y_a = chunked_rel_attention(q.reshape(shp), k.reshape(shp), v.reshape(shp), rel_bias[l])
        y_b = gated_short_conv(bg, cg, xh, conv_w[l])
        y_c = spatial_gating(su, sv, sg_ln_g[l], sg_ln_b[l], sg_w[l], sg_b[l])
        mixed = jnp.concatenate([y_a, y_b, y_c], axis=-1)
        g = group_norm_g[l].reshape(N_GROUPS, GROUP_DIM)
        mixed = rms_norm(mixed.reshape(b, s, N_GROUPS, GROUP_DIM), g).reshape(b, s, MIX_WIDTH)
        x = x + jnp.einsum('bse,ed->bsd', mixed, w_out[l])
        hdn = jnp.einsum('bsd,df->bsf', rms_norm(x, mlp_norm_g[l]), w_up[l])
        hdn = jnp.square(jax.nn.relu(hdn))
        x = x + jnp.einsum('bsf,fd->bsd', hdn, w_down[l])
    return rms_norm(x, final_norm_g)


_first_inputs_2 = second_inputs


def second_inputs(seed=0):
    import zlib

    import numpy as np

    out = dict(_first_inputs_2(seed))
    spreads = {}
    factors = {'mix_norm_g': 3.411,
     'sg_ln_g': 8.0,
     'sg_ln_b': 8.0,
     'sg_b': 8.0,
     'group_norm_g': 6.056,
     'mlp_norm_g': 5.096,
     'final_norm_g': 2.876}
    for name, (base, spread) in spreads.items():
        noise = np.random.default_rng([zlib.crc32(name.encode()), seed]).standard_normal(out[name].shape)
        drawn = base * np.exp(spread * noise) if base else spread * noise
        out[name] = __import__('jax').numpy.asarray(drawn.astype(out[name].dtype))
    for name, factor in factors.items():
        out[name] = (out[name] * factor).astype(out[name].dtype)
    return out


_narrow_inputs_2 = second_inputs


def second_inputs(seed=0):

    out = dict(_narrow_inputs_2(seed))
    wider = {'sg_ln_g': 12.0, 'sg_ln_b': 12.0, 'sg_b': 12.0, 'final_norm_g': 3.25}
    for name, times in wider.items():
        mean = out[name].mean()
        out[name] = (mean + times * (out[name] - mean)).astype(out[name].dtype)
    return out


D_MIX = D_MODEL
D_MLSTM = D_MIX // 2
D_POOL = D_MIX - D_MLSTM
N_MLSTM_HEADS = 4
HEAD_DIM = D_MLSTM // N_MLSTM_HEADS
POOL_WINDOWS = (2, 4, 8, 16)
N_POOL_GROUPS = len(POOL_WINDOWS)
POOL_GROUP_DIM = D_POOL // N_POOL_GROUPS
CONV_WIDTH_3 = 4
D_FF_3 = 4 * D_MODEL
OFF_Q = 0
OFF_K = OFF_Q + D_MLSTM
OFF_V = OFF_K + D_MLSTM
OFF_G = OFF_V + D_MLSTM
OFF_O = OFF_G + 2 * N_MLSTM_HEADS
OFF_P = OFF_O + D_MLSTM
D_IN_3 = OFF_P + D_POOL
ALPHA = (2.0 * DEPTH) ** 0.25
BETA = (8.0 * DEPTH) ** -0.25
LN_EPS = 1e-5


def layer_norm_3(x, g, b):
    xf = x.astype(jnp.float32)
    mu = xf.mean(-1, keepdims=True)
    var = jnp.square(xf - mu).mean(-1, keepdims=True)
    return ((xf - mu) * lax.rsqrt(var + LN_EPS) * g.astype(jnp.float32) + b.astype(jnp.float32)).astype(x.dtype)

def causal_conv(x, w):
    S = x.shape[1]
    xp = jnp.pad(x, ((0, 0), (CONV_WIDTH_3 - 1, 0), (0, 0)))
    y = w[0] * xp[:, 0:S]
    for j in range(1, CONV_WIDTH_3):
        y = y + w[j] * xp[:, j:j + S]
    return y

def mlstm_chunkwise(q, k, v, i_pre, f_pre):
    B, S, H, Dh = q.shape
    NC = S // CHUNK

    def to_chunks(t):
        t = t.reshape((B, NC, CHUNK, H) + t.shape[3:])
        return jnp.moveaxis(t, 3, 1)

    q, k, v = to_chunks(q), to_chunks(k), to_chunks(v)
    i_pre = to_chunks(i_pre)
    logf = to_chunks(jax.nn.log_sigmoid(f_pre))
    a = jnp.cumsum(logf, axis=-1)
    g = a[..., -1]

    w = g[..., None] - a + i_pre
    m_loc = w.max(-1)
    e = jnp.exp(w - m_loc[..., None])
    C_loc = jnp.einsum('bhnl,bhnlv,bhnlk->bhnvk', e, v, k)
    n_loc = jnp.einsum('bhnl,bhnlk->bhnk', e, k)

    def step(carry, inp):
        C, n, m = carry
        g_c, m_c, C_c, n_c = inp
        m_new = jnp.maximum(g_c + m, m_c)
        s_old = jnp.exp(g_c + m - m_new)
        s_new = jnp.exp(m_c - m_new)
        C_new = s_old[..., None, None] * C + s_new[..., None, None] * C_c
        n_new = s_old[..., None] * n + s_new[..., None] * n_c
        return (C_new, n_new, m_new), (C, n, m)

    init = (jnp.zeros((B, H, Dh, Dh), jnp.float32),
            jnp.zeros((B, H, Dh), jnp.float32),
            jnp.zeros((B, H), jnp.float32))
    xs = (jnp.moveaxis(g, 2, 0), jnp.moveaxis(m_loc, 2, 0),
          jnp.moveaxis(C_loc, 2, 0), jnp.moveaxis(n_loc, 2, 0))
    _, (C_prev, n_prev, m_prev) = lax.scan(step, init, xs)
    C_prev = jnp.moveaxis(C_prev, 0, 2)
    n_prev = jnp.moveaxis(n_prev, 0, 2)
    m_prev = jnp.moveaxis(m_prev, 0, 2)

    causal = jnp.tril(jnp.ones((CHUNK, CHUNK), dtype=bool))
    Dlog = a[..., :, None] - a[..., None, :] + i_pre[..., None, :]
    Dlog = jnp.where(causal, Dlog, -jnp.inf)
    m_inter = a + m_prev[..., None]
    m_t = jnp.maximum(m_inter, Dlog.max(-1))
    P = jnp.exp(Dlog - m_t[..., None])
    s_inter = jnp.exp(m_inter - m_t)
    qk = jnp.einsum('bhnld,bhnsd->bhnls', q, k) * P
    num = (jnp.einsum('bhnls,bhnsv->bhnlv', qk, v)
           + s_inter[..., None] * jnp.einsum('bhnvk,bhnlk->bhnlv', C_prev, q))
    den = qk.sum(-1) + s_inter * jnp.einsum('bhnk,bhnlk->bhnl', n_prev, q)
    h = num / jnp.maximum(jnp.abs(den), jnp.exp(-m_t))[..., None]
    return jnp.moveaxis(h, 1, 3).reshape(B, S, H * Dh)

def multiscale_pool(p, w_pool, scale):
    B, S, _ = p.shape
    pf = p.astype(jnp.float32)
    cs = jnp.cumsum(pf, axis=1)
    count = jnp.arange(1, S + 1, dtype=jnp.float32)[:, None]
    outs = []
    for gi, win in enumerate(POOL_WINDOWS):
        lo, hi = gi * POOL_GROUP_DIM, (gi + 1) * POOL_GROUP_DIM
        c = cs[..., lo:hi]
        lagged = jnp.pad(c[:, :S - win], ((0, 0), (win, 0), (0, 0)))
        mean = (c - lagged) / jnp.minimum(count, float(win))
        outs.append(mean - pf[..., lo:hi])
    d = jnp.stack(outs, axis=2)
    y = jnp.einsum('bsgc,gcd->bsgd', d, w_pool.astype(jnp.float32)).reshape(B, S, D_POOL)
    return (y * scale.astype(jnp.float32)).astype(p.dtype)

def hybrid_mixer(x, w_in, b_gate, w_conv, hn_g, w_pool, pool_scale, w_out):
    B, S, _ = x.shape
    u = x @ w_in
    qk = jax.nn.silu(causal_conv(u[..., OFF_Q:OFF_V], w_conv)).astype(jnp.float32)
    q = qk[..., :D_MLSTM].reshape(B, S, N_MLSTM_HEADS, HEAD_DIM)
    k = qk[..., D_MLSTM:].reshape(B, S, N_MLSTM_HEADS, HEAD_DIM) * (HEAD_DIM ** -0.5)
    v = u[..., OFF_V:OFF_G].astype(jnp.float32).reshape(B, S, N_MLSTM_HEADS, HEAD_DIM)
    gates = (u[..., OFF_G:OFF_O] + b_gate).astype(jnp.float32)
    i_pre = gates[..., :N_MLSTM_HEADS]
    f_pre = gates[..., N_MLSTM_HEADS:]
    h = mlstm_chunkwise(q, k, v, i_pre, f_pre).reshape(B, S, N_MLSTM_HEADS, HEAD_DIM)
    mu = h.mean(-1, keepdims=True)
    var = jnp.square(h - mu).mean(-1, keepdims=True)
    h = ((h - mu) * lax.rsqrt(var + LN_EPS)).reshape(B, S, D_MLSTM) * hn_g.astype(jnp.float32)
    y_m = (jax.nn.sigmoid(u[..., OFF_O:OFF_P].astype(jnp.float32)) * h).astype(x.dtype)
    y_p = multiscale_pool(u[..., OFF_P:D_IN_3], w_pool, pool_scale)
    return jnp.concatenate([y_m, y_p], axis=-1) @ w_out

def squared_relu_mlp(x, w1, w2):
    return jnp.square(jax.nn.relu(x @ w1)) @ w2

def third_inputs(seed: int = 0) -> dict:
    key = jax.random.key(seed)
    ks = jax.random.split(key, 16)
    L = DEPTH
    nrm = jax.random.normal
    x = nrm(ks[0], (BATCH, SEQ, D_MODEL), jnp.float32)
    w_in = nrm(ks[1], (L, D_MODEL, D_IN_3), jnp.float32) * D_MODEL ** -0.5
    b_i = 0.1 * nrm(ks[2], (L, N_MLSTM_HEADS), jnp.float32)
    b_f = jnp.linspace(3.0, 6.0, N_MLSTM_HEADS, dtype=jnp.float32)[None] + 0.1 * nrm(ks[3], (L, N_MLSTM_HEADS), jnp.float32)
    b_gate = jnp.concatenate([b_i, b_f], axis=-1)
    w_conv = nrm(ks[4], (L, CONV_WIDTH_3, 2 * D_MLSTM), jnp.float32) * CONV_WIDTH_3 ** -0.5
    hn_g = 1.0 + 0.02 * nrm(ks[5], (L, D_MLSTM), jnp.float32)
    w_pool = nrm(ks[6], (L, N_POOL_GROUPS, POOL_GROUP_DIM, POOL_GROUP_DIM), jnp.float32) * POOL_GROUP_DIM ** -0.5
    pool_scale = 1.0 + 0.02 * nrm(ks[7], (L, D_POOL), jnp.float32)
    w_out = nrm(ks[8], (L, D_MIX, D_MODEL), jnp.float32) * (D_MIX ** -0.5) * BETA
    ln1_g = 1.0 + 0.02 * nrm(ks[9], (L, D_MODEL), jnp.float32)
    ln1_b = 0.02 * nrm(ks[10], (L, D_MODEL), jnp.float32)
    w_ff1 = nrm(ks[11], (L, D_MODEL, D_FF_3), jnp.float32) * D_MODEL ** -0.5
    w_ff2 = nrm(ks[12], (L, D_FF_3, D_MODEL), jnp.float32) * (D_FF_3 ** -0.5) * BETA
    ln2_g = 1.0 + 0.02 * nrm(ks[13], (L, D_MODEL), jnp.float32)
    ln2_b = 0.02 * nrm(ks[14], (L, D_MODEL), jnp.float32)
    return {"x": x, "w_in": w_in, "b_gate": b_gate, "w_conv": w_conv, "hn_g": hn_g,
            "w_pool": w_pool, "pool_scale": pool_scale, "w_out": w_out,
            "ln1_g": ln1_g, "ln1_b": ln1_b, "w_ff1": w_ff1, "w_ff2": w_ff2,
            "ln2_g": ln2_g, "ln2_b": ln2_b}

def third_block(x, w_in, b_gate, w_conv, hn_g, w_pool, pool_scale, w_out,
              ln1_g, ln1_b, w_ff1, w_ff2, ln2_g, ln2_b):
    for l in range(DEPTH):
        mix = hybrid_mixer(x, w_in[l], b_gate[l], w_conv[l], hn_g[l], w_pool[l], pool_scale[l], w_out[l])
        x = layer_norm_3(ALPHA * x + mix, ln1_g[l], ln1_b[l])
        x = layer_norm_3(ALPHA * x + squared_relu_mlp(x, w_ff1[l], w_ff2[l]), ln2_g[l], ln2_b[l])
    return x


_first_inputs_3 = third_inputs


def third_inputs(seed=0):
    import zlib

    import numpy as np

    out = dict(_first_inputs_3(seed))
    spreads = {}
    factors = {'hn_g': 8.0,
     'pool_scale': 8.0,
     'ln1_g': 2.729,
     'ln1_b': 2.761,
     'ln2_g': 2.741,
     'ln2_b': 2.873}
    for name, (base, spread) in spreads.items():
        noise = np.random.default_rng([zlib.crc32(name.encode()), seed]).standard_normal(out[name].shape)
        drawn = base * np.exp(spread * noise) if base else spread * noise
        out[name] = __import__('jax').numpy.asarray(drawn.astype(out[name].dtype))
    for name, factor in factors.items():
        out[name] = (out[name] * factor).astype(out[name].dtype)
    return out


_narrow_inputs_3 = third_inputs


def third_inputs(seed=0):

    out = dict(_narrow_inputs_3(seed))
    wider = {'hn_g': 5.59, 'pool_scale': 3.61, 'ln2_g': 3.07, 'ln2_b': 3.08}
    for name, times in wider.items():
        mean = out[name].mean()
        out[name] = (mean + times * (out[name] - mean)).astype(out[name].dtype)
    return out


def setup_inputs(seed=0):
    out = dict(first_inputs(seed))
    for name, value in second_inputs(seed + 1).items():
        if name != "x":
            out[name + "_2"] = value
    for name, value in third_inputs(seed + 2).items():
        if name != "x":
            out[name + "_3"] = value
    return out


def reference(
    x, meta_tokens, norm_g, w_in, conv_w, conv_b, ln_g, ln_b, w_conv_out, lb_logits, gnorm_g,
    w_rec_out, w_out, final_g, mix_norm_g_2, w_in_2, rel_bias_2, conv_w_2, sg_ln_g_2, sg_ln_b_2,
    sg_w_2, sg_b_2, group_norm_g_2, w_out_2, mlp_norm_g_2, w_up_2, w_down_2, final_norm_g_2,
    w_in_3, b_gate_3, w_conv_3, hn_g_3, w_pool_3, pool_scale_3, w_out_3, ln1_g_3, ln1_b_3,
    w_ff1_3, w_ff2_3, ln2_g_3, ln2_b_3,
):
    x = first_block(
        x, meta_tokens, norm_g, w_in, conv_w, conv_b, ln_g, ln_b, w_conv_out, lb_logits,
        gnorm_g, w_rec_out, w_out, final_g,
    )
    x = second_block(
        x, mix_norm_g_2, w_in_2, rel_bias_2, conv_w_2, sg_ln_g_2, sg_ln_b_2, sg_w_2, sg_b_2,
        group_norm_g_2, w_out_2, mlp_norm_g_2, w_up_2, w_down_2, final_norm_g_2,
    )
    return third_block(
        x, w_in_3, b_gate_3, w_conv_3, hn_g_3, w_pool_3, pool_scale_3, w_out_3, ln1_g_3,
        ln1_b_3, w_ff1_3, w_ff2_3, ln2_g_3, ln2_b_3,
    )


_drawn_inputs = setup_inputs


def setup_inputs(seed=0):
    import zlib

    import numpy as np

    out = dict(_drawn_inputs(seed))
    spreads = {}
    factors = {'rel_bias_2': 2.765}
    for name, (base, spread) in spreads.items():
        noise = np.random.default_rng([zlib.crc32(name.encode()), seed]).standard_normal(out[name].shape)
        drawn = base * np.exp(spread * noise) if base else spread * noise
        out[name] = __import__('jax').numpy.asarray(drawn.astype(out[name].dtype))
    for name, factor in factors.items():
        out[name] = (out[name] * factor).astype(out[name].dtype)
    return out
```

```python
from contextlib import ExitStack

import numpy as np

import concourse.bass as bass
from concourse import mybir

F = mybir.dt.float32
FR = mybir.dt.float32r
I32 = mybir.dt.int32
ACT = mybir.ActivationFunctionType
ALU = mybir.AluOpType
AX = mybir.AxisListType.X

P = 128
D_MODEL = 1024
T = 1024
KT = 8
META = 16
TM = T + META
TAPS = 31
HIST = TAPS - 1
EPS = 1e-6
LN_EPS = 1e-5
HALVES = (64, 32, 16, 8, 4, 2, 1)
ALPHA = 2.0 ** 0.25
NEG = -1e30
BAND = 640

VECS = {}
_n = 0
for _name, _w in (("norm_g", 8), ("conv_w", 8 * TAPS), ("conv_b", 8), ("ln_g", 8), ("ln_b", 8), ("lb0", 8),
                  ("lb1", 8), ("gnorm_g", 8), ("final_g", 8), ("mix_g", 8), ("cw2", 6), ("gg2", 8),
                  ("mlp_g2", 8), ("fin_g2", 8), ("cw3", 32), ("hn_g", 4), ("pscale", 4), ("ln1_g", 8),
                  ("ln1_b", 8), ("ln2_g", 8), ("ln2_b", 8), ("b_i", 1), ("b_f", 1)):
    VECS[_name] = (_n, _w)
    _n += _w
NVEC = _n
CONSTS = {}
_n = 0
for _name, _w in (("ident", 128), ("ones", 128), ("selA8", 64), ("selB8", 1024), ("selA4", 32),
                  ("selB4", 512), ("tri", 128), ("tril_neg", 128),
                  ("inv", 16)):
    CONSTS[_name] = (_n, _w)
    _n += _w
NCONST = _n


class Lane:

    def __init__(self, eng, sem):
        self.eng, self.sem, self.count, self.seen = eng, sem, 0, {}

    def after(self, *tokens):
        for t in tokens:
            if t is None:
                continue
            if isinstance(t, list):
                self.after(*t)
                continue
            sem, value = t
            if self.seen.get(id(sem), 0) < value:
                self.eng.wait_ge(sem, value)
                self.seen[id(sem)] = value
        return self.eng

    def mark(self, instruction):
        self.count += 1
        instruction.then_inc(self.sem, 1)
        return (self.sem, self.count)


class Port:

    def __init__(self, lane, sem):
        self.lane, self.sem, self.count = lane, sem, 0

    def start(self, out, in_, *tokens):
        if self.count:
            self.lane.after((self.sem, self.count))
        self.lane.after(*tokens)
        self.count += 16
        self.lane.eng.dma_start(out, in_).then_inc(self.sem, 16)
        return (self.sem, self.count)


class Slot:

    def __init__(self, ap):
        self.ap, self.free = ap, []


class Ring:
    def __init__(self, slots):
        self.slots, self.n = slots, 0

    def take(self):
        s = self.slots[self.n % len(self.slots)]
        self.n += 1
        return s


def program(nc, A, stage=99):
    ctx = ExitStack()

    def sem(name):
        return ctx.enter_context(nc.semaphore(name))

    PE = Lane(nc.tensor, sem("pe_done"))
    VE = Lane(nc.vector, sem("dve_done"))
    SE = Lane(nc.scalar, sem("act_done"))
    GP = Lane(nc.gpsimd, sem("pool_done"))
    SP = Lane(nc.sync, sem("sp_done"))

    def sb(name, shape, dt=F, scope=ctx):
        return scope.enter_context(nc.sbuf_tensor(name, shape, dt))

    raw = sb("raw", [P, 2, KT * 128])
    wh = sb("wh", [P, 2, KT * 128], FR)
    wl = sb("wl", [P, 2, KT * 128], FR)
    hh = sb("hh", [P, KT, TM], FR)
    hl = sb("hl", [P, KT, TM], FR)
    vec = sb("vec", [P, NVEC])
    cst = sb("cst", [P, NCONST])
    psum = ctx.enter_context(nc.psum_tensor("psum", [P, 8, 512], F))

    def V(name, i=0, n=1):
        return vec[:, VECS[name][0] + i:VECS[name][0] + i + n]

    def C(name, parts=P):
        a, w = CONSTS[name]
        return cst[0:parts, a:a + w]

    ident, ones = C("ident"), C("ones")
    selA8 = C("selA8").rearrange("p (h m) -> p h m", h=8)
    selB8 = C("selB8", 8).rearrange("p (h m) -> p h m", h=8)
    selA4 = C("selA4").rearrange("p (t m) -> p t m", t=4)
    selB4 = C("selB4", 8).rearrange("p (t m) -> p t m", t=4)

    pairs = Ring([Slot(psum[:, 0:2, :]), Slot(psum[:, 2:4, :])])
    small = Slot(psum[:, 4, :])
    aux = Ring([Slot(psum[:, 5, :]), Slot(psum[:, 6, :]), Slot(psum[:, 7, :])])

    load_port = Ring([Port(SP, sem(f"ld{i}")) for i in range(4)])
    store_port = Ring([Port(SP, sem(f"st{i}")) for i in range(4)])
    w_port = [Port(SP, sem(f"wt{i}")) for i in range(2)]
    stores = []

    def load(out, in_, *tokens):
        return load_port.take().start(out, in_, *tokens)

    def store(out, in_, *tokens):
        t = store_port.take().start(out, in_, *tokens)
        stores.append(t)
        return t

    def act(out, in_, func, *tokens, **kw):
        return SE.mark(SE.after(*tokens).activation(out, in_, func, **kw))

    def tt(out, a, b, op, *tokens, lane=None):
        lane = lane or VE
        return lane.mark(lane.after(*tokens).tensor_tensor(out, a, b, op))

    def ts(out, a, s1, s2, op0, op1, *tokens):
        if s2 is None:
            return VE.mark(VE.after(*tokens).tensor_scalar(out, a, s1, None, op0))
        return VE.mark(VE.after(*tokens).tensor_scalar(out, a, s1, s2, op0, op1))

    def stt(out, a, s, b, op0, op1, *tokens):
        return VE.mark(VE.after(*tokens).scalar_tensor_tensor(out, a, s, b, op0, op1))

    def copy(out, in_, *tokens):
        return VE.mark(VE.after(*tokens).tensor_copy(out, in_))

    def recip(out, in_, *tokens):
        return VE.mark(VE.after(*tokens).reciprocal(out, in_))

    def zero(out, value, *tokens):
        return VE.mark(VE.after(*tokens).memset(out, value))

    def fp(ap):
        return ap.bitcast(F)

    jobs = []

    def pump(n=1):
        for _ in range(n):
            if not jobs:
                return
            try:
                next(jobs[0])
            except StopIteration:
                jobs.pop(0)

    def drain_jobs():
        while jobs:
            pump()

    def finish(job):
        while job in jobs:
            pump()

    NSLAB = A["wts"].shape[0]
    raw_free = [[], []]
    w_free = [[], []]
    raw_got = {}
    w_got = {}

    def w_fetch(i):
        if i < NSLAB and i not in raw_got:
            raw_got[i] = w_port[i % 2].start(raw[:, i % 2, :], A["wts"][i], raw_free[i % 2])

    def w_split(i):
        if i < NSLAB and i not in w_got:
            w_fetch(i)
            s = i % 2
            a = act(wh[:, s, :], raw[:, s, :], ACT.Copy, raw_got[i], w_free[s])
            b = tt(wl[:, s, :], raw[:, s, :], fp(wh[:, s, :]), ALU.subtract, a, w_free[s], lane=GP)
            raw_free[s] = [a, b]
            w_got[i] = [a, b]

    slab_no = [0]

    def next_slab():
        i = slab_no[0]
        slab_no[0] += 1
        w_split(i)
        w_fetch(i + 1)
        w_split(i + 1)
        w_fetch(i + 2)
        return i

    h_ready = [[] for _ in range(KT)]
    h_free = [[] for _ in range(KT)]

    def three(i, k):
        s = i % 2
        a, b = wh[:, s, k * 128:(k + 1) * 128], wl[:, s, k * 128:(k + 1) * 128]
        return a, b

    def gemm_fm(meta=False, last=False, src=None, ready=None, nk=KT, koff=0, slab=None, base=0):
        own = slab is None
        i = next_slab() if own else slab
        srch, srcl = src or (hh, hl)
        ready = h_ready if ready is None else ready
        off = META if src is None else 0
        pr = pairs.take()
        PE.after(w_got[i], pr.free)
        if meta:
            PE.after(small.free)
        frees = []
        for k in range(nk):
            PE.after(ready[k])
            a, b = three(i, k + base)
            n = 0
            for w, x in ((a, srch), (b, srch), (a, srcl)):
                first, final = k == 0 and n == 0, k == nk - 1 and n == 2
                for j in range(2):
                    ins = nc.tensor.matmul(pr.ap[:, j, :], w, x[:, k, off + j * 512:off + (j + 1) * 512],
                                           start=first, stop=final)
                if meta:
                    ins = nc.tensor.matmul(small.ap[:, 0:META], w, x[:, k, 0:META], start=first, stop=final)
                n += 1
            if last and k < nk - 1:
                frees.append([PE.mark(ins)])
            if k < nk - 1:
                pump()
        done = PE.mark(ins)
        frees.append([done])
        if own:
            w_free[i % 2] = [done]
        if last:
            for k in range(nk):
                h_free[k] = frees[k]
        pump()
        return pr, done, i

    def gemm_tm(meta=False, last=False):
        i = next_slab()
        pr = pairs.take()
        PE.after(w_got[i], pr.free, *h_ready)
        if meta:
            PE.after(small.free)
        tiles = [(pr.ap[:, t // 4, (t % 4) * 128:(t % 4) * 128 + 128], META + t * 128, 128) for t in range(8)]
        if meta:
            tiles.append((small.ap[0:META, 128:256], 0, META))
        for n, (out, c0, w) in enumerate(tiles):
            for k in range(KT):
                a, b = three(i, k)
                for q, (x, y) in enumerate(((hh, a), (hh, b), (hl, a))):
                    ins = nc.tensor.matmul(out, x[:, k, c0:c0 + w], y, start=(k == 0 and q == 0),
                                           stop=(k == KT - 1 and q == 2))
            if n < 8:
                pump()
        done = PE.mark(ins)
        w_free[i % 2] = [done]
        if last:
            for k in range(KT):
                h_free[k] = [done]
        return pr, done

    def put_h(k, src, *tokens, c0=META, n=T):
        a = act(hh[:, k, c0:c0 + n], src, ACT.Copy, *tokens, h_free[k])
        b = tt(hl[:, k, c0:c0 + n], src, fp(hh[:, k, c0:c0 + n]), ALU.subtract, a, *tokens)
        return [a, b]

    t_vec = load(vec[:, :], A["vec"])
    t_cst = load(cst[:, :], A["cst"])
    for ln in (PE, VE, SE, GP):
        ln.after(t_vec, t_cst)

    def flat(ap):
        return ap.rearrange("p a b -> p (a b)")

    O = B0 = sb("B0", [P, KT, T])
    s0 = ExitStack()
    X0 = sb("X0", [P, KT, TM], F, s0)
    sq0 = sb("sq0", [P, 2, TM], F, s0)
    R0 = sb("R0", [P, TM], F, s0)

    def sums(tiles, sqs, width, lhs=ones, square=True, rows=P, meta=False, tag=None):
        pr = pairs.take()
        PE.after(pr.free)
        if meta:
            PE.after(small.free)
        n = len(tiles)
        for t, (ap, toks) in enumerate(tiles):
            if square:
                q = sqs.take()
                a = act(q.ap[:, 0:width], ap, ACT.Square, toks, q.free)
                src = q.ap
            else:
                a, src = toks, ap
            PE.after(a)
            l = lhs(t) if callable(lhs) else lhs
            off = META if meta else 0
            for j in range(2):
                ins = nc.tensor.matmul(pr.ap[0:rows, j, :], l, src[:, off + j * 512:off + (j + 1) * 512],
                                       start=(t == 0), stop=(t == n - 1))
            if meta:
                ins = nc.tensor.matmul(small.ap[0:rows, 0:META], l, src[:, 0:META],
                                       start=(t == 0), stop=(t == n - 1))
            d = PE.mark(ins)
            if square:
                q.free = [d]
        return pr, d

    tx = [load(X0[:, k, :], A["xin"][k]) for k in range(KT)]
    sqr = Ring([Slot(sq0[:, i, :]) for i in range(2)])
    pr, d = sums([(X0[:, k, :], tx[k]) for k in range(KT)], sqr, TM, meta=True)
    a = act(R0[:, META:TM], flat(pr.ap), ACT.Sqrt, d, scale=1.0 / 1024, bias=EPS)
    b = act(R0[:, 0:META], small.ap[:, 0:META], ACT.Sqrt, d, scale=1.0 / 1024, bias=EPS)
    pr.free, small.free = [a], [b]
    r = recip(R0[:, :], R0[:, :], a, b)
    for k in range(KT):
        c = stt(X0[:, k, :], X0[:, k, :], V("norm_g", k), R0[:, :], ALU.mult, ALU.mult, r, tx[k], d)
        h_ready[k] = put_h(k, X0[:, k, :], c, c0=0, n=TM)
    s0_done = [t for k in range(KT) for t in h_ready[k]]
    s0.close()

    s1 = ExitStack()
    masks = sb("masks", [P, 7, 128], F, s1)
    rmask = sb("rmask", [P, TM], F, s1)
    fb = sb("fb", [P, 2, TM], F, s1)
    kb = sb("kb", [P, 2, TM], F, s1)
    qb = sb("qb", [P, 2, T], F, s1)
    vb = sb("vb", [P, 2, T], F, s1)
    vm = sb("vm", [META, 2, 128], F, s1)
    work = sb("work", [P, 4, TM], F, s1)
    Ab = sb("Ab", [P, T], F, s1)
    kdT = sb("kdT", [P, T], F, s1)
    kdm = sb("kdm", [META, 128], F, s1)
    Sb = sb("Sb", [P, T], F, s1)
    ebl = sb("ebl", [P, 2, 9], F, s1)
    lbv = sb("lbv", [P, 4, 8], F, s1)
    t_mask = load(flat(masks[:, :, :]), A["masks"], s0_done)
    z1 = zero(rmask[:, :], 1.0, s0_done)
    z2 = zero(rmask[:, META:TM].rearrange("p (c t) -> p c t", c=8)[:, :, 0:1], 0.0, z1)
    mx = tt(lbv[:, 0, :], V("lb0", 0, 8), V("lb1", 0, 8), ALU.max, s0_done)
    l0 = tt(lbv[:, 1, :], V("lb0", 0, 8), lbv[:, 0, :], ALU.subtract, mx)
    l1 = tt(lbv[:, 2, :], V("lb1", 0, 8), lbv[:, 0, :], ALU.subtract, mx)
    e0 = act(lbv[:, 1, :], lbv[:, 1, :], ACT.Exp, l0)
    e1 = act(lbv[:, 2, :], lbv[:, 2, :], ACT.Exp, l1)
    l2 = tt(lbv[:, 0, :], lbv[:, 1, :], lbv[:, 2, :], ALU.add, e0, e1)
    l3 = recip(lbv[:, 0, :], lbv[:, 0, :], l2)
    l4 = tt(lbv[:, 1, :], lbv[:, 1, :], lbv[:, 0, :], ALU.mult, l3)
    l5 = ts(lbv[:, 2, :], lbv[:, 1, :], -1.0, 1.0, ALU.mult, ALU.add, l4)
    lb_ready = [l4, l5]
    LB = lbv[:, 1, :]
    OML = lbv[:, 2, :]

    wk = Ring([Slot(work[:, i, :]) for i in range(4)])
    Aslot, kdslot, sslot = Slot(Ab), Slot(kdT), Slot(Sb)
    hd_free = [[], []]
    o_ready = [None] * 8
    A4 = lambda ap: ap.rearrange("p (c t) -> p c t", c=8)

    def half(ap, hs):
        v = ap.rearrange("p (n b) -> p n b", b=2 * hs)
        return v[:, :, 0:hs], v[:, :, hs:2 * hs]

    def hgrn(h, s, tf, tq, tv):
        f, kk, q, v = fb[:, s, :], kb[:, s, :], qb[:, s, :], vb[:, s, :]
        a = ts(f, f, OML[:, h:h + 1], LB[:, h:h + 1], ALU.mult, ALU.add, tf, lb_ready)
        tk = ts(kk, f, -1.0, 1.0, ALU.mult, ALU.add, a, hd_free[s])
        a = ts(f, f, 2.0 ** -63, None, ALU.max, None, a, tk)
        yield
        a = act(f, f, ACT.Ln, a)
        w = wk.take()
        cum = w.ap
        tb = VE.mark(VE.after(a, z2, w.free).tensor_tensor_scan(cum, rmask[:, :], f, 0.0, ALU.mult, ALU.add))
        tb = copy(f, cum, tb)
        w.free = [tb]
        yield
        bx, kx = f[:, META:TM], kk[:, META:TM]
        lastb = A4(bx)[:, :, 127:128]
        te1 = act(ebl[:, s, 0:1], f[:, META - 1:META], ACT.Exp, tb, hd_free[s])
        te2 = act(ebl[:, s, 1:9], lastb.rearrange("p c o -> p (c o)"), ACT.Exp, tb, hd_free[s])
        w = wk.take()
        c1 = tt(A4(w.ap[:, META:TM]), lastb.to_broadcast([P, 8, 128]), A4(bx), ALU.subtract, tb, w.free)
        c2 = tt(w.ap[:, 0:META], f[:, META - 1:META].to_broadcast([P, META]), f[:, 0:META], ALU.subtract,
                tb, w.free)
        e = act(w.ap, w.ap, ACT.Exp, c1, c2)
        kd = tt(w.ap, w.ap, kk, ALU.mult, e, tk)
        yield
        yield
        kfree = []
        for half_ in range(2):
            x = aux.take()
            PE.after(kd, x.free)
            for c in range(4):
                ins = nc.tensor.transpose(x.ap[:, c * 128:(c + 1) * 128],
                                          w.ap[:, META + (4 * half_ + c) * 128:META + (4 * half_ + c + 1) * 128],
                                          ident)
            d = PE.mark(ins)
            g = act(kdT[:, half_ * 512:(half_ + 1) * 512], x.ap, ACT.Copy, d, kdslot.free)
            x.free = [g]
            kfree.append(g)
            yield
        x = aux.take()
        PE.after(x.free)
        d = PE.mark(nc.tensor.transpose(x.ap[0:META, 0:128], w.ap[:, 0:META], ident))
        w.free = [d]
        gm = act(kdm[:, :], x.ap[0:META, 0:128], ACT.Copy, d, kdslot.free)
        x.free = [gm]
        yield
        x = aux.take()
        PE.after(x.free, gm, tv)
        d = PE.mark(nc.tensor.matmul(x.ap[:, 0:128], kdm[:, :], vm[:, s, :], start=True, stop=True))
        ss = copy(Sb[:, 0:128], x.ap[:, 0:128], d, sslot.free)
        x.free = [ss]
        yield
        for g in range(2):
            x = aux.take()
            PE.after(x.free, kfree[g])
            n = 4 if g == 0 else 3
            for c in range(4 * g, 4 * g + n):
                ins = nc.tensor.matmul(x.ap[:, (c % 4) * 128:(c % 4 + 1) * 128], kdT[:, c * 128:(c + 1) * 128],
                                       v[:, c * 128:(c + 1) * 128], start=True, stop=True)
            d = PE.mark(ins)
            for c in range(4 * g, 4 * g + n):
                ss = stt(Sb[:, (c + 1) * 128:(c + 2) * 128], Sb[:, c * 128:(c + 1) * 128],
                         ebl[:, s, c + 1:c + 2], x.ap[:, (c % 4) * 128:(c % 4 + 1) * 128],
                         ALU.mult, ALU.add, ss, d, te1, te2)
            x.free = [ss]
            yield
        kdslot.free = [d]
        pend = []
        ta = None

        def product(w, left, right, tok, hs, lv):
            nonlocal ta
            for g in range(2):
                x = aux.take()
                PE.after(x.free, tok)
                for c in range(4 * g, 4 * g + 4):
                    ins = nc.tensor.matmul(x.ap[:, (c % 4) * 128:(c % 4 + 1) * 128],
                                           left[:, c * 128:(c + 1) * 128], right[:, c * 128:(c + 1) * 128],
                                           start=True, stop=True)
                d = PE.mark(ins)
                dst = Ab[:, g * 512:(g + 1) * 512].rearrange("p (c t) -> p c t", c=4)
                src = x.ap.rearrange("p (c t) -> p c t", c=4)
                if lv == 0:
                    m = masks[:, 0:1, :].to_broadcast([P, 4, 128])
                    t = tt(dst, src, m, ALU.mult, d, Aslot.free, t_mask)
                    a_tok[g] = t
                else:
                    m = (masks[:, lv:lv + 1, :] if lv < 7 else
                         ident.rearrange("p (o t) -> p o t", o=1)).to_broadcast([P, 4, 128])
                    t = VE.mark(VE.after(d, a_tok[g]).copy_predicated(dst, m.bitcast(I32), src))
                    a_tok[g] = t
                x.free = [t]
            if w is not None:
                w.free = [d]

        a_tok = [None, None]
        for lv, hs in enumerate(HALVES):
            w = wk.take()
            u = w.ap[:, 0:T]
            n = T // (2 * hs)
            bv = bx.rearrange("p (n b) -> p n b", b=2 * hs)
            uv = u.rearrange("p (n b) -> p n b", b=2 * hs)
            dd = tt(uv, bv, bv[:, :, hs - 1:hs].to_broadcast([P, n, 2 * hs]), ALU.subtract, tb, w.free)
            ul, ur = half(u, hs)
            kl, _ = half(kx, hs)
            _, qr = half(q, hs)
            e1_ = act(ul, ul, ACT.Exp, dd, scale=-1.0)
            e2_ = act(ur, ur, ACT.Exp, dd)
            m1 = tt(ul, ul, kl, ALU.mult, e1_, tk)
            m2 = tt(ur, ur, qr, ALU.mult, e2_, tq)
            pend.append((w, u, u, [m1, m2], hs, lv))
            yield
            if len(pend) > 1:
                product(*pend.pop(0))
                yield
        w2 = wk.take()
        qe = w2.ap[:, 0:T]
        e = act(qe, bx, ACT.Exp, tb, w2.free)
        tqe = tt(qe, qe, q, ALU.mult, e, tq)
        yield
        product(*pend.pop(0))
        yield
        product(None, kx, q, [tk, tq], 0, 7)
        yield
        for g in range(2):
            x = aux.take()
            PE.after(x.free, a_tok[g], tqe, ss, tv)
            for c in range(4 * g, 4 * g + 4):
                o = x.ap[:, (c % 4) * 128:(c % 4 + 1) * 128]
                cc = slice(c * 128, (c + 1) * 128)
                nc.tensor.matmul(o, v[:, cc], Ab[:, cc], start=True, stop=False)
                ins = nc.tensor.matmul(o, Sb[:, cc], qe[:, cc], start=False, stop=True)
            d = PE.mark(ins)
            t = act(O[:, h, g * 512:(g + 1) * 512], x.ap, ACT.Copy, d)
            x.free = [t]
            yield
        w2.free = [d]
        Aslot.free, sslot.free = [d], [d]
        hd_free[s] = [d, t]
        o_ready[h] = t

    prev = None
    for h in range(8):
        s = h % 2
        pr, d, _ = gemm_fm(meta=True)
        a = act(fb[:, s, META:TM], flat(pr.ap), ACT.Sigmoid, d, hd_free[s], z2)
        b = act(fb[:, s, 0:META], small.ap[:, 0:META], ACT.Sigmoid, d)
        pr.free, small.free = [a], [b]
        tf = [a, b]
        pr, d, _ = gemm_fm()
        tq = act(qb[:, s, :], flat(pr.ap), ACT.Silu, d, hd_free[s])
        pr.free = [tq]
        pr, d = gemm_tm(meta=True)
        a = act(vb[:, s, :], flat(pr.ap), ACT.Copy, d, hd_free[s])
        b = act(vm[:, s, :], small.ap[0:META, 128:256], ACT.Copy, d, hd_free[s])
        pr.free, small.free = [a], [b]
        if prev is not None:
            finish(prev)
        prev = hgrn(h, s, tf, tq, [a, b])
        jobs.append(prev)

    GR = nc.dram_tensor("keep_gr", [KT, P, T], F, kind="Internal").ap()
    GC = nc.dram_tensor("keep_gc", [KT, P, T], F, kind="Internal").ap()
    SZ = nc.dram_tensor("keep_sz", [KT, P, T], F, kind="Internal").ap()
    gr_kept, gc_kept, sz_kept = [None] * 8, [None] * 8, [None] * 8

    def gate_out(buf, dram, m, func):
        pr, d, _ = gemm_fm()
        a = act(buf.ap, flat(pr.ap), func, d, buf.free)
        pr.free = [a]
        t = store(dram[m], buf.ap, a)
        buf.free = [t]
        return t

    gbuf = Ring([Slot(qb[:, 0, :]), Slot(vb[:, 0, :])])
    for g in gbuf.slots:
        g.free = [hd_free[0]]
    for m in range(8):
        gr_kept[m] = gate_out(gbuf.take(), GR, m, ACT.Sigmoid)
    finish(prev)
    s1_done = [hd_free[0], hd_free[1], gr_kept]
    s1.close()

    s2 = ExitStack()
    Cb = sb("Cb", [P, KT, T], F, s2)
    s3 = ExitStack()
    av = sb("av", [P, 2, HIST + T], F, s3)
    sg = sb("sg", [P, 2, TM], F, s3)
    tmp = sb("tmp", [P, 3, T], F, s3)
    R8 = sb("R8", [8, T], F, s3)
    tr = Ring([Slot(tmp[:, i, :]) for i in range(3)])
    for q in tr.slots:
        q.free = [s1_done]

    pr, d = sums([(O[:, h, :], [o_ready[h]]) for h in range(8)], tr, T, lhs=lambda h: selA8[:, h, :], rows=8)
    a = act(R8[:, :], flat(pr.ap[0:8, :, :]), ACT.Sqrt, d, s1_done, scale=1.0 / 128, bias=EPS)
    pr.free = [a]
    r8 = recip(R8[:, :], R8[:, :], a)

    avs = [Slot(av[:, i, :]) for i in range(2)]
    sgs = [Slot(sg[:, i, :]) for i in range(2)]
    za = zero(av[:, :, 0:HIST - META], 0.0, s1_done)
    for q in avs + sgs:
        q.free = [za, s1_done]
    c_ready = [None] * 8
    for m in range(8):
        u, w = avs[m % 2], sgs[m % 2]
        pr, d, _ = gemm_fm(meta=True)
        a = act(u.ap[:, HIST:], flat(pr.ap), ACT.Copy, d, u.free)
        b = act(u.ap[:, HIST - META:HIST], small.ap[:, 0:META], ACT.Copy, d)
        pr.free, small.free = [a], [b]
        pr, d, _ = gemm_fm(meta=True)
        a2 = act(w.ap[:, META:], flat(pr.ap), ACT.Sigmoid, d, w.free)
        b2 = act(w.ap[:, 0:META], small.ap[:, 0:META], ACT.Sigmoid, d)
        pr.free, small.free = [a2], [b2]
        t = tt(u.ap[:, HIST - META:], u.ap[:, HIST - META:], w.ap, ALU.mult, a, b, a2, b2)
        w.free = [t]
        c = ts(Cb[:, m, :], u.ap[:, 0:T], V("conv_w", m), V("conv_b", m), ALU.mult, ALU.add, t, s1_done)
        for j in range(1, TAPS):
            c = stt(Cb[:, m, :], u.ap[:, j:j + T], V("conv_w", 8 * j + m), Cb[:, m, :], ALU.mult, ALU.add, c)
        u.free = [c]
        c_ready[m] = c
        pr, d, _ = gemm_fm()
        q = tr.take()
        a = act(q.ap, flat(pr.ap), ACT.Silu, d, q.free)
        pr.free = [a]
        for j in range(2):
            x = aux.take()
            oh = O[:, m, j * 512:(j + 1) * 512]
            d = PE.mark(PE.after(x.free, r8).matmul(x.ap, selB8[:, m, :], R8[:, j * 512:(j + 1) * 512],
                                                    start=True, stop=True))
            t = stt(oh, oh, V("gnorm_g", m), x.ap, ALU.mult, ALU.mult, d, o_ready[m])
            x.free = [t]
            t = tt(oh, oh, q.ap[:, j * 512:(j + 1) * 512], ALU.mult, t, a)
        q.free = [t]
        o_ready[m] = t
        sz_kept[m] = gate_out(tr.take(), SZ, m, ACT.Silu)

    def conv_norm():
        xs = [aux.take(), aux.take()]
        PE.after(xs[0].free, xs[1].free)
        for k in range(8):
            PE.after(c_ready[k])
            for j in range(2):
                ins = nc.tensor.matmul(xs[j].ap, ones, Cb[:, k, j * 512:(j + 1) * 512],
                                       start=(k == 0), stop=(k == 7))
            yield
        d = PE.mark(ins)
        for k in range(8):
            for j in range(2):
                cj = Cb[:, k, j * 512:(j + 1) * 512]
                t = stt(cj, xs[j].ap, -1.0 / 1024, cj, ALU.mult, ALU.add, d, c_ready[k])
            c_ready[k] = t
            yield
        xs[0].free = xs[1].free = [t]
        xs = [aux.take(), aux.take()]
        PE.after(xs[0].free, xs[1].free)
        for k in range(8):
            q = tr.take()
            a = act(q.ap, Cb[:, k, :], ACT.Square, c_ready[k], q.free)
            yield
            PE.after(a)
            for j in range(2):
                ins = nc.tensor.matmul(xs[j].ap, ones, q.ap[:, j * 512:(j + 1) * 512],
                                       start=(k == 0), stop=(k == 7))
            d = PE.mark(ins)
            q.free = [d]
        R = sg[:, 0, 0:T]
        for j in range(2):
            a = act(R[:, j * 512:(j + 1) * 512], xs[j].ap, ACT.Sqrt, d, sgs[0].free, scale=1.0 / 1024, bias=EPS)
            xs[j].free = [a]
        r = recip(R, R, a)
        yield
        for k in range(8):
            q = tr.take()
            ld = load(q.ap, SZ[k], sz_kept[k], q.free)
            t = tt(Cb[:, k, :], Cb[:, k, :], R, ALU.mult, r, c_ready[k])
            a = act(Cb[:, k, :], Cb[:, k, :], ACT.Silu, t, scale=V("ln_g", k), bias=V("ln_b", k))
            t = tt(Cb[:, k, :], Cb[:, k, :], q.ap, ALU.mult, a, ld)
            q.free = [t]
            c_ready[k] = t
            yield

    jobs.append(conv_norm())
    gb = Ring([Slot(av[:, 0, 0:T]), Slot(av[:, 1, 0:T])])
    gb.slots[0].free, gb.slots[1].free = avs[0].free, avs[1].free
    for m in range(8):
        pr, d, _ = gemm_fm(last=(m == 7))
        buf = gb.take()
        a = act(buf.ap, flat(pr.ap), ACT.Sigmoid, d, buf.free)
        pr.free = [a]
        gc_kept[m] = store(GC[m], buf.ap, a)
        buf.free = [gc_kept[m]]
    drain_jobs()

    for k in range(8):
        h_ready[k] = put_h(k, Cb[:, k, :], c_ready[k])
    M = Cb
    m_ready = [None] * 8
    split_c = [list(t) for t in h_ready]
    gl = Ring([Slot(tmp[:, i, :]) for i in range(3)])
    for a_, b_ in zip(gl.slots, tr.slots):
        a_.free = b_.free

    def fetch(dram, m, kept):
        q = gl.take()
        return q, load(q.ap, dram[m], kept, q.free)

    nxt = fetch(GC, 0, gc_kept[0])
    for m in range(8):
        q, ld = nxt
        if m < 7:
            nxt = fetch(GC, m + 1, gc_kept[m + 1])
        pr, d, _ = gemm_fm(last=(m == 7))
        t = tt(M[:, m, :], flat(pr.ap), q.ap, ALU.mult, d, ld, split_c[m])
        pr.free, q.free = [t], [t]
        m_ready[m] = t
    for k in range(8):
        h_ready[k] = put_h(k, O[:, k, :], o_ready[k])
    split_o = [list(t) for t in h_ready]
    nxt = fetch(GR, 0, gr_kept[0])
    for m in range(8):
        q, ld = nxt
        if m < 7:
            nxt = fetch(GR, m + 1, gr_kept[m + 1])
        pr, d, _ = gemm_fm(last=(m == 7))
        t = tt(q.ap, flat(pr.ap), q.ap, ALU.mult, d, ld)
        pr.free = [t]
        t = tt(M[:, m, :], M[:, m, :], q.ap, ALU.add, t, m_ready[m])
        q.free = [t]
        m_ready[m] = t
    for k in range(8):
        h_ready[k] = put_h(k, M[:, k, :], m_ready[k])

    class Stats:

        def __init__(self, ring):
            self.banks = [aux.take(), aux.take()]
            self.ring, self.n, self.wait = ring, 0, None

        def add(self, ap, *tokens):
            q = self.ring.take()
            a = act(q.ap, ap, ACT.Square, q.free, *tokens)
            self.flush()
            self.wait = (q, a)

        def flush(self):
            if self.wait is None:
                return
            q, a = self.wait
            self.wait = None
            if self.n == 0:
                PE.after(self.banks[0].free, self.banks[1].free)
            PE.after(a)
            for j in range(2):
                ins = nc.tensor.matmul(self.banks[j].ap, ones, q.ap[:, j * 512:(j + 1) * 512],
                                       start=(self.n == 0), stop=(self.n == 7))
            self.d = PE.mark(ins)
            q.free = [self.d]
            self.n += 1

        def inverse_root(self, R, eps, *tokens):
            self.flush()
            out = []
            for j in range(2):
                r = R[:, j * 512:(j + 1) * 512]
                a = act(r, self.banks[j].ap, ACT.Sqrt, self.d, *tokens, scale=1.0 / 1024, bias=eps)
                self.banks[j].free = [a]
                out.append(recip(r, r, a))
            return out

    X = O
    x_ready = [None] * 8
    st = Stats(Ring([Slot(sg[:, i, 0:T]) for i in range(2)]))
    for q in st.ring.slots:
        q.free = [sgs[0].free, sgs[1].free, c_ready]

    def fetch_x(m):
        q = gl.take()
        return q, load(q.ap, A["xin"][m][:, META:TM], q.free)

    nxt = fetch_x(0)
    for m in range(8):
        q, ld = nxt
        if m < 7:
            nxt = fetch_x(m + 1)
        pr, d, _ = gemm_fm(last=(m == 7))
        t = tt(X[:, m, :], flat(pr.ap), q.ap, ALU.add, d, ld, split_o[m])
        pr.free, q.free = [t], [t]
        x_ready[m] = t
        st.add(X[:, m, :], t)
    R = av[:, 0, 0:T]
    r = st.inverse_root(R, EPS, gc_kept)
    st = Stats(st.ring)
    for k in range(8):
        x_ready[k] = stt(X[:, k, :], X[:, k, :], V("final_g", k), R, ALU.mult, ALU.mult, r, x_ready[k])
        st.add(X[:, k, :], x_ready[k])
    if stage == 2:
        for k in range(8):
            store(A["dbg"][k], X[:, k, :], x_ready[k])
        SP.after(*stores)
        return

    XS = nc.dram_tensor("keep_x", [KT, P, T], F, kind="Internal").ap()
    R2 = av[:, 1, 0:T]
    r = st.inverse_root(R2, EPS, gc_kept)
    nr = Ring([Slot(sg[:, 0, 0:T]), Slot(sg[:, 1, 0:T])])
    for q, w in zip(nr.slots, st.ring.slots):
        q.free = w.free
    xs_kept = [None] * 8

    def normed(q, k, name, R, r):
        t = stt(q.ap, X[:, k, :], V(name, k), R, ALU.mult, ALU.mult, r, x_ready[k], q.free)
        h_ready[k] = put_h(k, q.ap, t)
        q.free = list(h_ready[k])

    for k in range(8):
        xs_kept[k] = store(XS[k], X[:, k, :], x_ready[k])
        normed(nr.take(), k, "mix_g", R2, r)
    old = [xs_kept, nr.slots[0].free, nr.slots[1].free, x_ready, r]
    s3.close()
    s2.close()

    aux.slots.append(small)
    s4 = ExitStack()
    qa = sb("qa", [P, 2, T], F, s4)
    ka = sb("ka", [P, 2, T], F, s4)
    va = sb("va", [P, 2, T], F, s4)
    oa = sb("oa", [P, 8, 128], F, s4)
    bias = sb("bias", [P, 2, BAND], F, s4)
    pp = sb("pp", [P, 3, BAND], F, s4)
    pt = sb("pt", [P, 2, BAND], F, s4)
    st2 = sb("st2", [P, 4, 8], F, s4)
    ss2 = sb("ss2", [P, 8], F, s4)
    osq = sb("osq", [P, 8, 64], F, s4)
    zb = sb("zb", [P, T + 2], F, s4)
    gt = sb("gt", [P, 2, T], F, s4)
    vg = sb("vg", [P, 8, 256], F, s4)
    sgw = sb("sgw", [P, 4, 128], F, s4)
    sgc = sb("sgc", [P, 3, 256], F, s4)
    bst = sb("bst", [P, 8, 6], F, s4)
    bag = sb("bag", [P, 8, 2], F, s4)
    R8b = qa[0:8, 0, :]
    MX = B0
    t_sgw = load(flat(sgw[:, :, :]), A["sgw"], old)
    t_sgc = load(flat(sgc[:, :, :]), A["sgc"], old)
    t_ws = tt(sgw[:, :, :], sgw[:, :, :], C("tri").rearrange("p (o t) -> p o t", o=1).to_broadcast([P, 4, 128]),
              ALU.mult, t_sgw)
    zz = zero(zb[:, 0:2], 0.0, old)

    bias_r = Ring([Slot(bias[:, i, :]) for i in range(2)])
    pp_r = Ring([Slot(pp[:, i, :]) for i in range(3)])
    pt_r = Ring([Slot(pt[:, i, :]) for i in range(2)])
    for q in bias_r.slots + pp_r.slots + pt_r.slots:
        q.free = [old]
    S = Slot(psum[:, 4:6, :])
    PT = Slot(psum[:, 6:8, :])
    S.free = [small.free, aux.slots[0].free]
    PT.free = [aux.slots[1].free, aux.slots[2].free]
    qkv_free = [[old], [old]]
    oa_free = [old]
    mx_ready = [None] * 8

    def attention(j, s, tq, tk, tv):
        nonlocal oa_free
        items = [(hh_, i) for hh_ in range(2) for i in range(8)]
        got = {}
        bt = {}
        tb = None
        for n in range(len(items) + 3):
            if n < len(items):
                hh_, i = items[n]
                if i == 0:
                    bq = bias_r.take()
                    bt[hh_] = (bq, load(bq.ap, A["bias"][2 * j + hh_], bq.free))
                bq, tb = bt[hh_]
                nk = min(BAND, 128 * (i + 1))
                k0 = 128 * (i + 1) - nk
                lo = 64 * hh_
                PE.after(S.free, tq, tk)
                sp = flat(S.ap)
                for a0 in range(0, nk, 512):
                    w_ = min(512, nk - a0)
                    ins = nc.tensor.matmul(sp[:, a0:a0 + w_], qa[lo:lo + 64, s, i * 128:(i + 1) * 128],
                                           ka[lo:lo + 64, s, k0 + a0:k0 + a0 + w_], start=True, stop=True)
                d = PE.mark(ins)
                p = pp_r.take()
                c = n % 4
                mx_, nm, rs, ri = (st2[:, c, z:z + 1] for z in range(4))
                t = VE.mark(VE.after(d, tb, p.free).tensor_tensor_reduce(
                    p.ap[:, 0:nk], sp[:, 0:nk], bq.ap[:, BAND - nk:BAND], 1.0, -3.0e38, ALU.add, ALU.max, mx_))
                S.free = [t]
                if i == 7:
                    bq.free = [t]
                t = ts(nm, mx_, -1.0, None, ALU.mult, None, t)
                e = act(p.ap[:, 0:nk], p.ap[:, 0:nk], ACT.Exp, t, bias=nm, accum_out=rs)
                t = recip(ri, rs, e)
                got[n] = [p, nk, k0, ri, e, t, hh_, i]
            m = n - 2
            if 0 <= m < len(items):
                p, nk, k0, ri, e, t, hh_, i = got[m]
                PE.after(PT.free, e)
                px = flat(PT.ap)
                for b_ in range(nk // 128):
                    ins = nc.tensor.transpose(px[:, b_ * 128:(b_ + 1) * 128], p.ap[:, b_ * 128:(b_ + 1) * 128], ident)
                d = PE.mark(ins)
                q = pt_r.take()
                ev = act(q.ap[:, 0:nk], px[:, 0:nk], ACT.Copy, d, q.free)
                p.free = [d]
                PT.free = [ev]
                got[m].append((q, ev))
            m = n - 3
            if 0 <= m < len(items):
                p, nk, k0, ri, e, t, hh_, i, (q, ev) = got.pop(m)
                out = flat(PT.ap)[:, 896:960]
                PE.after(ev, tv, PT.free)
                for b_ in range(nk // 128):
                    kt = k0 // 128 + b_
                    ins = nc.tensor.matmul(out, q.ap[:, b_ * 128:(b_ + 1) * 128],
                                           va[:, s, kt * 128 + 64 * hh_:kt * 128 + 64 * hh_ + 64],
                                           start=(b_ == 0), stop=(b_ == nk // 128 - 1))
                d = PE.mark(ins)
                q.free = [d]
                o = ts(oa[:, i, 64 * hh_:64 * hh_ + 64], out, ri, None, ALU.mult, None, d, t, oa_free)
                PT.free = [o, ev]
                if i == 7:
                    oh = oa[:, :, 64 * hh_:64 * hh_ + 64]
                    t = tt(osq[:, :, :], oh, oh, ALU.mult, o)
                    t = VE.mark(VE.after(t).tensor_reduce(ss2[:, :], osq[:, :, :], AX, ALU.add))
                    a = act(ss2[:, :], ss2[:, :], ACT.Sqrt, t, scale=1.0 / 64, bias=EPS)
                    t = recip(ss2[:, :], ss2[:, :], a)
                    tn = tt(oh, oh, ss2[:, :].rearrange("p (t o) -> p t o", o=1).to_broadcast([P, 8, 64]),
                            ALU.mult, t)
            yield
            if n % 2:
                yield
        qkv_free[s] = [d]
        yield
        PE.after(S.free, tn)
        sp = flat(S.ap)
        for i in range(8):
            ins = nc.tensor.transpose(sp[:, i * 128:(i + 1) * 128], oa[:, i, :], ident)
        d = PE.mark(ins)
        oa_free = [d]
        t = act(MX[:, j, :], sp, ACT.Copy, d, xs_kept[j], scale=V("gg2", j))
        S.free = [t]
        mx_ready[j] = t

    prev = None
    for j in range(4):
        s = j % 2
        pr, d, _ = gemm_fm()
        tq = act(qa[:, s, :], flat(pr.ap), ACT.Copy, d, qkv_free[s], scale=0.125)
        pr.free = [tq]
        pr, d, _ = gemm_fm()
        tk = act(ka[:, s, :], flat(pr.ap), ACT.Copy, d, qkv_free[s])
        pr.free = [tk]
        pr, d = gemm_tm()
        tv = act(va[:, s, :], flat(pr.ap), ACT.Copy, d, qkv_free[s])
        pr.free = [tv]
        if prev is not None:
            finish(prev)
        prev = attention(j, s, tq, tk, tv)
        jobs.append(prev)

    gr_ = Ring([Slot(gt[:, i, :]) for i in range(2)])
    for q in gr_.slots:
        q.free = [old]
    zfree = [zz]
    for m in range(2):
        pr, d, _ = gemm_fm()
        a = act(zb[:, 2:], flat(pr.ap), ACT.Copy, d, zfree)
        pr.free = [a]
        pr, d, _ = gemm_fm()
        z = tt(zb[:, 2:], zb[:, 2:], flat(pr.ap), ALU.mult, d, a)
        pr.free = [z]
        pr, d, _ = gemm_fm()
        q = gr_.take()
        b = act(q.ap, flat(pr.ap), ACT.Copy, d, q.free)
        pr.free = [b]
        y = MX[:, 4 + m, :]
        c = ts(y, zb[:, 0:T], V("cw2", m), None, ALU.mult, None, z, xs_kept[4 + m])
        for w_ in (1, 2):
            c = stt(y, zb[:, w_:w_ + T], V("cw2", 2 * w_ + m), y, ALU.mult, ALU.add, c)
        zfree = [c]
        c = tt(y, y, q.ap, ALU.mult, c, b)
        q.free = [c]
        mx_ready[4 + m] = c
    for m in range(2):
        pr, d, _ = gemm_fm()
        a = act(MX[:, 6 + m, :], flat(pr.ap), ACT.Gelu, d, xs_kept[6 + m])
        pr.free = [a]
        mx_ready[6 + m] = a
    for m in range(2):
        pr, d = gemm_tm(last=(m == 1))
        a = act(vg[:, :, 128 * m:128 * (m + 1)], flat(pr.ap).rearrange("p (t c) -> p t c", t=8), ACT.Gelu, d, old)
        pr.free = [a]
    for i in range(8):
        t = VE.mark(VE.after(a, old).bn_stats(bst[:, i, :], vg[:, i, :]))
    for i in range(8):
        t2 = VE.mark(VE.after(t).bn_aggr(bag[:, i, :], bst[:, i, :]))
    b = act(bag[:, :, 1:2], bag[:, :, 1:2], ACT.Sqrt, t2, scale=1.0, bias=EPS)
    r = recip(bag[:, :, 1:2], bag[:, :, 1:2], b)
    for i in range(8):
        t = ts(vg[:, i, :], vg[:, i, :], bag[:, i, 0:1], bag[:, i, 1:2], ALU.subtract, ALU.mult, r)
    t = tt(vg[:, :, :], vg[:, :, :], sgc[:, 0:1, :].to_broadcast([P, 8, 256]), ALU.mult, t, t_sgc)
    tvg = tt(vg[:, :, :], vg[:, :, :], sgc[:, 1:2, :].to_broadcast([P, 8, 256]), ALU.add, t)
    finish(prev)
    aux2 = Ring([Slot(psum[:, i, :]) for i in range(4, 8)])
    for n, q in enumerate(aux2.slots):
        q.free = [S.free if n < 2 else PT.free]
    for m in range(2):
        for g in range(2):
            x = aux2.take()
            PE.after(x.free, tvg, t_ws)
            for b_ in range(4):
                for w_ in range(2):
                    ins = nc.tensor.matmul(x.ap[64 * w_:64 * w_ + 64, b_ * 128:(b_ + 1) * 128],
                                           vg[:, 4 * g + b_, (2 * m + w_) * 64:(2 * m + w_ + 1) * 64],
                                           sgw[:, 2 * m + w_, :], start=True, stop=True)
            d = PE.mark(ins)
            q = gr_.take()
            u = q.ap[:, 0:512].rearrange("p (b t) -> p b t", b=4)
            t = tt(u, x.ap.rearrange("p (b t) -> p b t", b=4),
                   sgc[:, 2:3, m * 128:(m + 1) * 128].to_broadcast([P, 4, 128]), ALU.add, d, q.free, t_sgc)
            x.free = [t]
            y = MX[:, 6 + m, g * 512:(g + 1) * 512]
            t = tt(y, y, q.ap[:, 0:512], ALU.mult, t, mx_ready[6 + m])
            q.free = [t]
        mx_ready[6 + m] = t
    pr, d = sums([(MX[:, 4 + k, :], [mx_ready[4 + k]]) for k in range(4)], gr_, T,
                 lhs=lambda k: selA4[:, k, :], rows=8)
    a = act(R8b[:, :], flat(pr.ap[0:8, :, :]), ACT.Sqrt, d, qkv_free, scale=1.0 / 64, bias=EPS)
    pr.free = [a]
    r = recip(R8b[:, :], R8b[:, :], a)
    for k in range(4):
        for g in range(2):
            x = aux2.take()
            d = PE.mark(PE.after(x.free, r).matmul(x.ap, selB4[:, k, :], R8b[:, g * 512:(g + 1) * 512],
                                                   start=True, stop=True))
            y = MX[:, 4 + k, g * 512:(g + 1) * 512]
            t = stt(y, y, V("gg2", 4 + k), x.ap, ALU.mult, ALU.mult, d, mx_ready[4 + k])
            x.free = [t]
        mx_ready[4 + k] = t
    for k in range(8):
        h_ready[k] = put_h(k, MX[:, k, :], mx_ready[k])
    split_m = [list(t) for t in h_ready]
    mix_done = [tvg, d, t, mx_ready, split_m, qkv_free, oa_free]
    s4.close()
    aux = aux2

    s5 = ExitStack()
    hdh = sb("hdh", [P, 4, T], FR, s5)
    hdl = sb("hdl", [P, 4, T], FR, s5)
    t5 = sb("t5", [P, 6, T], F, s5)
    R5 = sb("R5", [P, T], F, s5)[:, :]
    mean5 = sb("mean5", [P, T], F, s5)[:, :]
    sqr = Ring([Slot(t5[:, i, :]) for i in range(3)])
    tr = Ring([Slot(t5[:, 3 + i, :]) for i in range(3)])
    for q in sqr.slots + tr.slots:
        q.free = [mix_done]
    hd_free4 = [[mix_done] for _ in range(4)]
    hd_ready = [None] * 4


    def fetch_xs(m):
        q = tr.take()
        return q, load(q.ap, XS[m], q.free)

    st = Stats(sqr)
    nxt = fetch_xs(0)
    for m in range(8):
        q, ld = nxt
        if m < 7:
            nxt = fetch_xs(m + 1)
        pr, d, _ = gemm_fm(last=(m == 7))
        t = tt(X[:, m, :], flat(pr.ap), q.ap, ALU.add, d, ld, split_m[m])
        pr.free, q.free = [t], [t]
        x_ready[m] = t
        st.add(X[:, m, :], t)
    r = st.inverse_root(R5, EPS, mix_done)
    for k in range(8):
        normed(tr.take(), k, "mlp_g2", R5, r)

    def mlp(after_last):
        for g in range(8):
            for k in range(4):
                pr, d, _ = gemm_fm(last=(g == 7 and k == 3))
                q = tr.take()
                a = act(q.ap, flat(pr.ap), ACT.Relu, d, q.free)
                pr.free = [a]
                t = tt(q.ap, q.ap, q.ap, ALU.mult, a)
                a = act(hdh[:, k, :], q.ap, ACT.Copy, t, hd_free4[k])
                b = tt(hdl[:, k, :], q.ap, fp(hdh[:, k, :]), ALU.subtract, a)
                q.free = [b]
                hd_ready[k] = [a, b]
            for m2 in range(4):
                i = next_slab()
                for w_ in range(2):
                    m = 2 * m2 + w_
                    pr, d, _ = gemm_fm(src=(hdh, hdl), ready=hd_ready, nk=4, slab=i, base=4 * w_)
                    x_ready[m] = tt(X[:, m, :], X[:, m, :], flat(pr.ap), ALU.add, d, x_ready[m], *h_ready)
                    pr.free = [x_ready[m]]
                    if g == 7:
                        after_last(m)
                w_free[i % 2] = [d]
            for k in range(4):
                hd_free4[k] = [d]

    st = Stats(sqr)
    mlp(lambda m: st.add(X[:, m, :], x_ready[m]))
    r = st.inverse_root(R5, EPS, *h_ready)
    for k in range(8):
        x_ready[k] = stt(X[:, k, :], X[:, k, :], V("fin_g2", k), R5, ALU.mult, ALU.mult, r, x_ready[k])
        if stage > 3:
            h_ready[k] = put_h(k, X[:, k, :], x_ready[k])
            xs_kept[k] = store(XS[k], X[:, k, :], x_ready[k], xs_kept[k])
    if stage == 3:
        for k in range(8):
            store(A["dbg"][k], X[:, k, :], x_ready[k])
        SP.after(*stores)
        return
    split3 = [list(t) for t in h_ready]
    b2_done = [x_ready, split3, hd_free4, r, [q.free for q in tr.slots + sqr.slots]]
    s5.close()

    s6 = ExitStack()
    pre = sb("pre", [P, 2, T + 3], F, s6)
    q3 = sb("q3", [P, 2, T], F, s6)
    k3 = sb("k3", [P, 2, T], F, s6)
    v3 = sb("v3", [P, 2, 8, 129], F, s6)
    o3 = sb("o3", [P, 2, T], F, s6)
    row = sb("row", [4, 2, T], F, s6)
    mp = sb("mp", [4, 8], F, s6)
    uT = sb("uT", [P, 8, 4], F, s6)
    eT = sb("eT", [P, 8, 4], F, s6)
    Pm = sb("Pm", [P, T], F, s6)
    kd3 = sb("kd3", [P, T], F, s6)
    C3 = sb("C3", [P, 8, 129], F, s6)
    h3 = sb("h3", [P, T], F, s6)
    den = sb("den", [P, 2, 8], F, s6)
    bs3 = sb("bs3", [P, 8, 6], F, s6)
    ba3 = sb("ba3", [P, 8, 2], F, s6)
    pb = sb("pb", [P, 2, T], F, s6)
    wp = sb("wp", [P, 4, 128], F, s6)
    shf = kd3[0:4, :]
    Y = B0
    t_wp = load(flat(wp[:, :, :]), A["w_pool"], b2_done)
    z1 = zero(pre[:, :, 0:3], 0.0, b2_done)
    z2 = zero(v3[:, :, :, 128:129], 1.0, b2_done)
    z3 = zero(shf, 0.0, b2_done)
    z4 = zero(C3[:, 0, :], 0.0, b2_done)

    i_, f_, a_, u_, w_ = row[:, 0, :], row[:, 1, :], pb[0:4, 0, :], pb[0:4, 1, :], h3[0:4, :]
    pr, d, _ = gemm_fm()
    g1 = act(i_, flat(pr.ap[0:4, :, :]), ACT.Copy, d, b2_done)
    g2 = act(f_, flat(pr.ap[32:36, :, :]), ACT.Copy, d, b2_done)
    pr.free = [g1, g2]
    t = ts(i_, i_, V("b_i")[0:4, :], None, ALU.add, None, g1)
    ti = t
    t = ts(f_, f_, V("b_f")[0:4, :], None, ALU.add, None, g2)
    a = act(a_, f_, ACT.Abs, t)
    a = act(a_, a_, ACT.Exp, a, scale=-1.0)
    a = act(a_, a_, ACT.Ln, a, bias=1.0)
    t = ts(f_, f_, 0.0, None, ALU.min, None, t, a)
    t = tt(f_, f_, a_, ALU.subtract, t)
    t1 = zero(w_, 1.0, b2_done)
    t1 = zero(w_.rearrange("p (c t) -> p c t", c=8)[:, :, 0:1], 0.0, t1)
    ta = VE.mark(VE.after(t, t1).tensor_tensor_scan(a_, w_, f_, 0.0, ALU.mult, ALU.add))
    t = tt(u_, i_, a_, ALU.subtract, ta, ti)
    a8 = a_.rearrange("p (c t) -> p c t", c=8)
    s8 = shf.rearrange("p (c t) -> p c t", c=8)
    t2 = copy(s8[:, 1:8, 0:1], a8[:, 0:7, 127:128], ta, z3)
    tm = VE.mark(VE.after(t, t2).tensor_tensor_scan(i_, shf, u_, 0.0, ALU.add, ALU.max))
    i8 = i_.rearrange("p (c t) -> p c t", c=8)
    t = zero(mp[:, 0:1], 0.0, b2_done)
    t = tt(mp[:, 1:8].rearrange("p (c o) -> p c o", o=1), i8[:, 0:7, 127:128], a8[:, 0:7, 127:128], ALU.add, tm, t)
    t = tt(f_.rearrange("p (c t) -> p c t", c=8), mp[:, :].rearrange("p (c o) -> p c o", o=1).to_broadcast([4, 8, 128]),
           i8, ALU.subtract, t)
    t_si = act(f_, f_, ACT.Exp, t)
    t = tt(w_, a_, i_, ALU.add, tm)
    t = ts(w_, w_, -1.0, 87.0, ALU.mult, ALU.min, t)
    t_em = act(w_, w_, ACT.Exp, t)
    t_nm = ts(i_, i_, -1.0, None, ALU.mult, None, t)
    x = aux.take()
    PE.after(x.free, t_em)
    for c in range(8):
        nc.tensor.transpose(x.ap[:, 4 * c:4 * c + 4], u_[:, c * 128:(c + 1) * 128], ident[0:4, 0:4])
        ins = nc.tensor.transpose(x.ap[:, 64 + 4 * c:68 + 4 * c], w_[:, c * 128:(c + 1) * 128], ident[0:4, 0:4])
    d = PE.mark(ins)
    t_uT = copy(flat(uT[:, :, :]), x.ap[:, 0:32], d, b2_done)
    t_eT = copy(flat(eT[:, :, :]), x.ap[:, 64:96], d, b2_done)
    x.free = [t_eT]
    selB4r = selB8[0:4, :, :]

    p_free = [[z1], [z1]]
    hd3_free = [[b2_done], [b2_done]]
    Pm_free, kd_free, C_free, h3_free, den_free = [b2_done], [tm], [z4], [t_eT], [b2_done]
    y_ready = [None] * 8

    def conv4(src, dst, m, free, dfree, scale=None):
        c = ts(dst, src[:, 0:T], V("cw3", m), None, ALU.mult, None, *free, *dfree)
        for w in range(1, 4):
            c = stt(dst, src[:, w:w + T], V("cw3", 8 * w + m), dst, ALU.mult, ALU.add, c)
        a = act(dst, dst, ACT.Silu, c)
        return c, a

    def mlstm(h, s, tq, tk, tv, to):
        nonlocal Pm_free, kd_free, C_free, h3_free
        q, k, v, o = q3[:, s, :], k3[:, s, :], v3[:, s, :, :], o3[:, s, :]
        for g in range(2):
            x = aux.take()
            d = PE.mark(PE.after(x.free, t_nm).matmul(x.ap, selB4r[:, h, :], i_[:, g * 512:(g + 1) * 512],
                                                      start=True, stop=True))
            for c in range(4 * g, 4 * g + 4):
                t = stt(Pm[:, c * 128:(c + 1) * 128], x.ap[:, (c % 4) * 128:(c % 4 + 1) * 128], uT[:, c, h:h + 1],
                        C("tril_neg"), ALU.add, ALU.add, d, t_uT, Pm_free)
            x.free = [t]
            yield
        tp = act(Pm[:, :], Pm[:, :], ACT.Exp, t)
        yield
        for g in range(2):
            x = aux.take()
            PE.after(x.free, tk)
            for c in range(4):
                ins = nc.tensor.transpose(x.ap[:, c * 128:(c + 1) * 128],
                                          k[:, (4 * g + c) * 128:(4 * g + c + 1) * 128], ident)
            d = PE.mark(ins)
            for c in range(4):
                cc = 4 * g + c
                tkd = ts(kd3[:, cc * 128:(cc + 1) * 128], x.ap[:, c * 128:(c + 1) * 128],
                         Pm[:, cc * 128 + 127:cc * 128 + 128], None, ALU.mult, None, d, tp, kd_free)
            x.free = [tkd]
            yield
        for g in range(2):
            x = aux.take()
            PE.after(x.free, tk, tq)
            for c in range(4):
                cc = slice((4 * g + c) * 128, (4 * g + c + 1) * 128)
                ins = nc.tensor.matmul(x.ap[:, c * 128:(c + 1) * 128], k[:, cc], q[:, cc], start=True, stop=True)
            d = PE.mark(ins)
            tw = tt(Pm[:, g * 512:(g + 1) * 512], x.ap, Pm[:, g * 512:(g + 1) * 512], ALU.mult, d, tkd)
            x.free = [tw]
            yield
        for g in range(2):
            x = aux.take()
            d = PE.mark(PE.after(x.free, t_si).matmul(x.ap, selB4r[:, h, :], f_[:, g * 512:(g + 1) * 512],
                                                      start=True, stop=True))
            t = tt(q[:, g * 512:(g + 1) * 512], q[:, g * 512:(g + 1) * 512], x.ap, ALU.mult, d, tw)
            tqs = t
            t2_ = copy(den[:, 0, 4 * g:4 * g + 4].rearrange("p (c o) -> p c o", o=1),
                       x.ap.rearrange("p (c t) -> p c t", c=4)[:, :, 127:128], d, den_free)
            x.free = [t2_]
            yield
        ts_ = t2_
        tc = z4
        for c in range(7):
            x = aux.take()
            d = PE.mark(PE.after(x.free, tkd, tv).matmul(x.ap[:, 0:129], kd3[:, c * 128:(c + 1) * 128], v[:, c, :],
                                                         start=True, stop=True))
            tc = stt(C3[:, c + 1, :], C3[:, c, :], den[:, 0, c:c + 1], x.ap[:, 0:129], ALU.mult, ALU.add,
                     tc, d, ts_, C_free)
            x.free = [tc]
            if c % 2:
                yield
        kd_free = [d]
        for c in range(8):
            x = aux.take()
            cc = slice(c * 128, (c + 1) * 128)
            PE.after(x.free, tw, tqs, tc, tv)
            nc.tensor.matmul(x.ap[:, 0:129], Pm[:, cc], v[:, c, :], start=True, stop=False)
            d = PE.mark(nc.tensor.matmul(x.ap[:, 0:129], q[:, cc], C3[:, c, :], start=False, stop=True))
            dn = den[:, 1, c:c + 1]
            t = ts(dn, x.ap[:, 128:129], -1.0, None, ALU.mult, None, d)
            t = tt(dn, x.ap[:, 128:129], dn, ALU.max, t)
            t = tt(dn, dn, eT[:, c, h:h + 1], ALU.max, t, t_eT)
            t = recip(dn, dn, t)
            t = ts(h3[:, cc], x.ap[:, 0:128], dn, None, ALU.mult, None, t, h3_free)
            x.free = [t]
            t = VE.mark(VE.after(t).bn_stats(bs3[:, c, :], h3[:, cc]))
            if c % 2:
                yield
        Pm_free, C_free = [d], [d]
        for c in range(8):
            t2 = VE.mark(VE.after(t).bn_aggr(ba3[:, c, :], bs3[:, c, :]))
        a = act(ba3[:, :, 1:2], ba3[:, :, 1:2], ACT.Sqrt, t2, scale=1.0, bias=LN_EPS)
        r = recip(ba3[:, :, 1:2], ba3[:, :, 1:2], a)
        for c in range(8):
            cc = slice(c * 128, (c + 1) * 128)
            t = ts(h3[:, cc], h3[:, cc], ba3[:, c, 0:1], ba3[:, c, 1:2], ALU.subtract, ALU.mult, r)
        yield
        yield
        for g in range(2):
            x = aux.take()
            PE.after(x.free, t)
            for c in range(4):
                ins = nc.tensor.transpose(x.ap[:, c * 128:(c + 1) * 128],
                                          h3[:, (4 * g + c) * 128:(4 * g + c + 1) * 128], ident)
            d = PE.mark(ins)
            ty = stt(Y[:, h, g * 512:(g + 1) * 512], x.ap, V("hn_g", h), o[:, g * 512:(g + 1) * 512],
                     ALU.mult, ALU.mult, d, to, xs_kept[h], split3[h])
            x.free = [ty]
            yield
        h3_free = [d]
        hd3_free[s] = [d, ty, tqs, tc]
        y_ready[h] = ty

    prev = None
    pn = 0
    for h in range(4):
        s = h % 2
        out = []
        for m, dst in ((h, q3[:, s, :]), (4 + h, k3[:, s, :])):
            pz = pre[:, pn % 2, :]
            pr, d, _ = gemm_fm()
            a = act(pz[:, 3:], flat(pr.ap), ACT.Copy, d, p_free[pn % 2])
            pr.free = [a]
            c, a = conv4(pz, dst, m, [a, z1], hd3_free[s])
            p_free[pn % 2] = [c]
            pn += 1
            out.append(a)
        tq = out[0]
        tk = ts(k3[:, s, :], k3[:, s, :], 128.0 ** -0.5, None, ALU.mult, None, out[1])
        pr, d = gemm_tm()
        tv = act(v3[:, s, :, 0:128], flat(pr.ap).rearrange("p (t c) -> p t c", t=8), ACT.Copy, d, hd3_free[s], z2)
        pr.free = [tv]
        pr, d, _ = gemm_fm()
        to = act(o3[:, s, :], flat(pr.ap), ACT.Sigmoid, d, hd3_free[s])
        pr.free = [to]
        if prev is not None:
            finish(prev)
        prev = mlstm(h, s, tq, tk, tv, to)
        jobs.append(prev)

    pbs = [Slot(pb[:, 0, :]), Slot(pb[:, 1, :])]
    for q in pbs:
        q.free = [t_uT, t_eT]
    for g in range(4):
        pr, d, _ = gemm_fm(last=(g == 3))
        y = Y[:, 4 + g, :]
        t0 = act(y, flat(pr.ap), ACT.Copy, d, xs_kept[4 + g], split3[4 + g])
        pr.free = [t0]
        src, ts0 = y, [t0]
        for w in range(g + 1):
            n = 2 ** w
            q = pbs[w % 2]
            t1 = copy(q.ap[:, 0:n], src[:, 0:n], ts0, q.free)
            t2 = tt(q.ap[:, n:], src[:, n:], src[:, 0:T - n], ALU.add, ts0, q.free)
            ts0 = [t1, t2]
            if w:
                pbs[(w - 1) % 2].free = [t1, t2]
            src = q.ap
        win = 2 ** (g + 1)
        t3 = tt(src[:, 0:win], src[:, 0:win], C("inv")[:, 0:win], ALU.mult, ts0)
        t4 = stt(y[:, 0:win], y[:, 0:win], -1.0, src[:, 0:win], ALU.mult, ALU.add, t3)
        t5_ = stt(y[:, win:], src[:, win:], 1.0 / win, y[:, win:], ALU.mult, ALU.subtract, ts0)
        q.free = [t4, t5_]
        for j in range(2):
            pass
        y_ready[4 + g] = [t4, t5_]
    finish(prev)
    for g in range(4):
        for j in range(2):
            x = aux.take()
            yj = Y[:, 4 + g, j * 512:(j + 1) * 512]
            d = PE.mark(PE.after(x.free, y_ready[4 + g], t_wp).matmul(x.ap, wp[:, g, :], yj, start=True, stop=True))
            t = act(yj, x.ap, ACT.Copy, d, scale=V("pscale", g))
            x.free = [t]
        y_ready[4 + g] = t
    for k in range(8):
        h_ready[k] = put_h(k, Y[:, k, :], y_ready[k])
    split_y = [list(t) for t in h_ready]
    mix_done = [y_ready, split_y, hd3_free, Pm_free, kd_free, h3_free, p_free, t_uT, t_eT, t_si,
                [q.free for q in pbs], [q.free for q in aux.slots]]
    s6.close()

    s7 = ExitStack()
    hdh = sb("hdh3", [P, 4, T], FR, s7)
    hdl = sb("hdl3", [P, 4, T], FR, s7)
    t7 = sb("t7", [P, 6, T], F, s7)
    R7 = sb("R7", [P, T], F, s7)[:, :]
    sqr = Ring([Slot(t7[:, i, :]) for i in range(3)])
    tr = Ring([Slot(t7[:, 3 + i, :]) for i in range(3)])
    for q in sqr.slots + tr.slots:
        q.free = [mix_done]
    hd_free4 = [[mix_done] for _ in range(4)]

    class Sums:

        def __init__(self):
            self.banks = [aux.take(), aux.take()]
            self.n = 0

        def add(self, ap, *tokens):
            if self.n == 0:
                PE.after(self.banks[0].free, self.banks[1].free)
            PE.after(*tokens)
            for j in range(2):
                ins = nc.tensor.matmul(self.banks[j].ap, ones, ap[:, j * 512:(j + 1) * 512],
                                       start=(self.n == 0), stop=(self.n == 7))
            self.n += 1
            self.d = PE.mark(ins)

    def layer_norm(sums_, g, b, use):
        st = Stats(sqr)
        for k in range(8):
            for j in range(2):
                xj = X[:, k, j * 512:(j + 1) * 512]
                t = stt(xj, sums_.banks[j].ap, -1.0 / 1024, xj, ALU.mult, ALU.add, sums_.d, x_ready[k])
            x_ready[k] = t
            st.add(X[:, k, :], t)
        for q in sums_.banks:
            q.free = [t]
        r = st.inverse_root(R7, LN_EPS, mix_done)
        for k in range(8):
            t = stt(X[:, k, :], X[:, k, :], V(g, k), R7, ALU.mult, ALU.mult, r, x_ready[k])
            x_ready[k] = act(X[:, k, :], X[:, k, :], ACT.Identity, t, bias=V(b, k))
            use(k)

    sm = Sums()
    late = None
    nxt = fetch_xs(0)
    for m in range(8):
        q, ld = nxt
        if m < 7:
            nxt = fetch_xs(m + 1)
        pr, d, _ = gemm_fm(last=(m == 7))
        x_ready[m] = stt(X[:, m, :], q.ap, ALPHA, flat(pr.ap), ALU.mult, ALU.add, d, ld, split_y[m])
        pr.free, q.free = [x_ready[m]], [x_ready[m]]
        if late is not None:
            sm.add(X[:, late, :], x_ready[late])
        late = m
    sm.add(X[:, 7, :], x_ready[7])

    def split_x(k):
        h_ready[k] = put_h(k, X[:, k, :], x_ready[k])
        x_ready[k] = ts(X[:, k, :], X[:, k, :], ALPHA, None, ALU.mult, None, h_ready[k])

    layer_norm(sm, "ln1_g", "ln1_b", split_x)
    sm2 = Sums()
    pend = []

    def summed(m):
        pend.append(m)
        if len(pend) > 1:
            k = pend.pop(0)
            sm2.add(X[:, k, :], x_ready[k])

    mlp(summed)
    sm2.add(X[:, 7, :], x_ready[7])
    layer_norm(sm2, "ln2_g", "ln2_b", lambda k: store(A["out"][k], X[:, k, :], x_ready[k]))
    SP.after(*stores)


def slabs(I):
    def cut(w, cols):
        return [w[:, c:c + 128].reshape(8, 128, 128).transpose(1, 0, 2).reshape(128, 1024) for c in cols]

    def mlp(up, down):
        out = []
        for g in range(8):
            out += cut(up, [512 * g + 128 * k for k in range(4)])
            d = down[512 * g:512 * (g + 1)].reshape(4, 128, 4, 2, 128).transpose(2, 1, 3, 0, 4)
            out += [d[m].reshape(128, 1024) for m in range(4)]
        return out

    out = []
    w = I["w_in"][0]
    for h in range(8):
        out += cut(w, [4096 + 128 * h, 3072 + 128 * h, 5120 + 128 * h])
    out += cut(w, [8192 + 128 * m for m in range(8)])
    for m in range(8):
        out += cut(w, [128 * m, 1024 + 128 * m, 6144 + 128 * m, 2048 + 128 * m])
    out += cut(w, [7168 + 128 * m for m in range(8)])
    for name in ("w_conv_out", "w_rec_out", "w_out"):
        out += cut(I[name][0], [128 * m for m in range(8)])
    w = I["w_in_2"][0]
    for j in range(4):
        out += cut(w, [128 * j, 512 + 128 * j, 1024 + 128 * j])
    for m in range(2):
        out += cut(w, [1792 + 128 * m, 2048 + 128 * m, 1536 + 128 * m])
    out += cut(w, [2304, 2432, 2560, 2688])
    out += cut(I["w_out_2"][0], [128 * m for m in range(8)])
    out += mlp(I["w_up_2"][0], I["w_down_2"][0])
    w = I["w_in_3"][0]
    g = np.zeros((1024, 128), np.float32)
    g[:, 0:4] = w[:, 1536:1540]
    g[:, 32:36] = w[:, 1540:1544]
    out += cut(g, [0])
    for h in range(4):
        out += cut(w, [128 * h, 512 + 128 * h, 1024 + 128 * h, 1544 + 128 * h])
    out += cut(w, [2056 + 128 * g for g in range(4)])
    out += cut(I["w_out_3"][0], [128 * m for m in range(8)])
    out += mlp(I["w_ff1_3"][0], I["w_ff2_3"][0])
    return out


def consts():
    cst = np.zeros((128, NCONST), np.float32)

    def put(name, a):
        c0, w = CONSTS[name]
        cst[:a.shape[0], c0:c0 + w] = a.reshape(a.shape[0], -1)

    put("ident", np.eye(128, dtype=np.float32))
    put("ones", np.ones((128, 128), np.float32))
    a = np.zeros((128, 8, 8), np.float32)
    b = np.zeros((8, 8, 128), np.float32)
    for h in range(8):
        a[:, h, h] = 1
        b[h, h, :] = 1
    put("selA8", a)
    put("selB8", b)
    a = np.zeros((128, 4, 8), np.float32)
    b = np.zeros((8, 4, 128), np.float32)
    for t in range(4):
        a[:64, t, 2 * t] = 1
        a[64:, t, 2 * t + 1] = 1
        b[2 * t, t, :64] = 1
        b[2 * t + 1, t, 64:] = 1
    put("selA4", a)
    put("selB4", b)
    s, t = np.arange(128)[:, None], np.arange(128)[None, :]
    put("inv", np.broadcast_to((1.0 / np.arange(1, 17)).astype(np.float32), (128, 16)))
    put("tri", (s <= t).astype(np.float32))
    put("tril_neg", np.where(s <= t, 0, NEG).astype(np.float32))
    masks = np.stack([((s // (2 * h) == t // (2 * h)) & (s % (2 * h) < h) & (t % (2 * h) >= h))
                      for h in HALVES], 1).astype(np.float32)
    return cst, np.ascontiguousarray(masks.reshape(128, -1))


def vectors(I):
    v = np.zeros((128, NVEC), np.float32)

    def put(name, a):
        c0, w = VECS[name]
        v[:, c0:c0 + w] = a.reshape(w, 128).T

    put("norm_g", I["norm_g"])
    put("conv_w", I["conv_w"])
    put("conv_b", I["conv_b"])
    put("ln_g", I["ln_g"])
    put("ln_b", I["ln_b"])
    put("lb0", I["lb_logits"][0])
    put("lb1", I["lb_logits"][1])
    put("gnorm_g", I["gnorm_g"])
    put("final_g", I["final_g"])
    put("mix_g", I["mix_norm_g_2"])
    put("cw2", I["conv_w_2"])
    put("gg2", I["group_norm_g_2"])
    put("mlp_g2", I["mlp_norm_g_2"])
    put("fin_g2", I["final_norm_g_2"])
    put("cw3", I["w_conv_3"])
    put("hn_g", I["hn_g_3"])
    put("pscale", I["pool_scale_3"])
    put("ln1_g", I["ln1_g_3"])
    put("ln1_b", I["ln1_b_3"])
    put("ln2_g", I["ln2_g_3"])
    put("ln2_b", I["ln2_b_3"])
    v[0:4, VECS["b_i"][0]] = I["b_gate_3"][0, 0:4]
    v[0:4, VECS["b_f"][0]] = I["b_gate_3"][0, 4:8]
    return v


def layout(I):
    x = np.concatenate([I["meta_tokens"], I["x"][0]], 0)
    cst, masks = consts()
    rel = np.clip(np.arange(128)[:, None] + 512 - np.arange(BAND)[None, :], -128, 128) + 128
    bias = I["rel_bias_2"][0][:, rel]
    bias[:, 0:64, BAND - 64:] = NEG
    bias[:, 64:, 0:64] = NEG
    sgc = np.empty((128, 3, 256), np.float32)
    sgc[:, 0, :] = I["sg_ln_g_2"][0]
    sgc[:, 1, :] = I["sg_ln_b_2"][0]
    sgc[:, 2, :] = np.repeat(I["sg_b_2"][0].reshape(2, 2, 128).transpose(1, 0, 2), 64, 0).reshape(128, 256)
    return {
        "w_pool": np.ascontiguousarray(I["w_pool_3"][0].transpose(1, 0, 2).reshape(128, 512)),
        "bias": bias,
        "sgw": np.ascontiguousarray(I["sg_w_2"][0].transpose(2, 0, 1).reshape(128, 512)),
        "sgc": sgc.reshape(128, 768),
        "xin": np.ascontiguousarray(x.T.reshape(8, 128, TM)),
        "wts": np.stack(slabs(I)),
        "vec": vectors(I),
        "cst": cst,
        "masks": masks,
    }


_INS = ("xin", "wts", "vec", "cst", "masks", "bias", "sgw", "sgc", "w_pool")


def kernel(**inputs):
    import concourse.bacc as bacc
    from concourse.bass_utils import run_bass_kernel_spmd

    laid = layout({k: np.asarray(v) for k, v in inputs.items()})
    nc = bacc.Bacc("TRN2", target_bir_lowering=False, num_devices=1)
    arrays, A = {}, {}
    for name in _INS:
        a = np.ascontiguousarray(laid[name])
        arrays["in_" + name] = a
        A[name] = nc.dram_tensor("in_" + name, a.shape, F, kind="ExternalInput").ap()
    A["out"] = nc.dram_tensor("out_y", [KT, P, T], F, kind="ExternalOutput").ap()
    program(nc, A)
    r = run_bass_kernel_spmd(nc, [arrays], core_ids=[0])
    y = np.asarray(r.results[0]["out_y"])
    return np.ascontiguousarray(y.reshape(D_MODEL, T).T)[None]
```

```python
from contextlib import ExitStack

import numpy as np

import concourse.bass as bass
from concourse import mybir

F = mybir.dt.float32
FR = mybir.dt.float32r
I32 = mybir.dt.int32
ACT = mybir.ActivationFunctionType
ALU = mybir.AluOpType
AX = mybir.AxisListType.X

P = 128
D_MODEL = 1024
T = 1024
KT = 8
META = 16
TM = T + META
TAPS = 31
HIST = TAPS - 1
EPS = 1e-6
LN_EPS = 1e-5
HALVES = (64, 32, 16, 8, 4, 2, 1)
ALPHA = 2.0 ** 0.25
NEG = -1e30
BAND = 640

VECS = {}
_n = 0
for _name, _w in (("norm_g", 8), ("conv_w", 8 * TAPS), ("conv_b", 8), ("ln_g", 8), ("ln_b", 8), ("lb0", 8),
                  ("lb1", 8), ("gnorm_g", 8), ("final_g", 8), ("mix_g", 8), ("cw2", 6), ("gg2", 8),
                  ("mlp_g2", 8), ("fin_g2", 8), ("cw3", 32), ("hn_g", 4), ("pscale", 4), ("ln1_g", 8),
                  ("ln1_b", 8), ("ln2_g", 8), ("ln2_b", 8), ("b_i", 1), ("b_f", 1)):
    VECS[_name] = (_n, _w)
    _n += _w
NVEC = _n
CONSTS = {}
_n = 0
for _name, _w in (("ident", 128), ("ones", 128), ("selA8", 64), ("selB8", 1024), ("selA4", 32),
                  ("selB4", 512), ("tri", 128), ("tril_neg", 128),
                  ("inv", 16)):
    CONSTS[_name] = (_n, _w)
    _n += _w
NCONST = _n


class Lane:

    def __init__(self, eng, sem):
        self.eng, self.sem, self.count, self.seen = eng, sem, 0, {}

    def after(self, *tokens):
        for t in tokens:
            if t is None:
                continue
            if isinstance(t, list):
                self.after(*t)
                continue
            sem, value = t
            if self.seen.get(id(sem), 0) < value:
                self.eng.wait_ge(sem, value)
                self.seen[id(sem)] = value
        return self.eng

    def mark(self, instruction):
        self.count += 1
        instruction.then_inc(self.sem, 1)
        return (self.sem, self.count)


class Port:

    def __init__(self, lane, sem):
        self.lane, self.sem, self.count = lane, sem, 0

    def start(self, out, in_, *tokens):
        if self.count:
            self.lane.after((self.sem, self.count))
        self.lane.after(*tokens)
        self.count += 16
        self.lane.eng.dma_start(out, in_).then_inc(self.sem, 16)
        return (self.sem, self.count)


class Slot:

    def __init__(self, ap):
        self.ap, self.free = ap, []


class Ring:
    def __init__(self, slots):
        self.slots, self.n = slots, 0

    def take(self):
        s = self.slots[self.n % len(self.slots)]
        self.n += 1
        return s


def program(nc, A, stage=99):
    ctx = ExitStack()

    def sem(name):
        return ctx.enter_context(nc.semaphore(name))

    PE = Lane(nc.tensor, sem("pe_done"))
    VE = Lane(nc.vector, sem("dve_done"))
    SE = Lane(nc.scalar, sem("act_done"))
    GP = Lane(nc.gpsimd, sem("pool_done"))
    SP = Lane(nc.sync, sem("sp_done"))

    def sb(name, shape, dt=F, scope=ctx):
        return scope.enter_context(nc.sbuf_tensor(name, shape, dt))

    raw = sb("raw", [P, 2, KT * 128])
    wh = sb("wh", [P, 2, KT * 128], FR)
    wl = sb("wl", [P, 2, KT * 128], FR)
    hh = sb("hh", [P, KT, TM], FR)
    hl = sb("hl", [P, KT, TM], FR)
    vec = sb("vec", [P, NVEC])
    cst = sb("cst", [P, NCONST])
    psum = ctx.enter_context(nc.psum_tensor("psum", [P, 8, 512], F))

    def V(name, i=0, n=1):
        return vec[:, VECS[name][0] + i:VECS[name][0] + i + n]

    def C(name, parts=P):
        a, w = CONSTS[name]
        return cst[0:parts, a:a + w]

    ident, ones = C("ident"), C("ones")
    selA8 = C("selA8").rearrange("p (h m) -> p h m", h=8)
    selB8 = C("selB8", 8).rearrange("p (h m) -> p h m", h=8)
    selA4 = C("selA4").rearrange("p (t m) -> p t m", t=4)
    selB4 = C("selB4", 8).rearrange("p (t m) -> p t m", t=4)

    pairs = Ring([Slot(psum[:, 0:2, :]), Slot(psum[:, 2:4, :])])
    small = Slot(psum[:, 4, :])
    aux = Ring([Slot(psum[:, 5, :]), Slot(psum[:, 6, :]), Slot(psum[:, 7, :])])

    load_port = Ring([Port(SP, sem(f"ld{i}")) for i in range(4)])
    store_port = Ring([Port(SP, sem(f"st{i}")) for i in range(4)])
    w_port = [Port(SP, sem(f"wt{i}")) for i in range(2)]
    stores = []

    def load(out, in_, *tokens):
        return load_port.take().start(out, in_, *tokens)

    def store(out, in_, *tokens):
        t = store_port.take().start(out, in_, *tokens)
        stores.append(t)
        return t

    def act(out, in_, func, *tokens, **kw):
        return SE.mark(SE.after(*tokens).activation(out, in_, func, **kw))

    def tt(out, a, b, op, *tokens, lane=None):
        lane = lane or VE
        return lane.mark(lane.after(*tokens).tensor_tensor(out, a, b, op))

    def ts(out, a, s1, s2, op0, op1, *tokens):
        if s2 is None:
            return VE.mark(VE.after(*tokens).tensor_scalar(out, a, s1, None, op0))
        return VE.mark(VE.after(*tokens).tensor_scalar(out, a, s1, s2, op0, op1))

    def stt(out, a, s, b, op0, op1, *tokens):
        return VE.mark(VE.after(*tokens).scalar_tensor_tensor(out, a, s, b, op0, op1))

    def copy(out, in_, *tokens):
        return VE.mark(VE.after(*tokens).tensor_copy(out, in_))

    def recip(out, in_, *tokens):
        return VE.mark(VE.after(*tokens).reciprocal(out, in_))

    def zero(out, value, *tokens):
        return VE.mark(VE.after(*tokens).memset(out, value))

    def fp(ap):
        return ap.bitcast(F)

    jobs = []

    def pump(n=1):
        for _ in range(n):
            if not jobs:
                return
            try:
                next(jobs[0])
            except StopIteration:
                jobs.pop(0)

    def drain_jobs():
        while jobs:
            pump()

    def finish(job):
        while job in jobs:
            pump()

    NSLAB = A["wts"].shape[0]
    raw_free = [[], []]
    w_free = [[], []]
    raw_got = {}
    w_got = {}

    def w_fetch(i):
        if i < NSLAB and i not in raw_got:
            raw_got[i] = w_port[i % 2].start(raw[:, i % 2, :], A["wts"][i], raw_free[i % 2])

    def w_split(i):
        if i < NSLAB and i not in w_got:
            w_fetch(i)
            s = i % 2
            a = act(wh[:, s, :], raw[:, s, :], ACT.Copy, raw_got[i], w_free[s])
            b = tt(wl[:, s, :], raw[:, s, :], fp(wh[:, s, :]), ALU.subtract, a, w_free[s], lane=GP)
            raw_free[s] = [a, b]
            w_got[i] = [a, b]

    slab_no = [0]

    def next_slab():
        i = slab_no[0]
        slab_no[0] += 1
        w_split(i)
        w_fetch(i + 1)
        w_split(i + 1)
        w_fetch(i + 2)
        return i

    h_ready = [[] for _ in range(KT)]
    h_free = [[] for _ in range(KT)]

    def three(i, k):
        s = i % 2
        a, b = wh[:, s, k * 128:(k + 1) * 128], wl[:, s, k * 128:(k + 1) * 128]
        return a, b

    def gemm_fm(meta=False, last=False, src=None, ready=None, nk=KT, koff=0, slab=None, base=0):
        own = slab is None
        i = next_slab() if own else slab
        srch, srcl = src or (hh, hl)
        ready = h_ready if ready is None else ready
        off = META if src is None else 0
        pr = pairs.take()
        PE.after(w_got[i], pr.free)
        if meta:
            PE.after(small.free)
        frees = []
        for k in range(nk):
            PE.after(ready[k])
            a, b = three(i, k + base)
            n = 0
            for w, x in ((a, srch), (b, srch), (a, srcl)):
                first, final = k == 0 and n == 0, k == nk - 1 and n == 2
                for j in range(2):
                    ins = nc.tensor.matmul(pr.ap[:, j, :], w, x[:, k, off + j * 512:off + (j + 1) * 512],
                                           start=first, stop=final)
                if meta:
                    ins = nc.tensor.matmul(small.ap[:, 0:META], w, x[:, k, 0:META], start=first, stop=final)
                n += 1
            if last and k < nk - 1:
                frees.append([PE.mark(ins)])
            if k < nk - 1:
                pump()
        done = PE.mark(ins)
        frees.append([done])
        if own:
            w_free[i % 2] = [done]
        if last:
            for k in range(nk):
                h_free[k] = frees[k]
        pump()
        return pr, done, i

    def turn(blocks, g, *tokens):
        x = aux.take()
        PE.after(x.free, *tokens)
        for c in range(4):
            ins = nc.tensor.transpose(x.ap[:, c * 128:(c + 1) * 128], blocks[:, 4 * g + c, :], ident)
        d = PE.mark(ins)
        t = act(blocks[:, 4 * g:4 * g + 4, :], x.ap.rearrange("p (c t) -> p c t", c=4), ACT.Copy, d)
        x.free = [t]
        return t

    def put_h(k, src, *tokens, c0=META, n=T):
        a = act(hh[:, k, c0:c0 + n], src, ACT.Copy, *tokens, h_free[k])
        b = tt(hl[:, k, c0:c0 + n], src, fp(hh[:, k, c0:c0 + n]), ALU.subtract, a, *tokens)
        return [a, b]

    t_vec = load(vec[:, :], A["vec"])
    t_cst = load(cst[:, :], A["cst"])
    for ln in (PE, VE, SE, GP):
        ln.after(t_vec, t_cst)

    def flat(ap):
        return ap.rearrange("p a b -> p (a b)")

    O = B0 = sb("B0", [P, KT, T])
    s0 = ExitStack()
    X0 = sb("X0", [P, KT, TM], F, s0)
    sq0 = sb("sq0", [P, 2, TM], F, s0)
    R0 = sb("R0", [P, TM], F, s0)

    def sums(tiles, sqs, width, lhs=ones, square=True, rows=P, meta=False, tag=None):
        pr = pairs.take()
        PE.after(pr.free)
        if meta:
            PE.after(small.free)
        n = len(tiles)
        for t, (ap, toks) in enumerate(tiles):
            if square:
                q = sqs.take()
                a = act(q.ap[:, 0:width], ap, ACT.Square, toks, q.free)
                src = q.ap
            else:
                a, src = toks, ap
            PE.after(a)
            l = lhs(t) if callable(lhs) else lhs
            off = META if meta else 0
            for j in range(2):
                ins = nc.tensor.matmul(pr.ap[0:rows, j, :], l, src[:, off + j * 512:off + (j + 1) * 512],
                                       start=(t == 0), stop=(t == n - 1))
            if meta:
                ins = nc.tensor.matmul(small.ap[0:rows, 0:META], l, src[:, 0:META],
                                       start=(t == 0), stop=(t == n - 1))
            d = PE.mark(ins)
            if square:
                q.free = [d]
        return pr, d

    tx = [load(X0[:, k, :], A["xin"][k]) for k in range(KT)]
    sqr = Ring([Slot(sq0[:, i, :]) for i in range(2)])
    pr, d = sums([(X0[:, k, :], tx[k]) for k in range(KT)], sqr, TM, meta=True)
    a = act(R0[:, META:TM], flat(pr.ap), ACT.Sqrt, d, scale=1.0 / 1024, bias=EPS)
    b = act(R0[:, 0:META], small.ap[:, 0:META], ACT.Sqrt, d, scale=1.0 / 1024, bias=EPS)
    pr.free, small.free = [a], [b]
    r = recip(R0[:, :], R0[:, :], a, b)
    for k in range(KT):
        c = stt(X0[:, k, :], X0[:, k, :], V("norm_g", k), R0[:, :], ALU.mult, ALU.mult, r, tx[k], d)
        h_ready[k] = put_h(k, X0[:, k, :], c, c0=0, n=TM)
    s0_done = [t for k in range(KT) for t in h_ready[k]]
    s0.close()

    s1 = ExitStack()
    masks = sb("masks", [P, 7, 128], F, s1)
    rmask = sb("rmask", [P, TM], F, s1)
    fb = sb("fb", [P, 2, TM], F, s1)
    kb = sb("kb", [P, 2, TM], F, s1)
    qb = sb("qb", [P, 2, T], F, s1)
    vb = sb("vb", [P, 2, T], F, s1)
    vm = sb("vm", [META, 128], F, s1)
    vmT = sb("vmT", [P, 2, META], F, s1)
    work = sb("work", [P, 4, TM], F, s1)
    Ab = sb("Ab", [P, T], F, s1)
    kdT = sb("kdT", [P, T], F, s1)
    kdm = sb("kdm", [META, 128], F, s1)
    Sb = sb("Sb", [P, T], F, s1)
    ebl = sb("ebl", [P, 2, 9], F, s1)
    lbv = sb("lbv", [P, 4, 8], F, s1)
    t_mask = load(flat(masks[:, :, :]), A["masks"], s0_done)
    z1 = zero(rmask[:, :], 1.0, s0_done)
    z2 = zero(rmask[:, META:TM].rearrange("p (c t) -> p c t", c=8)[:, :, 0:1], 0.0, z1)
    mx = tt(lbv[:, 0, :], V("lb0", 0, 8), V("lb1", 0, 8), ALU.max, s0_done)
    l0 = tt(lbv[:, 1, :], V("lb0", 0, 8), lbv[:, 0, :], ALU.subtract, mx)
    l1 = tt(lbv[:, 2, :], V("lb1", 0, 8), lbv[:, 0, :], ALU.subtract, mx)
    e0 = act(lbv[:, 1, :], lbv[:, 1, :], ACT.Exp, l0)
    e1 = act(lbv[:, 2, :], lbv[:, 2, :], ACT.Exp, l1)
    l2 = tt(lbv[:, 0, :], lbv[:, 1, :], lbv[:, 2, :], ALU.add, e0, e1)
    l3 = recip(lbv[:, 0, :], lbv[:, 0, :], l2)
    l4 = tt(lbv[:, 1, :], lbv[:, 1, :], lbv[:, 0, :], ALU.mult, l3)
    l5 = ts(lbv[:, 2, :], lbv[:, 1, :], -1.0, 1.0, ALU.mult, ALU.add, l4)
    lb_ready = [l4, l5]
    LB = lbv[:, 1, :]
    OML = lbv[:, 2, :]

    wk = Ring([Slot(work[:, i, :]) for i in range(4)])
    Aslot, kdslot, sslot = Slot(Ab), Slot(kdT), Slot(Sb)
    hd_free, vm_free = [[], []], [[]]
    o_ready = [None] * 8
    A4 = lambda ap: ap.rearrange("p (c t) -> p c t", c=8)

    def half(ap, hs):
        v = ap.rearrange("p (n b) -> p n b", b=2 * hs)
        return v[:, :, 0:hs], v[:, :, hs:2 * hs]

    def hgrn(h, s, tf, tq, tv):
        f, kk, q, v = fb[:, s, :], kb[:, s, :], qb[:, s, :], vb[:, s, :]
        bx, kx = f[:, META:TM], kk[:, META:TM]
        lastb = A4(bx)[:, :, 127:128]
        kfree, a_tok = [None, None], [None, None]
        lev = [None] * 7

        a = ts(f, f, OML[:, h:h + 1], LB[:, h:h + 1], ALU.mult, ALU.add, tf, lb_ready)
        tk = ts(kk, f, -1.0, 1.0, ALU.mult, ALU.add, a, hd_free[s])
        a = ts(f, f, 2.0 ** -63, None, ALU.max, None, a, tk)
        tv0 = turn(A4(v), 0, tv)
        yield
        w = wk.take()
        a = act(w.ap, f, ACT.Ln, a, w.free)
        tb = VE.mark(VE.after(a, z2).tensor_tensor_scan(f, rmask[:, :], w.ap, 0.0, ALU.mult, ALU.add))
        w.free = [tb]
        tv = [tv0, turn(A4(v), 1, tv), tv]
        yield

        def below(lv):
            hs = HALVES[lv]
            w = wk.take()
            bv = bx.rearrange("p (n b) -> p n b", b=2 * hs)
            t = tt(w.ap[:, 0:T].rearrange("p (n b) -> p n b", b=2 * hs), bv,
                   bv[:, :, hs - 1:hs].to_broadcast([P, T // (2 * hs), 2 * hs]), ALU.subtract, tb, w.free, lane=GP)
            lev[lv] = [w, t]

        def exps(lv):
            w, t = lev[lv]
            ul, ur = half(w.ap[:, 0:T], HALVES[lv])
            lev[lv][1] = (act(ul, ul, ACT.Exp, t, scale=-1.0), act(ur, ur, ACT.Exp, t))

        def mults(lv):
            w, (e1, e2) = lev[lv]
            ul, ur = half(w.ap[:, 0:T], HALVES[lv])
            lev[lv][1] = [tt(ul, ul, half(kx, HALVES[lv])[0], ALU.mult, e1, tk),
                          tt(ur, ur, half(q, HALVES[lv])[1], ALU.mult, e2, tq)]

        def product(lv, g):
            if lv < 7:
                w, tok = lev[lv]
                left = right = w.ap
                m = masks[:, lv:lv + 1, :]
            else:
                left, right, tok = kx, q, [tk, tq]
                m = ident.rearrange("p (o t) -> p o t", o=1)
            x = aux.take()
            PE.after(x.free, tok)
            for c in range(4 * g, 4 * g + 4):
                ins = nc.tensor.matmul(x.ap[:, (c % 4) * 128:(c % 4 + 1) * 128],
                                       left[:, c * 128:(c + 1) * 128], right[:, c * 128:(c + 1) * 128],
                                       start=True, stop=True)
            d = PE.mark(ins)
            dst = Ab[:, g * 512:(g + 1) * 512].rearrange("p (c t) -> p c t", c=4)
            src = x.ap.rearrange("p (c t) -> p c t", c=4)
            m = m.to_broadcast([P, 4, 128])
            if lv == 7:
                t = tt(dst, src, m, ALU.mult, d, Aslot.free)
            else:
                t = VE.mark(VE.after(d, a_tok[g], t_mask).copy_predicated(dst, m.bitcast(I32), src))
                if g:
                    w.free = [d]
            a_tok[g] = t
            x.free = [t]

        def turned(g):
            x = aux.take()
            PE.after(kd, x.free)
            for c in range(4):
                ins = nc.tensor.transpose(x.ap[:, c * 128:(c + 1) * 128],
                                          wd.ap[:, META + (4 * g + c) * 128:META + (4 * g + c + 1) * 128], ident)
            d = PE.mark(ins)
            kfree[g] = act(kdT[:, g * 512:(g + 1) * 512], x.ap, ACT.Copy, d, kdslot.free)
            x.free = [kfree[g]]

        te1 = act(ebl[:, s, 0:1], f[:, META - 1:META], ACT.Exp, tb, hd_free[s])
        te2 = act(ebl[:, s, 1:9], lastb.rearrange("p c o -> p (c o)"), ACT.Exp, tb, hd_free[s])
        wd = wk.take()
        c1 = tt(A4(wd.ap[:, META:TM]), lastb.to_broadcast([P, 8, 128]), A4(bx), ALU.subtract, tb, wd.free)
        c2 = tt(wd.ap[:, 0:META], f[:, META - 1:META].to_broadcast([P, META]), f[:, 0:META], ALU.subtract,
                tb, wd.free)
        e = act(wd.ap, wd.ap, ACT.Exp, c1, c2)
        below(0)
        below(1)
        product(7, 0)
        yield
        kd = tt(wd.ap, wd.ap, kk, ALU.mult, e, tk)
        product(7, 1)
        exps(0)
        yield
        turned(0)
        mults(0)
        exps(1)
        yield
        turned(1)
        mults(1)
        below(2)
        yield
        product(0, 0)
        x = aux.take()
        PE.after(x.free)
        d = PE.mark(nc.tensor.transpose(x.ap[0:META, 0:128], wd.ap[:, 0:META], ident))
        wd.free = [d]
        gm = act(kdm[:, :], x.ap[0:META, 0:128], ACT.Copy, d, kdslot.free)
        x.free = [gm]
        x = aux.take()
        PE.after(x.free)
        d = PE.mark(nc.tensor.transpose(x.ap[0:META, 0:128], vmT[:, s, :], ident))
        gv = act(vm[:, :], x.ap[0:META, 0:128], ACT.Copy, d, vm_free[0])
        x.free = [gv]
        exps(2)
        below(3)
        yield
        x = aux.take()
        PE.after(x.free, gm, gv, tv)
        d = PE.mark(nc.tensor.matmul(x.ap[:, 0:128], kdm[:, :], vm[:, :], start=True, stop=True))
        vm_free[0] = [d]
        ss = act(Sb[:, 0:128], x.ap[:, 0:128], ACT.Copy, d, sslot.free)
        x.free = [ss]
        product(0, 1)
        yield

        def state(g, ss):
            x = aux.take()
            PE.after(x.free, kfree[g])
            n = 4 if g == 0 else 3
            for c in range(4 * g, 4 * g + n):
                ins = nc.tensor.matmul(x.ap[:, (c % 4) * 128:(c % 4 + 1) * 128], kdT[:, c * 128:(c + 1) * 128],
                                       v[:, c * 128:(c + 1) * 128], start=True, stop=True)
            d = PE.mark(ins)
            for c in range(4 * g, 4 * g + n):
                ss = stt(Sb[:, (c + 1) * 128:(c + 2) * 128], Sb[:, c * 128:(c + 1) * 128],
                         ebl[:, s, c + 1:c + 2], x.ap[:, (c % 4) * 128:(c % 4 + 1) * 128],
                         ALU.mult, ALU.add, ss, d, te1, te2)
            x.free = [ss]
            kdslot.free = [d]
            return ss

        w2 = None
        for lv in range(1, 7):
            if lv < 6:
                mults(lv + 1)
            product(lv, 0)
            if lv < 5:
                exps(lv + 2)
            elif lv == 5:
                w2 = wk.take()
                qe = w2.ap[:, 0:T]
                e = act(qe, bx, ACT.Exp, tb, w2.free)
            yield
            if lv < 4:
                below(lv + 3)
            if lv == 6:
                tqe = tt(qe, qe, q, ALU.mult, e, tq)
            product(lv, 1)
            if lv in (2, 4):
                yield
                ss = state(lv // 2 - 1, ss)
            yield
        for g in range(2):
            x = aux.take()
            PE.after(x.free, a_tok[g], tqe, ss, tv)
            for c in range(4 * g, 4 * g + 4):
                o = x.ap[:, (c % 4) * 128:(c % 4 + 1) * 128]
                cc = slice(c * 128, (c + 1) * 128)
                nc.tensor.matmul(o, v[:, cc], Ab[:, cc], start=True, stop=False)
                ins = nc.tensor.matmul(o, Sb[:, cc], qe[:, cc], start=False, stop=True)
            d = PE.mark(ins)
            t = act(O[:, h, g * 512:(g + 1) * 512], x.ap, ACT.Copy, d)
            x.free = [t]
            if g == 0:
                yield
        w2.free = [d]
        Aslot.free, sslot.free = [d], [d]
        hd_free[s] = [d, t]
        o_ready[h] = t

    prev = None
    for h in range(8):
        s = h % 2
        pr, d, _ = gemm_fm(meta=True)
        a = act(fb[:, s, META:TM], flat(pr.ap), ACT.Sigmoid, d, hd_free[s], z2)
        b = act(fb[:, s, 0:META], small.ap[:, 0:META], ACT.Sigmoid, d)
        pr.free, small.free = [a], [b]
        tf = [a, b]
        pr, d, _ = gemm_fm()
        tq = act(qb[:, s, :], flat(pr.ap), ACT.Silu, d, hd_free[s])
        pr.free = [tq]
        pr, d, _ = gemm_fm(meta=True)
        a = act(vb[:, s, :], flat(pr.ap), ACT.Copy, d, hd_free[s])
        b = act(vmT[:, s, :], small.ap[:, 0:META], ACT.Copy, d, hd_free[s])
        pr.free, small.free = [a], [b]
        if prev is not None:
            finish(prev)
        prev = hgrn(h, s, tf, tq, [a, b])
        jobs.append(prev)

    GR = nc.dram_tensor("keep_gr", [KT, P, T], F, kind="Internal").ap()
    GC = nc.dram_tensor("keep_gc", [KT, P, T], F, kind="Internal").ap()
    SZ = nc.dram_tensor("keep_sz", [KT, P, T], F, kind="Internal").ap()
    gr_kept, gc_kept, sz_kept = [None] * 8, [None] * 8, [None] * 8

    def gate_out(buf, dram, m, func):
        pr, d, _ = gemm_fm()
        a = act(buf.ap, flat(pr.ap), func, d, buf.free)
        pr.free = [a]
        t = store(dram[m], buf.ap, a)
        buf.free = [t]
        return t

    gbuf = Ring([Slot(qb[:, 0, :]), Slot(vb[:, 0, :])])
    for g in gbuf.slots:
        g.free = [hd_free[0]]
    for m in range(8):
        gr_kept[m] = gate_out(gbuf.take(), GR, m, ACT.Sigmoid)
    finish(prev)
    s1_done = [hd_free[0], hd_free[1], gr_kept]
    s1.close()

    s2 = ExitStack()
    Cb = sb("Cb", [P, KT, T], F, s2)
    s3 = ExitStack()
    av = sb("av", [P, 2, HIST + T], F, s3)
    sg = sb("sg", [P, 2, TM], F, s3)
    tmp = sb("tmp", [P, 3, T], F, s3)
    R8 = sb("R8", [8, T], F, s3)
    tr = Ring([Slot(tmp[:, i, :]) for i in range(3)])
    for q in tr.slots:
        q.free = [s1_done]

    pr, d = sums([(O[:, h, :], [o_ready[h]]) for h in range(8)], tr, T, lhs=lambda h: selA8[:, h, :], rows=8)
    a = act(R8[:, :], flat(pr.ap[0:8, :, :]), ACT.Sqrt, d, s1_done, scale=1.0 / 128, bias=EPS)
    pr.free = [a]
    r8 = recip(R8[:, :], R8[:, :], a)

    avs = [Slot(av[:, i, :]) for i in range(2)]
    sgs = [Slot(sg[:, i, :]) for i in range(2)]
    za = zero(av[:, :, 0:HIST - META], 0.0, s1_done)
    for q in avs + sgs:
        q.free = [za, s1_done]
    c_ready = [None] * 8
    for m in range(8):
        u, w = avs[m % 2], sgs[m % 2]
        pr, d, _ = gemm_fm(meta=True)
        a = act(u.ap[:, HIST:], flat(pr.ap), ACT.Copy, d, u.free)
        b = act(u.ap[:, HIST - META:HIST], small.ap[:, 0:META], ACT.Copy, d)
        pr.free, small.free = [a], [b]
        pr, d, _ = gemm_fm(meta=True)
        a2 = act(w.ap[:, META:], flat(pr.ap), ACT.Sigmoid, d, w.free)
        b2 = act(w.ap[:, 0:META], small.ap[:, 0:META], ACT.Sigmoid, d)
        pr.free, small.free = [a2], [b2]
        t = tt(u.ap[:, HIST - META:], u.ap[:, HIST - META:], w.ap, ALU.mult, a, b, a2, b2)
        w.free = [t]
        c = ts(Cb[:, m, :], u.ap[:, 0:T], V("conv_w", m), V("conv_b", m), ALU.mult, ALU.add, t, s1_done)
        for j in range(1, TAPS):
            c = stt(Cb[:, m, :], u.ap[:, j:j + T], V("conv_w", 8 * j + m), Cb[:, m, :], ALU.mult, ALU.add, c)
        u.free = [c]
        c_ready[m] = c
        pr, d, _ = gemm_fm()
        q = tr.take()
        a = act(q.ap, flat(pr.ap), ACT.Silu, d, q.free)
        pr.free = [a]
        for j in range(2):
            x = aux.take()
            oh = O[:, m, j * 512:(j + 1) * 512]
            d = PE.mark(PE.after(x.free, r8).matmul(x.ap, selB8[:, m, :], R8[:, j * 512:(j + 1) * 512],
                                                    start=True, stop=True))
            t = stt(oh, oh, V("gnorm_g", m), x.ap, ALU.mult, ALU.mult, d, o_ready[m])
            x.free = [t]
            t = tt(oh, oh, q.ap[:, j * 512:(j + 1) * 512], ALU.mult, t, a)
        q.free = [t]
        o_ready[m] = t
        sz_kept[m] = gate_out(tr.take(), SZ, m, ACT.Silu)

    def conv_norm():
        xs = [aux.take(), aux.take()]
        PE.after(xs[0].free, xs[1].free)
        for k in range(8):
            PE.after(c_ready[k])
            for j in range(2):
                ins = nc.tensor.matmul(xs[j].ap, ones, Cb[:, k, j * 512:(j + 1) * 512],
                                       start=(k == 0), stop=(k == 7))
            yield
        d = PE.mark(ins)
        for k in range(8):
            for j in range(2):
                cj = Cb[:, k, j * 512:(j + 1) * 512]
                t = stt(cj, xs[j].ap, -1.0 / 1024, cj, ALU.mult, ALU.add, d, c_ready[k])
            c_ready[k] = t
            yield
        xs[0].free = xs[1].free = [t]
        xs = [aux.take(), aux.take()]
        PE.after(xs[0].free, xs[1].free)
        for k in range(8):
            q = tr.take()
            a = act(q.ap, Cb[:, k, :], ACT.Square, c_ready[k], q.free)
            yield
            PE.after(a)
            for j in range(2):
                ins = nc.tensor.matmul(xs[j].ap, ones, q.ap[:, j * 512:(j + 1) * 512],
                                       start=(k == 0), stop=(k == 7))
            d = PE.mark(ins)
            q.free = [d]
        R = sg[:, 0, 0:T]
        for j in range(2):
            a = act(R[:, j * 512:(j + 1) * 512], xs[j].ap, ACT.Sqrt, d, sgs[0].free, scale=1.0 / 1024, bias=EPS)
            xs[j].free = [a]
        r = recip(R, R, a)
        yield
        for k in range(8):
            q = tr.take()
            ld = load(q.ap, SZ[k], sz_kept[k], q.free)
            t = tt(Cb[:, k, :], Cb[:, k, :], R, ALU.mult, r, c_ready[k])
            a = act(Cb[:, k, :], Cb[:, k, :], ACT.Silu, t, scale=V("ln_g", k), bias=V("ln_b", k))
            t = tt(Cb[:, k, :], Cb[:, k, :], q.ap, ALU.mult, a, ld)
            q.free = [t]
            c_ready[k] = t
            yield

    jobs.append(conv_norm())
    gb = Ring([Slot(av[:, 0, 0:T]), Slot(av[:, 1, 0:T])])
    gb.slots[0].free, gb.slots[1].free = avs[0].free, avs[1].free
    for m in range(8):
        pr, d, _ = gemm_fm(last=(m == 7))
        buf = gb.take()
        a = act(buf.ap, flat(pr.ap), ACT.Sigmoid, d, buf.free)
        pr.free = [a]
        gc_kept[m] = store(GC[m], buf.ap, a)
        buf.free = [gc_kept[m]]
    drain_jobs()

    for k in range(8):
        h_ready[k] = put_h(k, Cb[:, k, :], c_ready[k])
    M = Cb
    m_ready = [None] * 8
    split_c = [list(t) for t in h_ready]
    gl = Ring([Slot(tmp[:, i, :]) for i in range(3)])
    for a_, b_ in zip(gl.slots, tr.slots):
        a_.free = b_.free

    def fetch(dram, m, kept):
        q = gl.take()
        return q, load(q.ap, dram[m], kept, q.free)

    nxt = fetch(GC, 0, gc_kept[0])
    for m in range(8):
        q, ld = nxt
        if m < 7:
            nxt = fetch(GC, m + 1, gc_kept[m + 1])
        pr, d, _ = gemm_fm(last=(m == 7))
        t = tt(M[:, m, :], flat(pr.ap), q.ap, ALU.mult, d, ld, split_c[m])
        pr.free, q.free = [t], [t]
        m_ready[m] = t
    for k in range(8):
        h_ready[k] = put_h(k, O[:, k, :], o_ready[k])
    split_o = [list(t) for t in h_ready]
    nxt = fetch(GR, 0, gr_kept[0])
    for m in range(8):
        q, ld = nxt
        if m < 7:
            nxt = fetch(GR, m + 1, gr_kept[m + 1])
        pr, d, _ = gemm_fm(last=(m == 7))
        t = tt(q.ap, flat(pr.ap), q.ap, ALU.mult, d, ld)
        pr.free = [t]
        t = tt(M[:, m, :], M[:, m, :], q.ap, ALU.add, t, m_ready[m])
        q.free = [t]
        m_ready[m] = t
    for k in range(8):
        h_ready[k] = put_h(k, M[:, k, :], m_ready[k])

    class Stats:

        def __init__(self, ring):
            self.banks = [aux.take(), aux.take()]
            self.ring, self.n, self.wait = ring, 0, None

        def add(self, ap, *tokens):
            q = self.ring.take()
            a = act(q.ap, ap, ACT.Square, q.free, *tokens)
            self.flush()
            self.wait = (q, a)

        def flush(self):
            if self.wait is None:
                return
            q, a = self.wait
            self.wait = None
            if self.n == 0:
                PE.after(self.banks[0].free, self.banks[1].free)
            PE.after(a)
            for j in range(2):
                ins = nc.tensor.matmul(self.banks[j].ap, ones, q.ap[:, j * 512:(j + 1) * 512],
                                       start=(self.n == 0), stop=(self.n == 7))
            self.d = PE.mark(ins)
            q.free = [self.d]
            self.n += 1

        def inverse_root(self, R, eps, *tokens):
            self.flush()
            out = []
            for j in range(2):
                r = R[:, j * 512:(j + 1) * 512]
                a = act(r, self.banks[j].ap, ACT.Sqrt, self.d, *tokens, scale=1.0 / 1024, bias=eps)
                self.banks[j].free = [a]
                out.append(recip(r, r, a))
            return out

    X = O
    x_ready = [None] * 8
    st = Stats(Ring([Slot(sg[:, i, 0:T]) for i in range(2)]))
    for q in st.ring.slots:
        q.free = [sgs[0].free, sgs[1].free, c_ready]

    def fetch_x(m):
        q = gl.take()
        return q, load(q.ap, A["xin"][m][:, META:TM], q.free)

    nxt = fetch_x(0)
    for m in range(8):
        q, ld = nxt
        if m < 7:
            nxt = fetch_x(m + 1)
        pr, d, _ = gemm_fm(last=(m == 7))
        t = tt(X[:, m, :], flat(pr.ap), q.ap, ALU.add, d, ld, split_o[m])
        pr.free, q.free = [t], [t]
        x_ready[m] = t
        st.add(X[:, m, :], t)
    R = av[:, 0, 0:T]
    r = st.inverse_root(R, EPS, gc_kept)
    st = Stats(st.ring)
    for k in range(8):
        x_ready[k] = stt(X[:, k, :], X[:, k, :], V("final_g", k), R, ALU.mult, ALU.mult, r, x_ready[k])
        st.add(X[:, k, :], x_ready[k])
    if stage == 2:
        for k in range(8):
            store(A["dbg"][k], X[:, k, :], x_ready[k])
        SP.after(*stores)
        return

    XS = nc.dram_tensor("keep_x", [KT, P, T], F, kind="Internal").ap()
    R2 = av[:, 1, 0:T]
    r = st.inverse_root(R2, EPS, gc_kept)
    nr = Ring([Slot(sg[:, 0, 0:T]), Slot(sg[:, 1, 0:T])])
    for q, w in zip(nr.slots, st.ring.slots):
        q.free = w.free
    xs_kept = [None] * 8

    def normed(q, k, name, R, r):
        t = stt(q.ap, X[:, k, :], V(name, k), R, ALU.mult, ALU.mult, r, x_ready[k], q.free)
        h_ready[k] = put_h(k, q.ap, t)
        q.free = list(h_ready[k])

    for k in range(8):
        xs_kept[k] = store(XS[k], X[:, k, :], x_ready[k])
        normed(nr.take(), k, "mix_g", R2, r)
    old = [xs_kept, nr.slots[0].free, nr.slots[1].free, x_ready, r]
    s3.close()
    s2.close()

    aux.slots.append(small)
    s4 = ExitStack()
    qa = sb("qa", [P, 2, T], F, s4)
    ka = sb("ka", [P, 2, T], F, s4)
    va = sb("va", [P, 2, T], F, s4)
    oa = sb("oa", [P, 8, 128], F, s4)
    bias = sb("bias", [P, 2, BAND], F, s4)
    pp = sb("pp", [P, 3, BAND], F, s4)
    pt = sb("pt", [P, 2, BAND], F, s4)
    st2 = sb("st2", [P, 4, 8], F, s4)
    ss2 = sb("ss2", [P, 8], F, s4)
    rsum = sb("rsum", [P, 2, 8], F, s4)
    osq = sb("osq", [P, 8, 64], F, s4)
    zb = sb("zb", [P, T + 2], F, s4)
    gt = sb("gt", [P, 2, T], F, s4)
    vg = sb("vg", [P, 8, 256], F, s4)
    sgw = sb("sgw", [P, 4, 128], F, s4)
    sgc = sb("sgc", [P, 3, 256], F, s4)
    bst = sb("bst", [P, 8, 6], F, s4)
    bag = sb("bag", [P, 8, 2], F, s4)
    R8b = qa[0:8, 0, :]
    MX = B0
    t_sgw = load(flat(sgw[:, :, :]), A["sgw"], old)
    t_sgc = load(flat(sgc[:, :, :]), A["sgc"], old)
    t_ws = tt(sgw[:, :, :], sgw[:, :, :], C("tri").rearrange("p (o t) -> p o t", o=1).to_broadcast([P, 4, 128]),
              ALU.mult, t_sgw)
    zz = zero(zb[:, 0:2], 0.0, old)

    bias_r = Ring([Slot(bias[:, i, :]) for i in range(2)])
    pp_r = Ring([Slot(pp[:, i, :]) for i in range(3)])
    pt_r = Ring([Slot(pt[:, i, :]) for i in range(2)])
    for q in bias_r.slots + pp_r.slots + pt_r.slots:
        q.free = [old]
    S = Slot(psum[:, 4:6, :])
    TL, PT, OUT = Slot(psum[:, 5, 0:128]), Slot(psum[:, 6, :]), Slot(psum[:, 7, :])
    S.free = TL.free = [small.free, aux.slots[0].free]
    PT.free, OUT.free = aux.slots[1].free, aux.slots[2].free
    qkv_free = [[old], [old]]
    oa_free = [old]
    mx_ready = [None] * 8

    def attention(j, s, tq, tk, tv):
        nonlocal oa_free
        items = [(hh_, i) for hh_ in range(2) for i in range(8)]
        got = {}
        bt = {}
        tn = qkv_free[s]
        PE.after(S.free, TL.free, tv)
        for c in range(8):
            ins = nc.tensor.transpose(flat(S.ap)[:, c * 128:(c + 1) * 128], va[:, s, c * 128:(c + 1) * 128], ident)
        d = PE.mark(ins)
        tv = act(va[:, s, :], flat(S.ap), ACT.Copy, d)
        S.free = TL.free = [tv]
        yield
        for n in range(len(items) + 3):
            m = n - 3
            if n < len(items):
                hh2, i2 = items[n]
                if i2 == 0:
                    bq = bias_r.take()
                    bt[hh2] = (bq, load(bq.ap, A["bias"][2 * j + hh2], bq.free))
                bq, tb = bt[hh2]
                nk2 = min(BAND, 128 * (i2 + 1))
                k2 = 128 * (i2 + 1) - nk2
                lo = 64 * hh2
                PE.after(S.free, tq, tk)
                sp = flat(S.ap)
                if nk2 > 512:
                    PE.after(TL.free)
                for a0 in range(0, nk2, 512):
                    w_ = min(512, nk2 - a0)
                    ins = nc.tensor.matmul(sp[:, a0:a0 + w_], qa[lo:lo + 64, s, i2 * 128:(i2 + 1) * 128],
                                           ka[lo:lo + 64, s, k2 + a0:k2 + a0 + w_], start=True, stop=True)
                ds = PE.mark(ins)
            if m >= 0:
                p, nk, k0, e, hh_, i, q, ev = got.pop(m)
                out = OUT.ap[:, 64 * i:64 * i + 64]
                PE.after(ev, tv, OUT.free)
                for b_ in range(nk // 128):
                    kt = k0 // 128 + b_
                    ins = nc.tensor.matmul(out, q.ap[:, b_ * 128:(b_ + 1) * 128],
                                           va[:, s, kt * 128 + 64 * hh_:kt * 128 + 64 * hh_ + 64],
                                           start=(b_ == 0), stop=(b_ == nk // 128 - 1))
                dv = PE.mark(ins)
                q.free = [dv]
            if n < len(items):
                p2 = pp_r.take()
                c = n % 4
                mx_, nm2 = (st2[:, c, z:z + 1] for z in range(2))
                rs = rsum[:, hh2, i2:i2 + 1]
                t = VE.mark(VE.after(ds, tb, p2.free).tensor_tensor_reduce(
                    p2.ap[:, 0:nk2], sp[:, 0:nk2], bq.ap[:, BAND - nk2:BAND], 1.0, -3.0e38, ALU.add, ALU.max, mx_))
                S.free = [t]
                if nk2 > 512:
                    TL.free = [t]
                if i2 == 7:
                    bq.free = [t]
                t = ts(nm2, mx_, -1.0, None, ALU.mult, None, t)
                got[n] = [p2, nk2, k2, None, hh2, i2]
            yield
            if 0 <= n - 2 < len(items):
                g = got[n - 2]
                p3, nk3 = g[0], g[1]
                q3_ = pt_r.take()
                ev3 = []
                PE.after(g[3], PT.free)
                if nk3 > 512:
                    d = PE.mark(PE.after(TL.free).transpose(TL.ap, p3.ap[:, 512:640], ident))
                    TL.free = [act(q3_.ap[:, 512:640], TL.ap, ACT.Copy, d, q3_.free)]
                    ev3 += TL.free
                w3 = min(512, nk3)
                for b_ in range(w3 // 128):
                    ins = nc.tensor.transpose(PT.ap[:, b_ * 128:(b_ + 1) * 128], p3.ap[:, b_ * 128:(b_ + 1) * 128],
                                              ident)
                d = PE.mark(ins)
                PT.free = [act(q3_.ap[:, 0:w3], PT.ap[:, 0:w3], ACT.Copy, d, q3_.free)]
                p3.free = [d]
                g += [q3_, ev3 + PT.free]
            if n < len(items):
                got[n][3] = act(p2.ap[:, 0:nk2], p2.ap[:, 0:nk2], ACT.Exp, t, tn, bias=nm2, accum_out=rs)
            if m >= 0 and i == 7:
                oh = oa[:, :, 64 * hh_:64 * hh_ + 64]
                r = recip(rsum[:, hh_, :], rsum[:, hh_, :], e)
                wide = lambda ap: ap.rearrange("p (t o) -> p t o", o=1).to_broadcast([P, 8, 64])
                o = tt(oh, OUT.ap.rearrange("p (t c) -> p t c", t=8), wide(rsum[:, hh_, :]), ALU.mult, dv, r, oa_free)
                OUT.free = [o]
                t = tt(osq[:, :, :], oh, oh, ALU.mult, o)
                t = VE.mark(VE.after(t).tensor_reduce(ss2[:, :], osq[:, :, :], AX, ALU.add))
                a = act(ss2[:, :], ss2[:, :], ACT.Sqrt, t, scale=1.0 / 64, bias=EPS)
                t = recip(ss2[:, :], ss2[:, :], a)
                tn = tt(oh, oh, wide(ss2[:, :]), ALU.mult, t)
            if n in (6, 12):
                yield
        d = dv
        qkv_free[s] = [d]
        yield
        PE.after(S.free, TL.free, tn)
        sp = flat(S.ap)
        for i in range(8):
            ins = nc.tensor.transpose(sp[:, i * 128:(i + 1) * 128], oa[:, i, :], ident)
        d = PE.mark(ins)
        oa_free = [d]
        t = act(MX[:, j, :], sp, ACT.Copy, d, xs_kept[j], scale=V("gg2", j))
        S.free = TL.free = [t]
        mx_ready[j] = t

    prev = None
    for j in range(4):
        s = j % 2
        pr, d, _ = gemm_fm()
        tq = act(qa[:, s, :], flat(pr.ap), ACT.Copy, d, qkv_free[s], scale=0.125)
        pr.free = [tq]
        pr, d, _ = gemm_fm()
        tk = act(ka[:, s, :], flat(pr.ap), ACT.Copy, d, qkv_free[s])
        pr.free = [tk]
        pr, d, _ = gemm_fm()
        tv = act(va[:, s, :], flat(pr.ap), ACT.Copy, d, qkv_free[s])
        pr.free = [tv]
        if prev is not None:
            finish(prev)
        prev = attention(j, s, tq, tk, tv)
        jobs.append(prev)

    gr_ = Ring([Slot(gt[:, i, :]) for i in range(2)])
    for q in gr_.slots:
        q.free = [old]
    zfree = [zz]
    for m in range(2):
        pr, d, _ = gemm_fm()
        a = act(zb[:, 2:], flat(pr.ap), ACT.Copy, d, zfree)
        pr.free = [a]
        pr, d, _ = gemm_fm()
        z = tt(zb[:, 2:], zb[:, 2:], flat(pr.ap), ALU.mult, d, a)
        pr.free = [z]
        pr, d, _ = gemm_fm()
        q = gr_.take()
        b = act(q.ap, flat(pr.ap), ACT.Copy, d, q.free)
        pr.free = [b]
        y = MX[:, 4 + m, :]
        c = ts(y, zb[:, 0:T], V("cw2", m), None, ALU.mult, None, z, xs_kept[4 + m])
        for w_ in (1, 2):
            c = stt(y, zb[:, w_:w_ + T], V("cw2", 2 * w_ + m), y, ALU.mult, ALU.add, c)
        zfree = [c]
        c = tt(y, y, q.ap, ALU.mult, c, b)
        q.free = [c]
        mx_ready[4 + m] = c
    for m in range(2):
        pr, d, _ = gemm_fm()
        a = act(MX[:, 6 + m, :], flat(pr.ap), ACT.Gelu, d, xs_kept[6 + m])
        pr.free = [a]
        mx_ready[6 + m] = a
    for m in range(2):
        pr, d, _ = gemm_fm(last=(m == 1))
        v_ = vg[:, :, 128 * m:128 * (m + 1)]
        a = act(v_, flat(pr.ap).rearrange("p (t c) -> p t c", t=8), ACT.Gelu, d, old)
        PE.after(a)
        for c in range(8):
            ins = nc.tensor.transpose(flat(pr.ap)[:, c * 128:(c + 1) * 128], v_[:, c, :], ident)
        d = PE.mark(ins)
        a = act(v_, flat(pr.ap).rearrange("p (t c) -> p t c", t=8), ACT.Copy, d)
        pr.free = [a]
    for i in range(8):
        t = VE.mark(VE.after(a, old).bn_stats(bst[:, i, :], vg[:, i, :]))
    for i in range(8):
        t2 = VE.mark(VE.after(t).bn_aggr(bag[:, i, :], bst[:, i, :]))
    b = act(bag[:, :, 1:2], bag[:, :, 1:2], ACT.Sqrt, t2, scale=1.0, bias=EPS)
    r = recip(bag[:, :, 1:2], bag[:, :, 1:2], b)
    for i in range(8):
        t = ts(vg[:, i, :], vg[:, i, :], bag[:, i, 0:1], bag[:, i, 1:2], ALU.subtract, ALU.mult, r)
    t = tt(vg[:, :, :], vg[:, :, :], sgc[:, 0:1, :].to_broadcast([P, 8, 256]), ALU.mult, t, t_sgc)
    tvg = tt(vg[:, :, :], vg[:, :, :], sgc[:, 1:2, :].to_broadcast([P, 8, 256]), ALU.add, t)
    finish(prev)
    aux2 = Ring([Slot(psum[:, i, :]) for i in range(4, 8)])
    for n, q in enumerate(aux2.slots):
        q.free = [S.free, TL.free, PT.free, OUT.free]
    for m in range(2):
        for g in range(2):
            x = aux2.take()
            PE.after(x.free, tvg, t_ws)
            for b_ in range(4):
                for w_ in range(2):
                    ins = nc.tensor.matmul(x.ap[64 * w_:64 * w_ + 64, b_ * 128:(b_ + 1) * 128],
                                           vg[:, 4 * g + b_, (2 * m + w_) * 64:(2 * m + w_ + 1) * 64],
                                           sgw[:, 2 * m + w_, :], start=True, stop=True)
            d = PE.mark(ins)
            q = gr_.take()
            u = q.ap[:, 0:512].rearrange("p (b t) -> p b t", b=4)
            t = tt(u, x.ap.rearrange("p (b t) -> p b t", b=4),
                   sgc[:, 2:3, m * 128:(m + 1) * 128].to_broadcast([P, 4, 128]), ALU.add, d, q.free, t_sgc)
            x.free = [t]
            y = MX[:, 6 + m, g * 512:(g + 1) * 512]
            t = tt(y, y, q.ap[:, 0:512], ALU.mult, t, mx_ready[6 + m])
            q.free = [t]
        mx_ready[6 + m] = t
    pr, d = sums([(MX[:, 4 + k, :], [mx_ready[4 + k]]) for k in range(4)], gr_, T,
                 lhs=lambda k: selA4[:, k, :], rows=8)
    a = act(R8b[:, :], flat(pr.ap[0:8, :, :]), ACT.Sqrt, d, qkv_free, scale=1.0 / 64, bias=EPS)
    pr.free = [a]
    r = recip(R8b[:, :], R8b[:, :], a)
    for k in range(4):
        for g in range(2):
            x = aux2.take()
            d = PE.mark(PE.after(x.free, r).matmul(x.ap, selB4[:, k, :], R8b[:, g * 512:(g + 1) * 512],
                                                   start=True, stop=True))
            y = MX[:, 4 + k, g * 512:(g + 1) * 512]
            t = stt(y, y, V("gg2", 4 + k), x.ap, ALU.mult, ALU.mult, d, mx_ready[4 + k])
            x.free = [t]
        mx_ready[4 + k] = t
    for k in range(8):
        h_ready[k] = put_h(k, MX[:, k, :], mx_ready[k])
    split_m = [list(t) for t in h_ready]
    mix_done = [tvg, d, t, mx_ready, split_m, qkv_free, oa_free]
    s4.close()
    aux = aux2

    s5 = ExitStack()
    hdh = sb("hdh", [P, 4, T], FR, s5)
    hdl = sb("hdl", [P, 4, T], FR, s5)
    t5 = sb("t5", [P, 6, T], F, s5)
    R5 = sb("R5", [P, T], F, s5)[:, :]
    mean5 = sb("mean5", [P, T], F, s5)[:, :]
    sqr = Ring([Slot(t5[:, i, :]) for i in range(3)])
    tr = Ring([Slot(t5[:, 3 + i, :]) for i in range(3)])
    for q in sqr.slots + tr.slots:
        q.free = [mix_done]
    hd_free4 = [[mix_done] for _ in range(4)]
    hd_ready = [None] * 4


    def fetch_xs(m):
        q = tr.take()
        return q, load(q.ap, XS[m], q.free)

    st = Stats(sqr)
    nxt = fetch_xs(0)
    for m in range(8):
        q, ld = nxt
        if m < 7:
            nxt = fetch_xs(m + 1)
        pr, d, _ = gemm_fm(last=(m == 7))
        t = tt(X[:, m, :], flat(pr.ap), q.ap, ALU.add, d, ld, split_m[m])
        pr.free, q.free = [t], [t]
        x_ready[m] = t
        st.add(X[:, m, :], t)
    r = st.inverse_root(R5, EPS, mix_done)
    for k in range(8):
        normed(tr.take(), k, "mlp_g2", R5, r)

    def mlp(after_last):
        for g in range(8):
            for k in range(4):
                pr, d, _ = gemm_fm(last=(g == 7 and k == 3))
                q = tr.take()
                a = act(q.ap, flat(pr.ap), ACT.Relu, d, q.free)
                pr.free = [a]
                t = tt(q.ap, q.ap, q.ap, ALU.mult, a)
                a = act(hdh[:, k, :], q.ap, ACT.Copy, t, hd_free4[k])
                b = tt(hdl[:, k, :], q.ap, fp(hdh[:, k, :]), ALU.subtract, a)
                q.free = [b]
                hd_ready[k] = [a, b]
            for m2 in range(4):
                i = next_slab()
                for w_ in range(2):
                    m = 2 * m2 + w_
                    pr, d, _ = gemm_fm(src=(hdh, hdl), ready=hd_ready, nk=4, slab=i, base=4 * w_)
                    x_ready[m] = tt(X[:, m, :], X[:, m, :], flat(pr.ap), ALU.add, d, x_ready[m], *h_ready)
                    pr.free = [x_ready[m]]
                    if g == 7:
                        after_last(m)
                w_free[i % 2] = [d]
            for k in range(4):
                hd_free4[k] = [d]

    st = Stats(sqr)
    mlp(lambda m: st.add(X[:, m, :], x_ready[m]))
    r = st.inverse_root(R5, EPS, *h_ready)
    for k in range(8):
        x_ready[k] = stt(X[:, k, :], X[:, k, :], V("fin_g2", k), R5, ALU.mult, ALU.mult, r, x_ready[k])
        if stage > 3:
            h_ready[k] = put_h(k, X[:, k, :], x_ready[k])
            xs_kept[k] = store(XS[k], X[:, k, :], x_ready[k], xs_kept[k])
    if stage == 3:
        for k in range(8):
            store(A["dbg"][k], X[:, k, :], x_ready[k])
        SP.after(*stores)
        return
    split3 = [list(t) for t in h_ready]
    b2_done = [x_ready, split3, hd_free4, r, [q.free for q in tr.slots + sqr.slots]]
    s5.close()

    s6 = ExitStack()
    pre = sb("pre", [P, 2, T + 3], F, s6)
    q3 = sb("q3", [P, 2, T], F, s6)
    k3 = sb("k3", [P, 2, T], F, s6)
    v3 = sb("v3", [P, 2, 8, 129], F, s6)
    o3 = sb("o3", [P, 2, T], F, s6)
    row = sb("row", [4, 2, T], F, s6)
    mp = sb("mp", [4, 8], F, s6)
    uT = sb("uT", [P, 8, 4], F, s6)
    eT = sb("eT", [P, 8, 4], F, s6)
    Pm = sb("Pm", [P, T], F, s6)
    kd3 = sb("kd3", [P, T], F, s6)
    C3 = sb("C3", [P, 8, 129], F, s6)
    h3 = sb("h3", [P, T], F, s6)
    den = sb("den", [P, 2, 8], F, s6)
    bs3 = sb("bs3", [P, 8, 6], F, s6)
    ba3 = sb("ba3", [P, 8, 2], F, s6)
    pb = sb("pb", [P, 2, T], F, s6)
    wp = sb("wp", [P, 4, 128], F, s6)
    shf = kd3[0:4, :]
    Y = B0
    t_wp = load(flat(wp[:, :, :]), A["w_pool"], b2_done)
    z1 = zero(pre[:, :, 0:3], 0.0, b2_done)
    z2 = zero(v3[:, :, :, 128:129], 1.0, b2_done)
    z3 = zero(shf, 0.0, b2_done)
    z4 = zero(C3[:, 0, :], 0.0, b2_done)

    i_, f_, a_, u_, w_ = row[:, 0, :], row[:, 1, :], pb[0:4, 0, :], pb[0:4, 1, :], h3[0:4, :]
    pr, d, _ = gemm_fm()
    g1 = act(i_, flat(pr.ap[0:4, :, :]), ACT.Copy, d, b2_done)
    g2 = act(f_, flat(pr.ap[32:36, :, :]), ACT.Copy, d, b2_done)
    pr.free = [g1, g2]
    t = ts(i_, i_, V("b_i")[0:4, :], None, ALU.add, None, g1)
    ti = t
    t = ts(f_, f_, V("b_f")[0:4, :], None, ALU.add, None, g2)
    a = act(a_, f_, ACT.Abs, t)
    a = act(a_, a_, ACT.Exp, a, scale=-1.0)
    a = act(a_, a_, ACT.Ln, a, bias=1.0)
    t = ts(f_, f_, 0.0, None, ALU.min, None, t, a)
    t = tt(f_, f_, a_, ALU.subtract, t)
    t1 = zero(w_, 1.0, b2_done)
    t1 = zero(w_.rearrange("p (c t) -> p c t", c=8)[:, :, 0:1], 0.0, t1)
    ta = VE.mark(VE.after(t, t1).tensor_tensor_scan(a_, w_, f_, 0.0, ALU.mult, ALU.add))
    t = tt(u_, i_, a_, ALU.subtract, ta, ti)
    a8 = a_.rearrange("p (c t) -> p c t", c=8)
    s8 = shf.rearrange("p (c t) -> p c t", c=8)
    t2 = copy(s8[:, 1:8, 0:1], a8[:, 0:7, 127:128], ta, z3)
    tm = VE.mark(VE.after(t, t2).tensor_tensor_scan(i_, shf, u_, 0.0, ALU.add, ALU.max))
    i8 = i_.rearrange("p (c t) -> p c t", c=8)
    t = zero(mp[:, 0:1], 0.0, b2_done)
    t = tt(mp[:, 1:8].rearrange("p (c o) -> p c o", o=1), i8[:, 0:7, 127:128], a8[:, 0:7, 127:128], ALU.add, tm, t)
    t = tt(f_.rearrange("p (c t) -> p c t", c=8), mp[:, :].rearrange("p (c o) -> p c o", o=1).to_broadcast([4, 8, 128]),
           i8, ALU.subtract, t)
    t_si = act(f_, f_, ACT.Exp, t)
    t = tt(w_, a_, i_, ALU.add, tm)
    t = ts(w_, w_, -1.0, 87.0, ALU.mult, ALU.min, t)
    t_em = act(w_, w_, ACT.Exp, t)
    t_nm = ts(i_, i_, -1.0, None, ALU.mult, None, t)
    x = aux.take()
    PE.after(x.free, t_em)
    for c in range(8):
        nc.tensor.transpose(x.ap[:, 4 * c:4 * c + 4], u_[:, c * 128:(c + 1) * 128], ident[0:4, 0:4])
        ins = nc.tensor.transpose(x.ap[:, 64 + 4 * c:68 + 4 * c], w_[:, c * 128:(c + 1) * 128], ident[0:4, 0:4])
    d = PE.mark(ins)
    t_uT = copy(flat(uT[:, :, :]), x.ap[:, 0:32], d, b2_done)
    t_eT = copy(flat(eT[:, :, :]), x.ap[:, 64:96], d, b2_done)
    x.free = [t_eT]
    selB4r = selB8[0:4, :, :]

    p_free = [[z1], [z1]]
    hd3_free = [[b2_done], [b2_done]]
    Pm_free, kd_free, C_free, h3_free, den_free = [b2_done], [tm], [z4], [t_eT], [b2_done]
    y_ready = [None] * 8

    def conv4(src, dst, m, free, dfree, scale=None):
        c = ts(dst, src[:, 0:T], V("cw3", m), None, ALU.mult, None, *free, *dfree)
        for w in range(1, 4):
            c = stt(dst, src[:, w:w + T], V("cw3", 8 * w + m), dst, ALU.mult, ALU.add, c)
        a = act(dst, dst, ACT.Silu, c)
        return c, a

    def mlstm(h, s, tq, tk, tv, to):
        nonlocal Pm_free, kd_free, C_free, h3_free
        q, k, v, o = q3[:, s, :], k3[:, s, :], v3[:, s, :, :], o3[:, s, :]
        tv = [tv, turn(v[:, :, 0:128], 0, tv), turn(v[:, :, 0:128], 1, tv)]
        yield
        for g in range(2):
            x = aux.take()
            d = PE.mark(PE.after(x.free, t_nm).matmul(x.ap, selB4r[:, h, :], i_[:, g * 512:(g + 1) * 512],
                                                      start=True, stop=True))
            for c in range(4 * g, 4 * g + 4):
                t = stt(Pm[:, c * 128:(c + 1) * 128], x.ap[:, (c % 4) * 128:(c % 4 + 1) * 128], uT[:, c, h:h + 1],
                        C("tril_neg"), ALU.add, ALU.add, d, t_uT, Pm_free)
            x.free = [t]
            yield
        tp = act(Pm[:, :], Pm[:, :], ACT.Exp, t)
        yield
        for g in range(2):
            x = aux.take()
            PE.after(x.free, tk)
            for c in range(4):
                ins = nc.tensor.transpose(x.ap[:, c * 128:(c + 1) * 128],
                                          k[:, (4 * g + c) * 128:(4 * g + c + 1) * 128], ident)
            d = PE.mark(ins)
            for c in range(4):
                cc = 4 * g + c
                tkd = ts(kd3[:, cc * 128:(cc + 1) * 128], x.ap[:, c * 128:(c + 1) * 128],
                         Pm[:, cc * 128 + 127:cc * 128 + 128], None, ALU.mult, None, d, tp, kd_free)
            x.free = [tkd]
            yield
        for g in range(2):
            x = aux.take()
            PE.after(x.free, tk, tq)
            for c in range(4):
                cc = slice((4 * g + c) * 128, (4 * g + c + 1) * 128)
                ins = nc.tensor.matmul(x.ap[:, c * 128:(c + 1) * 128], k[:, cc], q[:, cc], start=True, stop=True)
            d = PE.mark(ins)
            tw = tt(Pm[:, g * 512:(g + 1) * 512], x.ap, Pm[:, g * 512:(g + 1) * 512], ALU.mult, d, tkd)
            x.free = [tw]
            yield
        for g in range(2):
            x = aux.take()
            d = PE.mark(PE.after(x.free, t_si).matmul(x.ap, selB4r[:, h, :], f_[:, g * 512:(g + 1) * 512],
                                                      start=True, stop=True))
            t = tt(q[:, g * 512:(g + 1) * 512], q[:, g * 512:(g + 1) * 512], x.ap, ALU.mult, d, tw)
            tqs = t
            t2_ = copy(den[:, 0, 4 * g:4 * g + 4].rearrange("p (c o) -> p c o", o=1),
                       x.ap.rearrange("p (c t) -> p c t", c=4)[:, :, 127:128], d, den_free)
            x.free = [t2_]
            yield
        ts_ = t2_
        tc = z4
        for c in range(7):
            x = aux.take()
            d = PE.mark(PE.after(x.free, tkd, tv).matmul(x.ap[:, 0:129], kd3[:, c * 128:(c + 1) * 128], v[:, c, :],
                                                         start=True, stop=True))
            tc = stt(C3[:, c + 1, :], C3[:, c, :], den[:, 0, c:c + 1], x.ap[:, 0:129], ALU.mult, ALU.add,
                     tc, d, ts_, C_free)
            x.free = [tc]
            if c % 2:
                yield
        kd_free = [d]
        for c in range(8):
            x = aux.take()
            cc = slice(c * 128, (c + 1) * 128)
            PE.after(x.free, tw, tqs, tc, tv)
            nc.tensor.matmul(x.ap[:, 0:129], Pm[:, cc], v[:, c, :], start=True, stop=False)
            d = PE.mark(nc.tensor.matmul(x.ap[:, 0:129], q[:, cc], C3[:, c, :], start=False, stop=True))
            dn = den[:, 1, c:c + 1]
            t = ts(dn, x.ap[:, 128:129], -1.0, None, ALU.mult, None, d)
            t = tt(dn, x.ap[:, 128:129], dn, ALU.max, t)
            t = tt(dn, dn, eT[:, c, h:h + 1], ALU.max, t, t_eT)
            t = recip(dn, dn, t)
            t = ts(h3[:, cc], x.ap[:, 0:128], dn, None, ALU.mult, None, t, h3_free)
            x.free = [t]
            t = VE.mark(VE.after(t).bn_stats(bs3[:, c, :], h3[:, cc]))
            if c % 2:
                yield
        Pm_free, C_free = [d], [d]
        for c in range(8):
            t2 = VE.mark(VE.after(t).bn_aggr(ba3[:, c, :], bs3[:, c, :]))
        a = act(ba3[:, :, 1:2], ba3[:, :, 1:2], ACT.Sqrt, t2, scale=1.0, bias=LN_EPS)
        r = recip(ba3[:, :, 1:2], ba3[:, :, 1:2], a)
        for c in range(8):
            cc = slice(c * 128, (c + 1) * 128)
            t = ts(h3[:, cc], h3[:, cc], ba3[:, c, 0:1], ba3[:, c, 1:2], ALU.subtract, ALU.mult, r)
        yield
        yield
        for g in range(2):
            x = aux.take()
            PE.after(x.free, t)
            for c in range(4):
                ins = nc.tensor.transpose(x.ap[:, c * 128:(c + 1) * 128],
                                          h3[:, (4 * g + c) * 128:(4 * g + c + 1) * 128], ident)
            d = PE.mark(ins)
            ty = stt(Y[:, h, g * 512:(g + 1) * 512], x.ap, V("hn_g", h), o[:, g * 512:(g + 1) * 512],
                     ALU.mult, ALU.mult, d, to, xs_kept[h], split3[h])
            x.free = [ty]
            yield
        h3_free = [d]
        hd3_free[s] = [d, ty, tqs, tc]
        y_ready[h] = ty

    prev = None
    pn = 0
    for h in range(4):
        s = h % 2
        out = []
        for m, dst in ((h, q3[:, s, :]), (4 + h, k3[:, s, :])):
            pz = pre[:, pn % 2, :]
            pr, d, _ = gemm_fm()
            a = act(pz[:, 3:], flat(pr.ap), ACT.Copy, d, p_free[pn % 2])
            pr.free = [a]
            c, a = conv4(pz, dst, m, [a, z1], hd3_free[s])
            p_free[pn % 2] = [c]
            pn += 1
            out.append(a)
        tq = out[0]
        tk = ts(k3[:, s, :], k3[:, s, :], 128.0 ** -0.5, None, ALU.mult, None, out[1])
        pr, d, _ = gemm_fm()
        tv = act(v3[:, s, :, 0:128], flat(pr.ap).rearrange("p (t c) -> p t c", t=8), ACT.Copy, d, hd3_free[s], z2)
        pr.free = [tv]
        pr, d, _ = gemm_fm()
        to = act(o3[:, s, :], flat(pr.ap), ACT.Sigmoid, d, hd3_free[s])
        pr.free = [to]
        if prev is not None:
            finish(prev)
        prev = mlstm(h, s, tq, tk, tv, to)
        jobs.append(prev)

    pbs = [Slot(pb[:, 0, :]), Slot(pb[:, 1, :])]
    for q in pbs:
        q.free = [t_uT, t_eT]
    for g in range(4):
        pr, d, _ = gemm_fm(last=(g == 3))
        y = Y[:, 4 + g, :]
        t0 = act(y, flat(pr.ap), ACT.Copy, d, xs_kept[4 + g], split3[4 + g])
        pr.free = [t0]
        src, ts0 = y, [t0]
        for w in range(g + 1):
            n = 2 ** w
            q = pbs[w % 2]
            t1 = copy(q.ap[:, 0:n], src[:, 0:n], ts0, q.free)
            t2 = tt(q.ap[:, n:], src[:, n:], src[:, 0:T - n], ALU.add, ts0, q.free)
            ts0 = [t1, t2]
            if w:
                pbs[(w - 1) % 2].free = [t1, t2]
            src = q.ap
        win = 2 ** (g + 1)
        t3 = tt(src[:, 0:win], src[:, 0:win], C("inv")[:, 0:win], ALU.mult, ts0)
        t4 = stt(y[:, 0:win], y[:, 0:win], -1.0, src[:, 0:win], ALU.mult, ALU.add, t3)
        t5_ = stt(y[:, win:], src[:, win:], 1.0 / win, y[:, win:], ALU.mult, ALU.subtract, ts0)
        q.free = [t4, t5_]
        for j in range(2):
            pass
        y_ready[4 + g] = [t4, t5_]
    finish(prev)
    for g in range(4):
        for j in range(2):
            x = aux.take()
            yj = Y[:, 4 + g, j * 512:(j + 1) * 512]
            d = PE.mark(PE.after(x.free, y_ready[4 + g], t_wp).matmul(x.ap, wp[:, g, :], yj, start=True, stop=True))
            t = act(yj, x.ap, ACT.Copy, d, scale=V("pscale", g))
            x.free = [t]
        y_ready[4 + g] = t
    for k in range(8):
        h_ready[k] = put_h(k, Y[:, k, :], y_ready[k])
    split_y = [list(t) for t in h_ready]
    mix_done = [y_ready, split_y, hd3_free, Pm_free, kd_free, h3_free, p_free, t_uT, t_eT, t_si,
                [q.free for q in pbs], [q.free for q in aux.slots]]
    s6.close()

    s7 = ExitStack()
    hdh = sb("hdh3", [P, 4, T], FR, s7)
    hdl = sb("hdl3", [P, 4, T], FR, s7)
    t7 = sb("t7", [P, 6, T], F, s7)
    R7 = sb("R7", [P, T], F, s7)[:, :]
    sqr = Ring([Slot(t7[:, i, :]) for i in range(3)])
    tr = Ring([Slot(t7[:, 3 + i, :]) for i in range(3)])
    for q in sqr.slots + tr.slots:
        q.free = [mix_done]
    hd_free4 = [[mix_done] for _ in range(4)]

    class Sums:

        def __init__(self):
            self.banks = [aux.take(), aux.take()]
            self.n = 0

        def add(self, ap, *tokens):
            if self.n == 0:
                PE.after(self.banks[0].free, self.banks[1].free)
            PE.after(*tokens)
            for j in range(2):
                ins = nc.tensor.matmul(self.banks[j].ap, ones, ap[:, j * 512:(j + 1) * 512],
                                       start=(self.n == 0), stop=(self.n == 7))
            self.n += 1
            self.d = PE.mark(ins)

    def layer_norm(sums_, g, b, use):
        st = Stats(sqr)
        for k in range(8):
            for j in range(2):
                xj = X[:, k, j * 512:(j + 1) * 512]
                t = stt(xj, sums_.banks[j].ap, -1.0 / 1024, xj, ALU.mult, ALU.add, sums_.d, x_ready[k])
            x_ready[k] = t
            st.add(X[:, k, :], t)
        for q in sums_.banks:
            q.free = [t]
        r = st.inverse_root(R7, LN_EPS, mix_done)
        for k in range(8):
            t = stt(X[:, k, :], X[:, k, :], V(g, k), R7, ALU.mult, ALU.mult, r, x_ready[k])
            x_ready[k] = act(X[:, k, :], X[:, k, :], ACT.Identity, t, bias=V(b, k))
            use(k)

    sm = Sums()
    late = None
    nxt = fetch_xs(0)
    for m in range(8):
        q, ld = nxt
        if m < 7:
            nxt = fetch_xs(m + 1)
        pr, d, _ = gemm_fm(last=(m == 7))
        x_ready[m] = stt(X[:, m, :], q.ap, ALPHA, flat(pr.ap), ALU.mult, ALU.add, d, ld, split_y[m])
        pr.free, q.free = [x_ready[m]], [x_ready[m]]
        if late is not None:
            sm.add(X[:, late, :], x_ready[late])
        late = m
    sm.add(X[:, 7, :], x_ready[7])

    def split_x(k):
        h_ready[k] = put_h(k, X[:, k, :], x_ready[k])
        x_ready[k] = ts(X[:, k, :], X[:, k, :], ALPHA, None, ALU.mult, None, h_ready[k])

    layer_norm(sm, "ln1_g", "ln1_b", split_x)
    sm2 = Sums()
    pend = []

    def summed(m):
        pend.append(m)
        if len(pend) > 1:
            k = pend.pop(0)
            sm2.add(X[:, k, :], x_ready[k])

    mlp(summed)
    sm2.add(X[:, 7, :], x_ready[7])
    layer_norm(sm2, "ln2_g", "ln2_b", lambda k: store(A["out"][k], X[:, k, :], x_ready[k]))
    SP.after(*stores)


def slabs(I):
    def cut(w, cols):
        return [w[:, c:c + 128].reshape(8, 128, 128).transpose(1, 0, 2).reshape(128, 1024) for c in cols]

    def mlp(up, down):
        out = []
        for g in range(8):
            out += cut(up, [512 * g + 128 * k for k in range(4)])
            d = down[512 * g:512 * (g + 1)].reshape(4, 128, 4, 2, 128).transpose(2, 1, 3, 0, 4)
            out += [d[m].reshape(128, 1024) for m in range(4)]
        return out

    out = []
    w = I["w_in"][0]
    for h in range(8):
        out += cut(w, [4096 + 128 * h, 3072 + 128 * h, 5120 + 128 * h])
    out += cut(w, [8192 + 128 * m for m in range(8)])
    for m in range(8):
        out += cut(w, [128 * m, 1024 + 128 * m, 6144 + 128 * m, 2048 + 128 * m])
    out += cut(w, [7168 + 128 * m for m in range(8)])
    for name in ("w_conv_out", "w_rec_out", "w_out"):
        out += cut(I[name][0], [128 * m for m in range(8)])
    w = I["w_in_2"][0]
    for j in range(4):
        out += cut(w, [128 * j, 512 + 128 * j, 1024 + 128 * j])
    for m in range(2):
        out += cut(w, [1792 + 128 * m, 2048 + 128 * m, 1536 + 128 * m])
    out += cut(w, [2304, 2432, 2560, 2688])
    out += cut(I["w_out_2"][0], [128 * m for m in range(8)])
    out += mlp(I["w_up_2"][0], I["w_down_2"][0])
    w = I["w_in_3"][0]
    g = np.zeros((1024, 128), np.float32)
    g[:, 0:4] = w[:, 1536:1540]
    g[:, 32:36] = w[:, 1540:1544]
    out += cut(g, [0])
    for h in range(4):
        out += cut(w, [128 * h, 512 + 128 * h, 1024 + 128 * h, 1544 + 128 * h])
    out += cut(w, [2056 + 128 * g for g in range(4)])
    out += cut(I["w_out_3"][0], [128 * m for m in range(8)])
    out += mlp(I["w_ff1_3"][0], I["w_ff2_3"][0])
    return out


def consts():
    cst = np.zeros((128, NCONST), np.float32)

    def put(name, a):
        c0, w = CONSTS[name]
        cst[:a.shape[0], c0:c0 + w] = a.reshape(a.shape[0], -1)

    put("ident", np.eye(128, dtype=np.float32))
    put("ones", np.ones((128, 128), np.float32))
    a = np.zeros((128, 8, 8), np.float32)
    b = np.zeros((8, 8, 128), np.float32)
    for h in range(8):
        a[:, h, h] = 1
        b[h, h, :] = 1
    put("selA8", a)
    put("selB8", b)
    a = np.zeros((128, 4, 8), np.float32)
    b = np.zeros((8, 4, 128), np.float32)
    for t in range(4):
        a[:64, t, 2 * t] = 1
        a[64:, t, 2 * t + 1] = 1
        b[2 * t, t, :64] = 1
        b[2 * t + 1, t, 64:] = 1
    put("selA4", a)
    put("selB4", b)
    s, t = np.arange(128)[:, None], np.arange(128)[None, :]
    put("inv", np.broadcast_to((1.0 / np.arange(1, 17)).astype(np.float32), (128, 16)))
    put("tri", (s <= t).astype(np.float32))
    put("tril_neg", np.where(s <= t, 0, NEG).astype(np.float32))
    masks = np.stack([((s // (2 * h) == t // (2 * h)) & (s % (2 * h) < h) & (t % (2 * h) >= h))
                      for h in HALVES], 1).astype(np.float32)
    return cst, np.ascontiguousarray(masks.reshape(128, -1))


def vectors(I):
    v = np.zeros((128, NVEC), np.float32)

    def put(name, a):
        c0, w = VECS[name]
        v[:, c0:c0 + w] = a.reshape(w, 128).T

    put("norm_g", I["norm_g"])
    put("conv_w", I["conv_w"])
    put("conv_b", I["conv_b"])
    put("ln_g", I["ln_g"])
    put("ln_b", I["ln_b"])
    put("lb0", I["lb_logits"][0])
    put("lb1", I["lb_logits"][1])
    put("gnorm_g", I["gnorm_g"])
    put("final_g", I["final_g"])
    put("mix_g", I["mix_norm_g_2"])
    put("cw2", I["conv_w_2"])
    put("gg2", I["group_norm_g_2"])
    put("mlp_g2", I["mlp_norm_g_2"])
    put("fin_g2", I["final_norm_g_2"])
    put("cw3", I["w_conv_3"])
    put("hn_g", I["hn_g_3"])
    put("pscale", I["pool_scale_3"])
    put("ln1_g", I["ln1_g_3"])
    put("ln1_b", I["ln1_b_3"])
    put("ln2_g", I["ln2_g_3"])
    put("ln2_b", I["ln2_b_3"])
    v[0:4, VECS["b_i"][0]] = I["b_gate_3"][0, 0:4]
    v[0:4, VECS["b_f"][0]] = I["b_gate_3"][0, 4:8]
    return v


def layout(I):
    x = np.concatenate([I["meta_tokens"], I["x"][0]], 0)
    cst, masks = consts()
    rel = np.clip(np.arange(128)[:, None] + 512 - np.arange(BAND)[None, :], -128, 128) + 128
    bias = I["rel_bias_2"][0][:, rel]
    bias[:, 0:64, BAND - 64:] = NEG
    bias[:, 64:, 0:64] = NEG
    sgc = np.empty((128, 3, 256), np.float32)
    sgc[:, 0, :] = I["sg_ln_g_2"][0]
    sgc[:, 1, :] = I["sg_ln_b_2"][0]
    sgc[:, 2, :] = np.repeat(I["sg_b_2"][0].reshape(2, 2, 128).transpose(1, 0, 2), 64, 0).reshape(128, 256)
    return {
        "w_pool": np.ascontiguousarray(I["w_pool_3"][0].transpose(1, 0, 2).reshape(128, 512)),
        "bias": bias,
        "sgw": np.ascontiguousarray(I["sg_w_2"][0].transpose(2, 0, 1).reshape(128, 512)),
        "sgc": sgc.reshape(128, 768),
        "xin": np.ascontiguousarray(x.T.reshape(8, 128, TM)),
        "wts": np.stack(slabs(I)),
        "vec": vectors(I),
        "cst": cst,
        "masks": masks,
    }


_INS = ("xin", "wts", "vec", "cst", "masks", "bias", "sgw", "sgc", "w_pool")


def kernel(**inputs):
    import concourse.bacc as bacc
    from concourse.bass_utils import run_bass_kernel_spmd

    laid = layout({k: np.asarray(v) for k, v in inputs.items()})
    nc = bacc.Bacc("TRN2", target_bir_lowering=False, num_devices=1)
    arrays, A = {}, {}
    for name in _INS:
        a = np.ascontiguousarray(laid[name])
        arrays["in_" + name] = a
        A[name] = nc.dram_tensor("in_" + name, a.shape, F, kind="ExternalInput").ap()
    A["out"] = nc.dram_tensor("out_y", [KT, P, T], F, kind="ExternalOutput").ap()
    program(nc, A)
    r = run_bass_kernel_spmd(nc, [arrays], core_ids=[0])
    y = np.asarray(r.results[0]["out_y"])
    return np.ascontiguousarray(y.reshape(D_MODEL, T).T)[None]
```

```python
from contextlib import ExitStack

import numpy as np

import concourse.bass as bass
from concourse import mybir

F = mybir.dt.float32
FR = mybir.dt.float32r
I32 = mybir.dt.int32
ACT = mybir.ActivationFunctionType
ALU = mybir.AluOpType
AX = mybir.AxisListType.X

P = 128
D_MODEL = 1024
T = 1024
KT = 8
META = 16
TM = T + META
TAPS = 31
HIST = TAPS - 1
EPS = 1e-6
LN_EPS = 1e-5
HALVES = (64, 32, 16, 8, 4, 2, 1)
ALPHA = 2.0 ** 0.25
NEG = -1e30
BAND = 640

VECS = {}
_n = 0
for _name, _w in (("norm_g", 8), ("conv_w", 8 * TAPS), ("conv_b", 8), ("ln_g", 8), ("ln_b", 8), ("lb0", 8),
                  ("lb1", 8), ("gnorm_g", 8), ("final_g", 8), ("mix_g", 8), ("cw2", 6), ("gg2", 8),
                  ("mlp_g2", 8), ("fin_g2", 8), ("cw3", 32), ("hn_g", 4), ("pscale", 4), ("ln1_g", 8),
                  ("ln1_b", 8), ("ln2_g", 8), ("ln2_b", 8), ("b_i", 1), ("b_f", 1)):
    VECS[_name] = (_n, _w)
    _n += _w
NVEC = _n
CONSTS = {}
_n = 0
for _name, _w in (("ident", 128), ("ones", 128), ("selA8", 64), ("selB8", 1024), ("selA4", 32),
                  ("selB4", 512), ("tri", 128), ("tril_neg", 128),
                  ("inv", 16)):
    CONSTS[_name] = (_n, _w)
    _n += _w
NCONST = _n


class Lane:

    def __init__(self, eng, sem):
        self.eng, self.sem, self.count, self.seen = eng, sem, 0, {}

    def after(self, *tokens):
        for t in tokens:
            if t is None:
                continue
            if isinstance(t, list):
                self.after(*t)
                continue
            sem, value = t
            if self.seen.get(id(sem), 0) < value:
                self.eng.wait_ge(sem, value)
                self.seen[id(sem)] = value
        return self.eng

    def mark(self, instruction):
        self.count += 1
        instruction.then_inc(self.sem, 1)
        return (self.sem, self.count)


class Port:

    def __init__(self, lane, sem):
        self.lane, self.sem, self.count = lane, sem, 0

    def start(self, out, in_, *tokens):
        if self.count:
            self.lane.after((self.sem, self.count))
        self.lane.after(*tokens)
        self.count += 16
        self.lane.eng.dma_start(out, in_).then_inc(self.sem, 16)
        return (self.sem, self.count)


class Slot:

    def __init__(self, ap):
        self.ap, self.free = ap, []


class Ring:
    def __init__(self, slots):
        self.slots, self.n = slots, 0

    def take(self):
        s = self.slots[self.n % len(self.slots)]
        self.n += 1
        return s


HEAD = 348
REST = (TM - HEAD) // 2


def program(nc, A):
    ctx = ExitStack()

    def sem(name):
        return ctx.enter_context(nc.semaphore(name))

    PE = Lane(nc.tensor, sem("pe_done"))
    VE = Lane(nc.vector, sem("dve_done"))
    SE = Lane(nc.scalar, sem("act_done"))
    GP = Lane(nc.gpsimd, sem("pool_done"))
    SP = Lane(nc.sync, sem("sp_done"))

    def sb(name, shape, dt=F, scope=ctx):
        return scope.enter_context(nc.sbuf_tensor(name, shape, dt))

    raw = sb("raw", [P, 2, KT * 128])
    wh = sb("wh", [P, 2, KT * 128], FR)
    wl = sb("wl", [P, 2, KT * 128], FR)
    hh = sb("hh", [P, KT, TM], FR)
    hl = sb("hl", [P, KT, TM], FR)
    vec = sb("vec", [P, NVEC])
    cst = sb("cst", [P, NCONST])
    rr = sb("rr", [P, 2, 9])
    gmix = sb("gmix", [P, 8])
    psum = ctx.enter_context(nc.psum_tensor("psum", [P, 8, 512], F))

    def V(name, i=0, n=1):
        return vec[:, VECS[name][0] + i:VECS[name][0] + i + n]

    def C(name, parts=P):
        a, w = CONSTS[name]
        return cst[0:parts, a:a + w]

    ident, ones = C("ident"), C("ones")
    selA8 = C("selA8").rearrange("p (h m) -> p h m", h=8)
    selB8 = C("selB8", 8).rearrange("p (h m) -> p h m", h=8)
    selA4 = C("selA4").rearrange("p (t m) -> p t m", t=4)
    selB4 = C("selB4", 8).rearrange("p (t m) -> p t m", t=4)

    pairs = Ring([Slot(psum[:, 0:2, :]), Slot(psum[:, 2:4, :])])
    small = Slot(psum[:, 4, :])
    aux = Ring([Slot(psum[:, 5, :]), Slot(psum[:, 6, :]), Slot(psum[:, 7, :])])

    load_port = Ring([Port(SP, sem(f"ld{i}")) for i in range(4)])
    store_port = Ring([Port(SP, sem(f"st{i}")) for i in range(4)])
    w_port = [Port(SP, sem(f"wt{i}")) for i in range(2)]
    stores = []

    def load(out, in_, *tokens):
        return load_port.take().start(out, in_, *tokens)

    def store(out, in_, *tokens):
        t = store_port.take().start(out, in_, *tokens)
        stores.append(t)
        return t

    def act(out, in_, func, *tokens, **kw):
        return SE.mark(SE.after(*tokens).activation(out, in_, func, **kw))

    def tt(out, a, b, op, *tokens, lane=None):
        lane = lane or VE
        return lane.mark(lane.after(*tokens).tensor_tensor(out, a, b, op))

    def ts(out, a, s1, s2, op0, op1, *tokens):
        if s2 is None:
            return VE.mark(VE.after(*tokens).tensor_scalar(out, a, s1, None, op0))
        return VE.mark(VE.after(*tokens).tensor_scalar(out, a, s1, s2, op0, op1))

    def stt(out, a, s, b, op0, op1, *tokens):
        return VE.mark(VE.after(*tokens).scalar_tensor_tensor(out, a, s, b, op0, op1))

    def copy(out, in_, *tokens):
        return VE.mark(VE.after(*tokens).tensor_copy(out, in_))

    def recip(out, in_, *tokens):
        return VE.mark(VE.after(*tokens).reciprocal(out, in_))

    def zero(out, value, *tokens):
        return VE.mark(VE.after(*tokens).memset(out, value))

    def fp(ap):
        return ap.bitcast(F)

    jobs = []

    def pump(n=1):
        for _ in range(n):
            if not jobs:
                return
            try:
                next(jobs[0])
            except StopIteration:
                jobs.pop(0)

    def drain_jobs():
        while jobs:
            pump()

    def finish(job):
        while job in jobs:
            pump()

    NSLAB = A["wts"].shape[0]
    raw_free = [[], []]
    w_free = [[], []]
    raw_got = {}
    w_got = {}

    def w_fetch(i):
        if i < NSLAB and i not in raw_got:
            raw_got[i] = w_port[i % 2].start(raw[:, i % 2, :], A["wts"][i], raw_free[i % 2])

    def w_split(i):
        if i < NSLAB and i not in w_got:
            w_fetch(i)
            s = i % 2
            a = act(wh[:, s, :], raw[:, s, :], ACT.Copy, raw_got[i], w_free[s])
            b = tt(wl[:, s, :], raw[:, s, :], fp(wh[:, s, :]), ALU.subtract, a, w_free[s], lane=GP)
            raw_free[s] = [a, b]
            w_got[i] = [a, b]

    slab_no = [0]

    def next_slab():
        i = slab_no[0]
        slab_no[0] += 1
        w_split(i)
        w_fetch(i + 1)
        w_split(i + 1)
        w_fetch(i + 2)
        return i

    h_ready = [[] for _ in range(KT)]
    h_free = [[] for _ in range(KT)]

    def three(i, k):
        s = i % 2
        a, b = wh[:, s, k * 128:(k + 1) * 128], wl[:, s, k * 128:(k + 1) * 128]
        return a, b

    def products(pr, i, k, kw, first, final, xh, xl, off, meta):
        a, b = three(i, kw)
        if meta:
            parts = [(pr.ap[:, j, 0:REST], HEAD + j * REST, REST) for j in range(2)]
            head = [(small.ap[:, 0:HEAD], 0, HEAD)]
            groups = [parts, head] if first else [parts + head]
        else:
            groups = [[(pr.ap[:, j, :], off + j * 512, 512) for j in range(2)]]
        for g in groups:
            if meta and g is groups[-1]:
                PE.after(small.free)
            for n, (w, x) in enumerate(((a, xh), (b, xh), (a, xl))):
                for out, c, width in g:
                    ins = nc.tensor.matmul(out, w, x[:, k, c:c + width], start=first and n == 0,
                                           stop=final and n == 2)
        return ins

    def with_meta(pr, dst, func, *tokens):
        a = act(dst[:, 0:HEAD], small.ap[:, 0:HEAD], func, *tokens)
        small.free = [a]
        b = act(dst[:, HEAD:TM].rearrange("p (j t) -> p j t", j=2), pr.ap[:, :, 0:REST], func, *tokens)
        pr.free = [b]
        return [a, b]

    ahead = []

    def split_ahead():
        w_split(slab_no[0])
        w_fetch(slab_no[0] + 1)
        w_split(slab_no[0] + 1)
        w_fetch(slab_no[0] + 2)

    def duo(meta=False, order=range(KT)):
        ids = [next_slab(), slab_no[0]]
        slab_no[0] += 1
        w_fetch(ids[1] + 1)
        prs = [pairs.take(), pairs.take()]
        out = [None, None]
        order = list(order)
        for n in range(KT + 1):
            for e in range(2):
                if not 0 <= n - e < KT:
                    continue
                k = order[n - e]
                if n == e:
                    PE.after(w_got[ids[e]], prs[e].free)
                assert h_ready[k] is not None
                PE.after(h_ready[k])
                ins = products(prs[e], ids[e], k, k, n == e, n - e == KT - 1, hh, hl, META, meta and e == 0)
                if n - e == KT - 1:
                    d = PE.mark(ins)
                    w_free[ids[e] % 2] = [d]
                    out[e] = (prs[e], d, ids[e])
                    w_split(ids[e] + 2)
                    w_fetch(ids[e] + 3)
                pump()
        ahead.extend(out)

    def gemm_fm(meta=False, last=False, src=None, ready=None, nk=KT, slab=None, base=0):
        if ahead:
            return ahead.pop(0)
        own = slab is None
        i = next_slab() if own else slab
        srch, srcl = src or (hh, hl)
        ready = h_ready if ready is None else ready
        off = META if src is None else 0
        pr = pairs.take()
        PE.after(w_got[i], pr.free)
        frees = []
        for k in range(nk):
            PE.after(ready[k])
            ins = products(pr, i, k, k + base, k == 0, k == nk - 1, srch, srcl, off, meta)
            if last and k < nk - 1:
                frees.append([PE.mark(ins)])
            if k < nk - 1:
                pump()
        done = PE.mark(ins)
        frees.append([done])
        if own:
            w_free[i % 2] = [done]
        if last:
            for k in range(nk):
                h_free[k] = frees[k]
            if own:
                split_ahead()
        pump()
        return pr, done, i

    def turn(blocks, g, *tokens):
        x = aux.take()
        PE.after(x.free, *tokens)
        for c in range(4):
            ins = nc.tensor.transpose(x.ap[:, c * 128:(c + 1) * 128], blocks[:, 4 * g + c, :], ident)
        d = PE.mark(ins)
        t = act(blocks[:, 4 * g:4 * g + 4, :], x.ap.rearrange("p (c t) -> p c t", c=4), ACT.Copy, d)
        x.free = [t]
        return t

    def put_h(k, src, *tokens, c0=META, n=T):
        a = act(hh[:, k, c0:c0 + n], src, ACT.Copy, *tokens, h_free[k])
        b = tt(hl[:, k, c0:c0 + n], src, fp(hh[:, k, c0:c0 + n]), ALU.subtract, a, *tokens, h_free[k],
               lane=GP if k in (3, 5, 7) else VE)
        return [a, b]

    O = B0 = sb("B0", [P, KT, T])
    s0 = ExitStack()
    X0 = sb("X0", [P, KT, TM], F, s0)
    sq0 = sb("sq0", [P, 2, TM], F, s0)
    R0 = sb("R0", [P, TM], F, s0)

    tx = [load(X0[:, k, :], A["xin"][k]) for k in range(KT)]
    t_vec = load(vec[:, :], A["vec"])
    t_cst = load(cst[:, :], A["cst"])
    w_fetch(0)
    w_fetch(1)
    for ln in (PE, GP):
        ln.after(t_vec, t_cst)

    def put_all(make):
        late = None

        def close():
            k, src, a, tokens, then = late
            b = tt(hl[:, k, :][:, TM - src.shape[1]:], src, fp(hh[:, k, :])[:, TM - src.shape[1]:], ALU.subtract,
                   a, tokens, h_free[k], lane=GP if k in (3, 5, 7) else VE)
            h_ready[k] = [a, b]
            then([a, b])

        for k in range(KT):
            src, tokens, then = make(k)
            a = act(hh[:, k, :][:, TM - src.shape[1]:], src, ACT.Copy, tokens, h_free[k])
            if late:
                close()
            late = (k, src, a, tokens, then)
        close()

    def flat(ap):
        return ap.rearrange("p a b -> p (a b)")

    def sums(tiles, sqs, width, lhs=ones, square=True, rows=P):
        pr = pairs.take()
        PE.after(pr.free)
        n = len(tiles)
        for t, (ap, toks) in enumerate(tiles):
            if square:
                q = sqs.take()
                a = act(q.ap[:, 0:width], ap, ACT.Square, toks, q.free)
                src = q.ap
            else:
                a, src = toks, ap
            PE.after(a)
            l = lhs(t) if callable(lhs) else lhs
            off = 0
            for j in range(2):
                ins = nc.tensor.matmul(pr.ap[0:rows, j, :], l, src[:, off + j * 512:off + (j + 1) * 512],
                                       start=(t == 0), stop=(t == n - 1))
            d = PE.mark(ins)
            if square:
                q.free = [d]
        return pr, d

    rr_free = [None, None]

    class Stats:

        def __init__(self, acc, ring, slot=0, raw=False, free=None):
            self.acc, self.ring, self.slot, self.raw = acc, ring, slot, raw
            self.n, self.t, self.late = 0, free, None

        def add(self, ap, *tokens, lane=None, scale=1.0, now=False):
            if self.raw:
                if self.n == 0:
                    self.first = ap
                    self.t = [self.t, list(tokens)]
                else:
                    a_, self.first = (self.acc if self.n > 1 else self.first), None
                    self.t = tt(self.acc, a_, ap, ALU.add, self.t, *tokens, lane=lane or GP)
            elif self.n == 0:
                self.t = act(self.acc, ap, ACT.Square, self.t, *tokens, scale=scale)
            else:
                q = self.ring.take()
                a = act(q.ap, ap, ACT.Square, q.free, *tokens, scale=scale)
                self.flush()
                self.late = (q, a, lane or GP)
                if now:
                    self.flush()
            self.n += 1

        def flush(self):
            if self.late is not None:
                q, a, lane = self.late
                self.t = tt(self.acc, self.acc, q.ap, ALU.add, a, self.t, lane=lane)
                q.free = [self.t]
                self.late = None

        def by_token(self, func, meta=False, **kw):
            self.flush()
            x = aux.take()
            off = META if meta else 0
            PE.after(x.free, self.t)
            for c in range(8):
                ins = nc.tensor.matmul(x.ap[:, c:c + 1], self.acc[:, off + c * 128:off + (c + 1) * 128], ones[:, 0:1],
                                       start=True, stop=True)
            if meta:
                ins = nc.tensor.matmul(x.ap[0:META, 8:9], self.acc[:, 0:META], ones[:, 0:1], start=True, stop=True)
            self.d = PE.mark(ins)
            r = rr[:, self.slot, :]
            t = [act(r[:, 0:8], x.ap[:, 0:8], func, self.d, rr_free[self.slot], **kw)]
            if meta:
                t.append(act(r[0:META, 8:9], x.ap[0:META, 8:9], func, self.d, rr_free[self.slot], **kw))
            x.free = t
            return r, t

        def inverse_root(self, R, eps, *tokens, meta=False):
            r, t = self.by_token(ACT.Sqrt, meta, scale=1.0 / 1024, bias=eps)
            u = [recip(r[:, 0:8], r[:, 0:8], t)]
            if meta:
                u.append(recip(r[0:META, 8:9], r[0:META, 8:9], t))
            return spread(R, self.slot, u, *tokens, meta=meta)

    def spread(R, slot, ready, *tokens, meta=False):
        r = rr[:, slot, :]
        out = []
        off = META if meta else 0
        if meta:
            x = aux.take()
            d = PE.mark(PE.after(x.free, ready).matmul(x.ap[:, 0:META], r[0:META, 8:9].to_broadcast([META, P]),
                                                       ident[0:META, 0:META], start=True, stop=True))
            out.append(act(R[:, 0:META], x.ap[:, 0:META], ACT.Copy, d, *tokens))
            x.free = [out[-1]]
        for g in range(2):
            x = aux.take()
            PE.after(x.free, ready)
            for c in range(4):
                ins = nc.tensor.matmul(x.ap[:, c * 128:(c + 1) * 128],
                                       r[:, 4 * g + c:4 * g + c + 1].to_broadcast([P, P]), ident,
                                       start=True, stop=True)
            d = PE.mark(ins)
            out.append(act(R[:, off + g * 512:off + (g + 1) * 512], x.ap, ACT.Copy, d, *tokens))
            x.free = [out[-1]]
        rr_free[slot] = [d]
        return out

    sqr = Ring([Slot(sq0[:, i, :]) for i in range(2)])
    acc0 = sb("acc0", [P, TM], F, s0)
    st = Stats(acc0[:, :], sqr)
    for k in range(KT):
        st.add(X0[:, k, :], tx[k], lane=VE)
    w_split(0)
    w_split(1)
    r = st.inverse_root(R0, EPS, meta=True)
    VE.after(t_vec, t_cst)
    SE.after(t_vec, t_cst)
    def first(k):
        c = stt(X0[:, k, :], X0[:, k, :], V("norm_g", k), R0[:, :], ALU.mult, ALU.mult, r, tx[k], st.t)
        return X0[:, k, :], [c], lambda t: None

    put_all(first)
    s0_done = [t for k in range(KT) for t in h_ready[k]]
    s0.close()

    s1 = ExitStack()
    masks = sb("masks", [P, 7, 128], F, s1)
    rmask = sb("rmask", [P, TM], F, s1)
    fb = sb("fb", [P, 2, TM], F, s1)
    kb = sb("kb", [P, 2, TM], F, s1)
    qb = sb("qb", [P, 2, T], F, s1)
    vb = sb("vb", [P, 2, T], F, s1)
    vm = sb("vm", [META, 128], F, s1)
    vmT = sb("vmT", [P, 2, META], F, s1)
    work = sb("work", [P, 4, TM], F, s1)
    Ab = sb("Ab", [P, T], F, s1)
    kdT = sb("kdT", [P, T], F, s1)
    kdm = sb("kdm", [META, 128], F, s1)
    Sb = sb("Sb", [P, T], F, s1)
    ebl = sb("ebl", [P, 2, 9], F, s1)
    lbv = sb("lbv", [P, 4, 8], F, s1)
    t_mask = load(flat(masks[:, :, :]), A["masks"], s0_done)
    z1 = zero(rmask[:, :], 1.0, s0_done)
    z2 = zero(rmask[:, META:TM].rearrange("p (c t) -> p c t", c=8)[:, :, 0:1], 0.0, z1)
    mx = tt(lbv[:, 0, :], V("lb0", 0, 8), V("lb1", 0, 8), ALU.max, s0_done)
    l0 = tt(lbv[:, 1, :], V("lb0", 0, 8), lbv[:, 0, :], ALU.subtract, mx)
    l1 = tt(lbv[:, 2, :], V("lb1", 0, 8), lbv[:, 0, :], ALU.subtract, mx)
    e0 = act(lbv[:, 1, :], lbv[:, 1, :], ACT.Exp, l0)
    e1 = act(lbv[:, 2, :], lbv[:, 2, :], ACT.Exp, l1)
    l2 = tt(lbv[:, 0, :], lbv[:, 1, :], lbv[:, 2, :], ALU.add, e0, e1)
    l3 = recip(lbv[:, 0, :], lbv[:, 0, :], l2)
    l4 = tt(lbv[:, 1, :], lbv[:, 1, :], lbv[:, 0, :], ALU.mult, l3)
    l5 = ts(lbv[:, 2, :], lbv[:, 1, :], -1.0, 1.0, ALU.mult, ALU.add, l4)
    lb_ready = [l4, l5]
    LB = lbv[:, 1, :]
    OML = lbv[:, 2, :]

    wk = Ring([Slot(work[:, i, :]) for i in range(4)])
    Aslot, kdslot, sslot = Slot(Ab), Slot(kdT), Slot(Sb)
    hd_free, vm_free = [[], []], [[]]
    o_ready = [None] * 8
    A4 = lambda ap: ap.rearrange("p (c t) -> p c t", c=8)

    def half(ap, hs):
        v = ap.rearrange("p (n b) -> p n b", b=2 * hs)
        return v[:, :, 0:hs], v[:, :, hs:2 * hs]

    def hgrn(h, s, tf, tq, tv):
        f, kk, q, v = fb[:, s, :], kb[:, s, :], qb[:, s, :], vb[:, s, :]
        bx, kx = f[:, META:TM], kk[:, META:TM]
        lastb = A4(bx)[:, :, 127:128]
        kfree, a_tok = [None, None], [None, None]
        lev = [None] * 7

        a = ts(f, f, OML[:, h:h + 1], LB[:, h:h + 1], ALU.mult, ALU.add, tf, lb_ready)
        tk = ts(kk, f, -1.0, 1.0, ALU.mult, ALU.add, a, hd_free[s])
        a = ts(f, f, 2.0 ** -63, None, ALU.max, None, a, tk)
        tv0 = turn(A4(v), 0, tv)
        yield
        w = wk.take()
        a = act(w.ap, f, ACT.Ln, a, w.free)
        tb = VE.mark(VE.after(a, z2).tensor_tensor_scan(f, rmask[:, :], w.ap, 0.0, ALU.mult, ALU.add))
        w.free = [tb]
        tv = [tv0, turn(A4(v), 1, tv), tv]
        yield

        def below(lv):
            hs = HALVES[lv]
            w = wk.take()
            bv = bx.rearrange("p (n b) -> p n b", b=2 * hs)
            t = tt(w.ap[:, 0:T].rearrange("p (n b) -> p n b", b=2 * hs), bv,
                   bv[:, :, hs - 1:hs].to_broadcast([P, T // (2 * hs), 2 * hs]), ALU.subtract, tb, w.free, lane=GP)
            lev[lv] = [w, t]

        def exps(lv):
            w, t = lev[lv]
            ul, ur = half(w.ap[:, 0:T], HALVES[lv])
            lev[lv][1] = (act(ul, ul, ACT.Exp, t, scale=-1.0), act(ur, ur, ACT.Exp, t))

        def mults(lv):
            w, (e1, e2) = lev[lv]
            ul, ur = half(w.ap[:, 0:T], HALVES[lv])
            lev[lv][1] = [tt(ul, ul, half(kx, HALVES[lv])[0], ALU.mult, e1, tk),
                          tt(ur, ur, half(q, HALVES[lv])[1], ALU.mult, e2, tq)]

        def product(lv, g):
            if lv < 7:
                w, tok = lev[lv]
                left = right = w.ap
                m = masks[:, lv:lv + 1, :]
            else:
                left, right, tok = kx, q, [tk, tq]
                m = ident.rearrange("p (o t) -> p o t", o=1)
            x = aux.take()
            PE.after(x.free, tok)
            for c in range(4 * g, 4 * g + 4):
                ins = nc.tensor.matmul(x.ap[:, (c % 4) * 128:(c % 4 + 1) * 128],
                                       left[:, c * 128:(c + 1) * 128], right[:, c * 128:(c + 1) * 128],
                                       start=True, stop=True)
            d = PE.mark(ins)
            dst = Ab[:, g * 512:(g + 1) * 512].rearrange("p (c t) -> p c t", c=4)
            src = x.ap.rearrange("p (c t) -> p c t", c=4)
            m = m.to_broadcast([P, 4, 128])
            if lv == 7:
                t = tt(dst, src, m, ALU.mult, d, Aslot.free)
            else:
                t = VE.mark(VE.after(d, a_tok[g], t_mask).copy_predicated(dst, m.bitcast(I32), src))
                if g:
                    w.free = [d]
            a_tok[g] = t
            x.free = [t]

        def turned(g):
            x = aux.take()
            PE.after(kd, x.free)
            for c in range(4):
                ins = nc.tensor.transpose(x.ap[:, c * 128:(c + 1) * 128],
                                          wd.ap[:, META + (4 * g + c) * 128:META + (4 * g + c + 1) * 128], ident)
            d = PE.mark(ins)
            kfree[g] = act(kdT[:, g * 512:(g + 1) * 512], x.ap, ACT.Copy, d, kdslot.free)
            x.free = [kfree[g]]

        te1 = act(ebl[:, s, 0:1], f[:, META - 1:META], ACT.Exp, tb, hd_free[s])
        te2 = act(ebl[:, s, 1:9], lastb.rearrange("p c o -> p (c o)"), ACT.Exp, tb, hd_free[s])
        wd = wk.take()
        c1 = tt(A4(wd.ap[:, META:TM]), lastb.to_broadcast([P, 8, 128]), A4(bx), ALU.subtract, tb, wd.free)
        c2 = tt(wd.ap[:, 0:META], f[:, META - 1:META].to_broadcast([P, META]), f[:, 0:META], ALU.subtract,
                tb, wd.free)
        e = act(wd.ap, wd.ap, ACT.Exp, c1, c2)
        below(0)
        below(1)
        product(7, 0)
        yield
        kd = tt(wd.ap, wd.ap, kk, ALU.mult, e, tk)
        product(7, 1)
        exps(0)
        yield
        turned(0)
        mults(0)
        exps(1)
        yield
        turned(1)
        mults(1)
        below(2)
        yield
        product(0, 0)
        x = aux.take()
        PE.after(x.free)
        d = PE.mark(nc.tensor.transpose(x.ap[0:META, 0:128], wd.ap[:, 0:META], ident))
        wd.free = [d]
        gm = act(kdm[:, :], x.ap[0:META, 0:128], ACT.Copy, d, kdslot.free)
        x.free = [gm]
        x = aux.take()
        PE.after(x.free)
        d = PE.mark(nc.tensor.transpose(x.ap[0:META, 0:128], vmT[:, s, :], ident))
        gv = act(vm[:, :], x.ap[0:META, 0:128], ACT.Copy, d, vm_free[0])
        x.free = [gv]
        exps(2)
        below(3)
        yield
        x = aux.take()
        PE.after(x.free, gm, gv, tv)
        d = PE.mark(nc.tensor.matmul(x.ap[:, 0:128], kdm[:, :], vm[:, :], start=True, stop=True))
        vm_free[0] = [d]
        ss = act(Sb[:, 0:128], x.ap[:, 0:128], ACT.Copy, d, sslot.free)
        x.free = [ss]
        product(0, 1)
        yield

        def state(g, ss):
            x = aux.take()
            PE.after(x.free, kfree[g])
            n = 4 if g == 0 else 3
            for c in range(4 * g, 4 * g + n):
                ins = nc.tensor.matmul(x.ap[:, (c % 4) * 128:(c % 4 + 1) * 128], kdT[:, c * 128:(c + 1) * 128],
                                       v[:, c * 128:(c + 1) * 128], start=True, stop=True)
            d = PE.mark(ins)
            for c in range(4 * g, 4 * g + n):
                ss = stt(Sb[:, (c + 1) * 128:(c + 2) * 128], Sb[:, c * 128:(c + 1) * 128],
                         ebl[:, s, c + 1:c + 2], x.ap[:, (c % 4) * 128:(c % 4 + 1) * 128],
                         ALU.mult, ALU.add, ss, d, te1, te2)
            x.free = [ss]
            kdslot.free = [d]
            return ss

        w2 = None
        for lv in range(1, 7):
            if lv < 6:
                mults(lv + 1)
            product(lv, 0)
            if lv < 5:
                exps(lv + 2)
            elif lv == 5:
                w2 = wk.take()
                qe = w2.ap[:, 0:T]
                e = act(qe, bx, ACT.Exp, tb, w2.free)
            yield
            if lv < 4:
                below(lv + 3)
            if lv == 6:
                tqe = tt(qe, qe, q, ALU.mult, e, tq)
            product(lv, 1)
            if lv in (2, 4):
                yield
                ss = state(lv // 2 - 1, ss)
            yield
        for g in range(2):
            x = aux.take()
            PE.after(x.free, a_tok[g], tqe, ss, tv)
            for c in range(4 * g, 4 * g + 4):
                o = x.ap[:, (c % 4) * 128:(c % 4 + 1) * 128]
                cc = slice(c * 128, (c + 1) * 128)
                nc.tensor.matmul(o, v[:, cc], Ab[:, cc], start=True, stop=False)
                ins = nc.tensor.matmul(o, Sb[:, cc], qe[:, cc], start=False, stop=True)
            d = PE.mark(ins)
            t = act(O[:, h, g * 512:(g + 1) * 512], x.ap, ACT.Copy, d)
            x.free = [t]
            if g == 0:
                yield
        w2.free = [d]
        Aslot.free, sslot.free = [d], [d]
        hd_free[s] = [d, t]
        o_ready[h] = t

    prev = None
    duo(meta=True)
    for h in range(8):
        s = h % 2
        pr, d, _ = gemm_fm(meta=True)
        tf = with_meta(pr, fb[:, s, :], ACT.Sigmoid, d, hd_free[s], z2)
        pr, d, _ = gemm_fm()
        tq = act(qb[:, s, :], flat(pr.ap), ACT.Silu, d, hd_free[s])
        pr.free = [tq]
        pr, d, _ = gemm_fm(meta=True)
        b = act(vmT[:, s, :], small.ap[:, 0:META], ACT.Copy, d, hd_free[s])
        b = act(vb[:, s, 0:HEAD - META], small.ap[:, META:HEAD], ACT.Copy, d)
        a = act(vb[:, s, HEAD - META:].rearrange("p (j t) -> p j t", j=2), pr.ap[:, :, 0:REST], ACT.Copy, d)
        pr.free, small.free = [a], [b]
        if prev is not None:
            finish(prev)
        prev = hgrn(h, s, tf, tq, [a, b])
        jobs.append(prev)

    GR = nc.dram_tensor("keep_gr", [KT, P, T], F, kind="Internal").ap()
    GC = nc.dram_tensor("keep_gc", [KT, P, T], F, kind="Internal").ap()
    SZ = nc.dram_tensor("keep_sz", [KT, P, T], F, kind="Internal").ap()
    gr_kept, gc_kept, sz_kept = [None] * 8, [None] * 8, [None] * 8

    def gate_out(buf, dram, m, func):
        pr, d, _ = gemm_fm()
        a = act(buf.ap, flat(pr.ap), func, d, buf.free)
        pr.free = [a]
        t = store(dram[m], buf.ap, a)
        buf.free = [t]
        return t

    gbuf = Ring([Slot(qb[:, 0, :]), Slot(vb[:, 0, :])])
    for g in gbuf.slots:
        g.free = [hd_free[0]]
    for m in range(8):
        gr_kept[m] = gate_out(gbuf.take(), GR, m, ACT.Sigmoid)
    finish(prev)
    s1_done = [hd_free[0], hd_free[1], gr_kept]
    s1.close()

    s2 = ExitStack()
    Cb = sb("Cb", [P, KT, T], F, s2)
    s3 = ExitStack()
    av = sb("av", [P, 2, HIST + T], F, s3)
    sg = sb("sg", [P, 2, TM], F, s3)
    tmp = sb("tmp", [P, 3, T], F, s3)
    R8 = sb("R8", [8, T], F, s3)
    accc = sb("accc", [P, T], F, s3)
    tr = Ring([Slot(tmp[:, i, :]) for i in range(3)])
    for q in tr.slots:
        q.free = [s1_done]

    r8 = [None, None]

    def head_norm():
        xs = [aux.take(), aux.take()]
        PE.after(xs[0].free, xs[1].free)
        for h in range(8):
            q = tr.take()
            a = act(q.ap, O[:, h, :], ACT.Square, o_ready[h], q.free)
            yield
            PE.after(a)
            for j in range(2):
                ins = nc.tensor.matmul(xs[j].ap[0:8, :], selA8[:, h, :], q.ap[:, j * 512:(j + 1) * 512],
                                       start=(h == 0), stop=(h == 7))
            d = PE.mark(ins)
            q.free = [d]
        for j in range(2):
            R = R8[:, j * 512:(j + 1) * 512]
            a = act(R, xs[j].ap[0:8, :], ACT.Sqrt, d, s1_done, scale=1.0 / 128, bias=EPS)
            xs[j].free = [a]
            r8[j] = recip(R, R, a)
            yield

    avs = [Slot(av[:, i, :]) for i in range(2)]
    sgs = [Slot(sg[:, i, :]) for i in range(2)]
    za = zero(av[:, :, 0:HIST - META], 0.0, s1_done)
    for q in avs + sgs:
        q.free = [za, s1_done]
    c_ready = [None] * 8
    cs = Stats(accc[:, :], None, 0, raw=True, free=[s1_done])

    def convolve(m, u, t):
        c = ts(Cb[:, m, :], u.ap[:, 0:T], V("conv_w", m), V("conv_b", m), ALU.mult, ALU.add, t, s1_done)
        for j in range(1, TAPS):
            c = stt(Cb[:, m, :], u.ap[:, j:j + T], V("conv_w", 8 * j + m), Cb[:, m, :], ALU.mult, ALU.add, c)
            if j < TAPS - 1:
                yield
        u.free = [c]
        c_ready[m] = c

    jobs.append(head_norm())
    prev = None
    for m in range(8):
        u, w = avs[m % 2], sgs[m % 2]
        pr, d, _ = gemm_fm(meta=True)
        a = with_meta(pr, u.ap[:, HIST - META:], ACT.Copy, d, u.free)
        pr, d, _ = gemm_fm(meta=True)
        b = with_meta(pr, w.ap, ACT.Sigmoid, d, w.free)
        t = tt(u.ap[:, HIST - META:], u.ap[:, HIST - META:], w.ap, ALU.mult, a, b)
        w.free = [t]
        if m:
            finish(prev)
            cs.add(Cb[:, m - 1, :], c_ready[m - 1])
        if m == 0:
            drain_jobs()
        prev = convolve(m, u, t)
        jobs.append(prev)
        pr, d, _ = gemm_fm()
        q = tr.take()
        a = act(q.ap, flat(pr.ap), ACT.Silu, d, q.free)
        pr.free = [a]
        for j in range(2):
            x = aux.take()
            oh = O[:, m, j * 512:(j + 1) * 512]
            d = PE.mark(PE.after(x.free, r8[j]).matmul(x.ap, selB8[:, m, :], R8[:, j * 512:(j + 1) * 512],
                                                    start=True, stop=True))
            t = stt(oh, oh, V("gnorm_g", m), x.ap, ALU.mult, ALU.mult, d, o_ready[m])
            x.free = [t]
            t = tt(oh, oh, q.ap[:, j * 512:(j + 1) * 512], ALU.mult, t, a)
        q.free = [t]
        o_ready[m] = t
        sz_kept[m] = gate_out(tr.take(), SZ, m, ACT.Silu)

    def conv_norm():
        R = sg[:, 0, 0:T]
        cs.add(Cb[:, 7, :], c_ready[7], lane=VE)
        yield
        _, t = cs.by_token(ACT.Copy, scale=1.0 / 1024)
        yield
        r = spread(R, 0, t, sgs[0].free)
        yield
        st = Stats(accc[:, :], tr, 1, free=[cs.d])
        for k in range(8):
            c_ready[k] = tt(Cb[:, k, :], Cb[:, k, :], R, ALU.subtract, r, c_ready[k], cs.t)
            st.add(Cb[:, k, :], c_ready[k])
            yield
            yield
        yield
        r = st.inverse_root(R, EPS, c_ready)
        yield
        yield
        for k in range(8):
            q = tr.take()
            ld = load(q.ap, SZ[k], sz_kept[k], q.free)
            t = tt(Cb[:, k, :], Cb[:, k, :], R, ALU.mult, r, c_ready[k])
            a = act(Cb[:, k, :], Cb[:, k, :], ACT.Silu, t, scale=V("ln_g", k), bias=V("ln_b", k))
            yield
            yield
            t = tt(Cb[:, k, :], Cb[:, k, :], q.ap, ALU.mult, a, ld)
            q.free = [t]
            c_ready[k] = t
            yield

    gb = Ring([Slot(sg[:, 1, 0:T])])
    gb.slots[0].free = sgs[1].free
    for m in range(8):
        pr, d, _ = gemm_fm(last=(m == 7))
        buf = gb.take()
        a = act(buf.ap, flat(pr.ap), ACT.Sigmoid, d, buf.free)
        pr.free = [a]
        gc_kept[m] = store(GC[m], buf.ap, a)
        buf.free = [gc_kept[m]]
        if m == 3:
            finish(prev)
            gb.slots += [Slot(av[:, i, 0:T]) for i in range(2)]
            gb.slots[1].free, gb.slots[2].free = avs[0].free, avs[1].free
            prev = conv_norm()
            jobs.append(prev)

    for k in range(8):
        h_ready[k] = put_h(k, O[:, k, :], o_ready[k])
    split_o = [list(t) for t in h_ready]
    gl = Ring(gb.slots[1:])

    def fetch(dram, m, kept):
        q = gl.take()
        return q, load(q.ap, dram[m], kept, q.free)

    m_ready = [None] * 8
    nxt = fetch(GR, 0, gr_kept[0])
    duo()
    for m in range(8):
        q, ld = nxt
        if m < 7:
            nxt = fetch(GR, m + 1, gr_kept[m + 1])
        pr, d, _ = gemm_fm(last=(m == 7))
        t = tt(O[:, m, :], flat(pr.ap), q.ap, ALU.mult, d, ld, split_o[m])
        pr.free, q.free = [t], [t]
        m_ready[m] = t
    finish(prev)
    for k in range(8):
        h_ready[k] = put_h(k, Cb[:, k, :], c_ready[k])
    split_c = [list(t) for t in h_ready]
    nxt = fetch(GC, 0, gc_kept[0])
    duo()
    for m in range(8):
        q, ld = nxt
        if m < 7:
            nxt = fetch(GC, m + 1, gc_kept[m + 1])
        pr, d, _ = gemm_fm(last=(m == 7))
        t = tt(q.ap, flat(pr.ap), q.ap, ALU.mult, d, ld)
        pr.free = [t]
        t = tt(O[:, m, :], O[:, m, :], q.ap, ALU.add, t, m_ready[m])
        q.free = [t]
        m_ready[m] = t
    for k in range(8):
        h_ready[k] = put_h(k, O[:, k, :], m_ready[k])

    X = O
    x_ready = [None] * 8
    split_o = [list(t) for t in h_ready]
    st_ring = Ring([Slot(Cb[:, 4 + i, :]) for i in range(4)])
    for q in st_ring.slots:
        q.free = [split_c]
    st = Stats(Cb[:, 0, :], st_ring, 0, free=[split_c])
    sg_ = Stats(Cb[:, 1, :], st_ring, 1, free=[split_c])

    def fetch_x(m):
        q = gl.take()
        return q, load(q.ap, A["xin"][m][:, META:TM], q.free)

    nxt = fetch_x(0)
    duo()
    for m in range(8):
        q, ld = nxt
        if m < 7:
            nxt = fetch_x(m + 1)
        pr, d, _ = gemm_fm(last=(m == 7))
        t = tt(X[:, m, :], flat(pr.ap), q.ap, ALU.add, d, ld, split_o[m])
        pr.free, q.free = [t], [t]
        x_ready[m] = t
        lane = GP if m < 7 else VE
        st.add(X[:, m, :], t, lane=lane, now=m < 7)
        sg_.add(X[:, m, :], t, lane=lane, scale=V("final_g", m), now=m < 7)
    R, R12 = Cb[:, 2, :], Cb[:, 3, :]
    ra, ta = st.by_token(ACT.Copy, scale=1.0 / 1024)
    rb, tb = sg_.by_token(ACT.Copy, scale=1.0 / 1024)
    r8_, rb8 = ra[:, 0:8], rb[:, 0:8]
    a = act(r8_, r8_, ACT.Sqrt, ta, bias=EPS)
    a = recip(r8_, r8_, a)
    b = tt(rb8, rb8, r8_, ALU.mult, a, tb)
    b = tt(rb8, rb8, r8_, ALU.mult, b)
    b = act(rb8, rb8, ACT.Sqrt, b, bias=EPS)
    b = recip(rb8, rb8, b)
    b = tt(rb8, rb8, r8_, ALU.mult, b)
    tg = tt(gmix[:, :], V("final_g", 0, 8), V("mix_g", 0, 8), ALU.mult)
    r12 = spread(R12, 1, b, split_c)

    XS = nc.dram_tensor("keep_x", [KT, P, T], F, kind="Internal").ap()
    nr = st_ring
    xs_kept = [None] * 8

    def normed(ring, gain, R, r):
        def make(k):
            q = ring.take()
            t = stt(q.ap, X[:, k, :], gain(k), R, ALU.mult, ALU.mult, r, x_ready[k], q.free)

            def then(t):
                q.free = t

            return q.ap, [t], then

        put_all(make)

    normed(nr, lambda k: gmix[:, k:k + 1], R12, [r12, tg])
    r = spread(R, 0, a, split_c)
    for k in range(8):
        x_ready[k] = stt(X[:, k, :], X[:, k, :], V("final_g", k), R, ALU.mult, ALU.mult, r, x_ready[k], st.t, sg_.t)

    def keep_x():
        for k in (6, 7, 4, 5, 0, 1, 2, 3):
            xs_kept[k] = store(XS[k], X[:, k, :], x_ready[k])
            yield

    duo()
    jobs.append(keep_x())
    old = [xs_kept, [q.free for q in nr.slots], x_ready, r]
    s3.close()
    s2.close()

    aux.slots.append(small)
    s45 = ExitStack()
    xs0 = Slot(sb("xs0", [P, T], F, s45)[:, :])
    xs0.free = [old]
    s4 = ExitStack()
    qa = sb("qa", [P, 2, T], F, s4)
    ka = sb("ka", [P, 2, T], F, s4)
    va = sb("va", [P, 2, T], F, s4)
    oa = sb("oa", [P, 8, 128], F, s4)
    bias = sb("bias", [P, 2, BAND], F, s4)
    pp = sb("pp", [P, 3, BAND], F, s4)
    pt = sb("pt", [P, 2, BAND], F, s4)
    st2 = sb("st2", [P, 4, 8], F, s4)
    ss2 = sb("ss2", [P, 8], F, s4)
    rsum = sb("rsum", [P, 2, 8], F, s4)
    zb = sb("zb", [P, T + 2], F, s4)
    gt = sb("gt", [P, 2, T], F, s4)
    vg = sb("vg", [P, 8, 256], F, s4)
    osq = vg[:, :, 0:64]
    sgw = sb("sgw", [P, 4, 128], F, s4)
    sgc = sb("sgc", [P, 3, 256], F, s4)
    bst = sb("bst", [P, 8, 6], F, s4)
    bag = sb("bag", [P, 8, 2], F, s4)
    R8b = qa[0:8, 0, :]
    MX = B0
    t_sgw = load(flat(sgw[:, :, :]), A["sgw"], old)
    t_sgc = load(flat(sgc[:, :, :]), A["sgc"], old)
    t_ws = tt(sgw[:, :, :], sgw[:, :, :], C("tri").rearrange("p (o t) -> p o t", o=1).to_broadcast([P, 4, 128]),
              ALU.mult, t_sgw)
    zz = zero(zb[:, 0:2], 0.0, old)

    bias_r = Ring([Slot(bias[:, i, :]) for i in range(2)])
    pp_r = Ring([Slot(pp[:, i, :]) for i in range(3)])
    pt_r = Ring([Slot(pt[:, i, :]) for i in range(2)])
    for q in bias_r.slots + pp_r.slots + pt_r.slots:
        q.free = [old]
    S = Slot(psum[:, 4:6, :])
    TL, PT, OUT = Slot(psum[:, 5, 0:128]), Slot(psum[:, 6, :]), Slot(psum[:, 7, :])
    qkv_free = [[old], [old]]
    oa_free = [old]
    mx_ready = [None] * 8

    def attention(j, s, tq, tk, tv):
        nonlocal oa_free
        items = [(hh_, i) for hh_ in range(2) for i in range(8)]
        got = {}
        bt = {}
        tn = qkv_free[s]
        PE.after(S.free, TL.free, tv)
        for c in range(8):
            ins = nc.tensor.transpose(flat(S.ap)[:, c * 128:(c + 1) * 128], va[:, s, c * 128:(c + 1) * 128], ident)
        d = PE.mark(ins)
        tv = act(va[:, s, :], flat(S.ap), ACT.Copy, d)
        S.free = TL.free = [tv]
        yield
        for n in range(len(items) + 3):
            m = n - 3
            if n < len(items):
                hh2, i2 = items[n]
                if i2 == 0:
                    bq = bias_r.take()
                    bt[hh2] = (bq, load(bq.ap, A["bias"][2 * j + hh2], bq.free))
                bq, tb = bt[hh2]
                nk2 = min(BAND, 128 * (i2 + 1))
                k2 = 128 * (i2 + 1) - nk2
                lo = 64 * hh2
                PE.after(S.free, tq, tk)
                sp = flat(S.ap)
                if nk2 > 512:
                    PE.after(TL.free)
                for a0 in range(0, nk2, 512):
                    w_ = min(512, nk2 - a0)
                    ins = nc.tensor.matmul(sp[:, a0:a0 + w_], qa[lo:lo + 64, s, i2 * 128:(i2 + 1) * 128],
                                           ka[lo:lo + 64, s, k2 + a0:k2 + a0 + w_], start=True, stop=True)
                ds = PE.mark(ins)
            if m >= 0:
                p, nk, k0, e, hh_, i, q, ev = got.pop(m)
                out = OUT.ap[:, 64 * i:64 * i + 64]
                PE.after(ev, tv, OUT.free)
                for b_ in range(nk // 128):
                    kt = k0 // 128 + b_
                    ins = nc.tensor.matmul(out, q.ap[:, b_ * 128:(b_ + 1) * 128],
                                           va[:, s, kt * 128 + 64 * hh_:kt * 128 + 64 * hh_ + 64],
                                           start=(b_ == 0), stop=(b_ == nk // 128 - 1))
                dv = PE.mark(ins)
                q.free = [dv]
            if n < len(items):
                p2 = pp_r.take()
                c = n % 4
                mx_, nm2 = (st2[:, c, z:z + 1] for z in range(2))
                rs = rsum[:, hh2, i2:i2 + 1]
                t = VE.mark(VE.after(ds, tb, p2.free).tensor_tensor_reduce(
                    p2.ap[:, 0:nk2], sp[:, 0:nk2], bq.ap[:, BAND - nk2:BAND], 1.0, -3.0e38, ALU.add, ALU.max, mx_))
                S.free = [t]
                if nk2 > 512:
                    TL.free = [t]
                if i2 == 7:
                    bq.free = [t]
                t = ts(nm2, mx_, -1.0, None, ALU.mult, None, t)
                got[n] = [p2, nk2, k2, None, hh2, i2]
            yield
            if 0 <= n - 2 < len(items):
                g = got[n - 2]
                p3, nk3 = g[0], g[1]
                q3_ = pt_r.take()
                ev3 = []
                PE.after(g[3], PT.free)
                if nk3 > 512:
                    d = PE.mark(PE.after(TL.free).transpose(TL.ap, p3.ap[:, 512:640], ident))
                    TL.free = [act(q3_.ap[:, 512:640], TL.ap, ACT.Copy, d, q3_.free)]
                    ev3 += TL.free
                w3 = min(512, nk3)
                for b_ in range(w3 // 128):
                    ins = nc.tensor.transpose(PT.ap[:, b_ * 128:(b_ + 1) * 128], p3.ap[:, b_ * 128:(b_ + 1) * 128],
                                              ident)
                d = PE.mark(ins)
                PT.free = [act(q3_.ap[:, 0:w3], PT.ap[:, 0:w3], ACT.Copy, d, q3_.free)]
                p3.free = [d]
                g += [q3_, ev3 + PT.free]
            if n < len(items):
                got[n][3] = act(p2.ap[:, 0:nk2], p2.ap[:, 0:nk2], ACT.Exp, t, tn, bias=nm2, accum_out=rs)
            if m >= 0 and i == 7:
                oh = oa[:, :, 64 * hh_:64 * hh_ + 64]
                r = recip(rsum[:, hh_, :], rsum[:, hh_, :], e)
                wide = lambda ap: ap.rearrange("p (t o) -> p t o", o=1).to_broadcast([P, 8, 64])
                o = tt(oh, OUT.ap.rearrange("p (t c) -> p t c", t=8), wide(rsum[:, hh_, :]), ALU.mult, dv, r, oa_free)
                OUT.free = [o]
                t = tt(osq, oh, oh, ALU.mult, o, vg_done[0])
                t = VE.mark(VE.after(t).tensor_reduce(ss2[:, :], osq, AX, ALU.add))
                a = act(ss2[:, :], ss2[:, :], ACT.Sqrt, t, scale=1.0 / 64, bias=EPS)
                t = recip(ss2[:, :], ss2[:, :], a)
                tn = tt(oh, oh, wide(ss2[:, :]), ALU.mult, t)
            if n in (6, 12):
                yield
        d = dv
        qkv_free[s] = [d]
        yield
        PE.after(S.free, TL.free, tn)
        sp = flat(S.ap)
        for i in range(8):
            ins = nc.tensor.transpose(sp[:, i * 128:(i + 1) * 128], oa[:, i, :], ident)
        d = PE.mark(ins)
        oa_free = [d]
        t = act(MX[:, j, :], sp, ACT.Copy, d, xs_kept[j], scale=V("gg2", j))
        S.free = TL.free = [t]
        mx_ready[j] = t

    gr_ = Ring([Slot(gt[:, i, :]) for i in range(2)])
    for q in gr_.slots:
        q.free = [old]

    def group_norm(ks, R8, free, then=None):
        xs = [aux.take(), aux.take()]
        PE.after(xs[0].free, xs[1].free)
        for k in ks:
            q = gr_.take()
            a = act(q.ap, MX[:, 4 + k, :], ACT.Square, mx_ready[4 + k], q.free)
            yield
            PE.after(a)
            for g in range(2):
                ins = nc.tensor.matmul(xs[g].ap[0:8, :], selA4[:, k, :], q.ap[:, g * 512:(g + 1) * 512],
                                       start=(k == ks[0]), stop=(k == ks[-1]))
            d = PE.mark(ins)
            q.free = [d]
        r = []
        for g in range(2):
            R = R8[:, g * 512:(g + 1) * 512]
            a = act(R, xs[g].ap[0:8, :], ACT.Sqrt, d, free, scale=1.0 / 64, bias=EPS)
            xs[g].free = [a]
            r.append(recip(R, R, a))
        for _ in range(5):
            yield
        for k in ks:
            for g in range(2):
                x = aux.take()
                d = PE.mark(PE.after(x.free, r[g]).matmul(x.ap, selB4[:, k, :], R8[:, g * 512:(g + 1) * 512],
                                                          start=True, stop=True))
                y = MX[:, 4 + k, g * 512:(g + 1) * 512]
                t = stt(y, y, V("gg2", 4 + k), x.ap, ALU.mult, ALU.mult, d, mx_ready[4 + k])
                x.free = [t]
            mx_ready[4 + k] = t
            gn_done[0] = [d]
            yield
        if then is not None:
            then()

    gn_done = [None]

    def spatial(ready):
        t = []
        for m in range(2):
            for g in range(2):
                t.append(turn(vg[:, :, 128 * m:128 * (m + 1)], g, ready[m]))
                yield
        for i in range(8):
            b = VE.mark(VE.after(t, old).bn_stats(bst[:, i, :], vg[:, i, :]))
            b = VE.mark(VE.after(b).bn_aggr(bag[:, i, :], bst[:, i, :]))
            if i % 2:
                yield
        b = act(bag[:, :, 1:2], bag[:, :, 1:2], ACT.Sqrt, b, scale=1.0, bias=EPS)
        r = recip(bag[:, :, 1:2], bag[:, :, 1:2], b)
        yield
        for i in range(8):
            t = ts(vg[:, i, :], vg[:, i, :], bag[:, i, 0:1], bag[:, i, 1:2], ALU.subtract, ALU.mult, r)
            t = tt(vg[:, i, :], vg[:, i, :], sgc[:, 0, :], ALU.mult, t, t_sgc)
            t = tt(vg[:, i, :], vg[:, i, :], sgc[:, 1, :], ALU.add, t)
            yield
        for m in range(2):
            for g in range(2):
                x = aux.take()
                PE.after(x.free, t, t_ws)
                for b_ in range(4):
                    for w_ in range(2):
                        ins = nc.tensor.matmul(x.ap[64 * w_:64 * w_ + 64, b_ * 128:(b_ + 1) * 128],
                                               vg[:, 4 * g + b_, (2 * m + w_) * 64:(2 * m + w_ + 1) * 64],
                                               sgw[:, 2 * m + w_, :], start=True, stop=True)
                d = PE.mark(ins)
                q = gr_.take()
                u = q.ap[:, 0:512].rearrange("p (b t) -> p b t", b=4)
                t2 = tt(u, x.ap.rearrange("p (b t) -> p b t", b=4),
                        sgc[:, 2:3, m * 128:(m + 1) * 128].to_broadcast([P, 4, 128]), ALU.add, d, q.free, t_sgc)
                x.free = [t2]
                y = MX[:, 6 + m, g * 512:(g + 1) * 512]
                t2 = tt(y, y, q.ap[:, 0:512], ALU.mult, t2, mx_ready[6 + m])
                q.free = [t2]
                yield
            mx_ready[6 + m] = t2
        vg_done[0] = [d]
        yield from group_norm([2, 3], zb[0:8, 2:], old)

    vg_done = [None]
    ready = []
    for m in range(2):
        pr, d, _ = gemm_fm()
        a = act(vg[:, :, 128 * m:128 * (m + 1)], flat(pr.ap).rearrange("p (t c) -> p t c", t=8), ACT.Gelu, d, old)
        pr.free = [a]
        ready.append(a)
    side = spatial(ready)
    jobs.append(side)
    for m in range(2):
        pr, d, _ = gemm_fm()
        assert xs_kept[6 + m]
        a = act(MX[:, 6 + m, :], flat(pr.ap), ACT.Gelu, d, xs_kept[6 + m])
        pr.free = [a]
        mx_ready[6 + m] = a

    prev = None
    for j in range(4):
        s = j % 2
        pr, d, _ = gemm_fm()
        tq = act(qa[:, s, :], flat(pr.ap), ACT.Copy, d, qkv_free[s], scale=0.125)
        pr.free = [tq]
        pr, d, _ = gemm_fm()
        tk = act(ka[:, s, :], flat(pr.ap), ACT.Copy, d, qkv_free[s])
        pr.free = [tk]
        pr, d, _ = gemm_fm()
        tv = act(va[:, s, :], flat(pr.ap), ACT.Copy, d, qkv_free[s])
        pr.free = [tv]
        if j == 0:
            finish(side)
            S.free = TL.free = PT.free = OUT.free = [q.free for q in aux.slots]
            zfree = [zz, gn_done[0]]
        else:
            finish(prev)
        prev = attention(j, s, tq, tk, tv)
        jobs.append(prev)

    def tile_norm(m, then):
        for q in aux.slots:
            q.free = [q.free, S.free, TL.free, PT.free, OUT.free]
        yield from group_norm([m], qa[0:8, 0, :], [qkv_free[0], gn_done[0]], then)

    for m in range(2):
        pr, d, _ = gemm_fm()
        a = act(zb[:, 2:], flat(pr.ap), ACT.Copy, d, zfree)
        pr.free = [a]
        pr, d, _ = gemm_fm()
        z = tt(zb[:, 2:], zb[:, 2:], flat(pr.ap), ALU.mult, d, a)
        pr.free = [z]
        y = MX[:, 4 + m, :]
        c = ts(y, zb[:, 0:T], V("cw2", m), None, ALU.mult, None, z, xs_kept[4 + m])
        for w_ in (1, 2):
            c = stt(y, zb[:, w_:w_ + T], V("cw2", 2 * w_ + m), y, ALU.mult, ALU.add, c)
        zfree = [c]
        pr, d, _ = gemm_fm(last=(m == 1))
        q = gr_.take()
        b = act(q.ap, flat(pr.ap), ACT.Copy, d, q.free)
        pr.free = [b]
        c = tt(y, y, q.ap, ALU.mult, c, b)
        q.free = [c]
        mx_ready[4 + m] = c
        if m == 0:
            jobs.append(tile_norm(0, None))
    drain_jobs()

    def last_tile():
        h_ready[5] = put_h(5, MX[:, 5, :], mx_ready[5])

    for k in (0, 1, 2):
        h_ready[k] = put_h(k, MX[:, k, :], mx_ready[k])
    jobs.append(tile_norm(1, last_tile))
    pump()
    for k in (3, 6, 7, 4):
        h_ready[k] = put_h(k, MX[:, k, :], mx_ready[k])
    h_ready[5] = None
    nxt = (xs0, load(xs0.ap, XS[0], xs0.free, xs_kept[0]))
    duo(order=(0, 1, 2, 3, 6, 7, 4, 5))
    drain_jobs()
    split_m = [list(t) for t in h_ready]
    mix_done = [mx_ready, split_m, qkv_free, oa_free, gn_done, vg_done, zfree, [q.free for q in gr_.slots]]
    s4.close()

    s5 = ExitStack()
    hdh = sb("hdh", [P, 4, T], FR, s5)
    hdl = sb("hdl", [P, 4, T], FR, s5)
    t5 = sb("t5", [P, 6, T], F, s5)
    R5 = sb("R5", [P, T], F, s5)[:, :]
    acc5 = sb("acc5", [P, T], F, s5)[:, :]
    sqr = Ring([Slot(t5[:, i, :]) for i in range(3)])
    tr = Ring([Slot(t5[:, 3 + i, :]) for i in range(3)])
    for q in sqr.slots + tr.slots:
        q.free = [mix_done]
    hd_free4 = [[mix_done] for _ in range(4)]
    hd_ready = [None] * 4


    def fetch_xs(m):
        q = tr.take()
        return q, load(q.ap, XS[m], q.free)

    st = Stats(acc5, sqr, free=[mix_done])
    for m in range(8):
        q, ld = nxt
        if m < 7:
            nxt = fetch_xs(m + 1)
        pr, d, _ = gemm_fm(last=(m == 7))
        t = tt(X[:, m, :], flat(pr.ap), q.ap, ALU.add, d, ld, split_m[m])
        pr.free, q.free = [t], [t]
        x_ready[m] = t
        st.add(X[:, m, :], t, lane=GP if m < 7 else VE, now=m < 7)
    r = st.inverse_root(R5, EPS, mix_done)
    normed(tr, lambda k: V("mlp_g2", k), R5, r)
    duo()

    def mlp(after_last):
        for g in range(8):
            for k in range(4):
                pr, d, _ = gemm_fm(last=(g == 7 and k == 3))
                q = tr.take()
                a = act(q.ap, flat(pr.ap), ACT.Relu, d, q.free)
                pr.free = [a]
                t = tt(q.ap, q.ap, q.ap, ALU.mult, a)
                a = act(hdh[:, k, :], q.ap, ACT.Copy, t, hd_free4[k])
                b = tt(hdl[:, k, :], q.ap, fp(hdh[:, k, :]), ALU.subtract, a)
                q.free = [b]
                hd_ready[k] = [a, b]
            for m2 in range(4):
                i = next_slab()
                for w_ in range(2):
                    m = 2 * m2 + w_
                    pr, d, _ = gemm_fm(src=(hdh, hdl), ready=hd_ready, nk=4, slab=i, base=4 * w_)
                    x_ready[m] = tt(X[:, m, :], X[:, m, :], flat(pr.ap), ALU.add, d, x_ready[m], *h_ready)
                    pr.free = [x_ready[m]]
                    if g == 7:
                        after_last(m)
                w_free[i % 2] = [d]
            for k in range(4):
                hd_free4[k] = [d]
        split_ahead()

    st = Stats(acc5, sqr, free=[st.d])
    mlp(lambda m: st.add(X[:, m, :], x_ready[m], lane=VE))
    r = st.inverse_root(R5, EPS, *h_ready)

    def last_norm(k):
        x_ready[k] = stt(X[:, k, :], X[:, k, :], V("fin_g2", k), R5, ALU.mult, ALU.mult, r, x_ready[k], st.t)
        xs_kept[k] = store(XS[k], X[:, k, :], x_ready[k], xs_kept[k])
        return X[:, k, :], [x_ready[k]], lambda t: None

    put_all(last_norm)
    split3 = [list(t) for t in h_ready]
    b2_done = [xs0.free, x_ready, split3, hd_free4, r, [q.free for q in tr.slots + sqr.slots]]
    s5.close()
    s45.close()

    s6 = ExitStack()
    pre = sb("pre", [P, 2, T + 3], F, s6)
    q3 = sb("q3", [P, 2, T], F, s6)
    k3 = sb("k3", [P, 2, T], F, s6)
    v3 = sb("v3", [P, 2, 8, 129], F, s6)
    o3 = sb("o3", [P, 2, T], F, s6)
    row = sb("row", [4, 2, T], F, s6)
    mp = sb("mp", [4, 8], F, s6)
    uT = sb("uT", [P, 8, 4], F, s6)
    eT = sb("eT", [P, 8, 4], F, s6)
    Pm = sb("Pm", [P, T], F, s6)
    kd3 = sb("kd3", [P, T], F, s6)
    C3 = sb("C3", [P, 8, 129], F, s6)
    h3 = sb("h3", [P, T], F, s6)
    den = sb("den", [P, 2, 8], F, s6)
    bs3 = sb("bs3", [P, 8, 6], F, s6)
    ba3 = sb("ba3", [P, 8, 2], F, s6)
    pb = sb("pb", [P, 2, T], F, s6)
    wp = sb("wp", [P, 4, 128], F, s6)
    shf = kd3[0:4, :]
    Y = B0
    t_wp = load(flat(wp[:, :, :]), A["w_pool"], b2_done)
    z1 = zero(pre[:, :, 0:3], 0.0, b2_done)
    z2 = zero(v3[:, :, :, 128:129], 1.0, b2_done)
    z3 = zero(shf, 0.0, b2_done)
    z4 = zero(C3[:, 0, :], 0.0, b2_done)

    duo()
    i_, f_, a_, u_, w_ = row[:, 0, :], row[:, 1, :], pb[0:4, 0, :], pb[0:4, 1, :], h3[0:4, :]
    pr, d, _ = gemm_fm()
    g1 = act(i_, flat(pr.ap[0:4, :, :]), ACT.Copy, d, b2_done)
    g2 = act(f_, flat(pr.ap[32:36, :, :]), ACT.Copy, d, b2_done)
    pr.free = [g1, g2]
    t = ts(i_, i_, V("b_i")[0:4, :], None, ALU.add, None, g1)
    ti = t
    t = ts(f_, f_, V("b_f")[0:4, :], None, ALU.add, None, g2)
    a = act(a_, f_, ACT.Abs, t)
    a = act(a_, a_, ACT.Exp, a, scale=-1.0)
    a = act(a_, a_, ACT.Ln, a, bias=1.0)
    t = ts(f_, f_, 0.0, None, ALU.min, None, t, a)
    t = tt(f_, f_, a_, ALU.subtract, t)
    t1 = zero(w_, 1.0, b2_done)
    t1 = zero(w_.rearrange("p (c t) -> p c t", c=8)[:, :, 0:1], 0.0, t1)
    ta = VE.mark(VE.after(t, t1).tensor_tensor_scan(a_, w_, f_, 0.0, ALU.mult, ALU.add))
    t = tt(u_, i_, a_, ALU.subtract, ta, ti)
    a8 = a_.rearrange("p (c t) -> p c t", c=8)
    s8 = shf.rearrange("p (c t) -> p c t", c=8)
    t2 = copy(s8[:, 1:8, 0:1], a8[:, 0:7, 127:128], ta, z3)
    tm = VE.mark(VE.after(t, t2).tensor_tensor_scan(i_, shf, u_, 0.0, ALU.add, ALU.max))
    i8 = i_.rearrange("p (c t) -> p c t", c=8)
    t = zero(mp[:, 0:1], 0.0, b2_done)
    t = tt(mp[:, 1:8].rearrange("p (c o) -> p c o", o=1), i8[:, 0:7, 127:128], a8[:, 0:7, 127:128], ALU.add, tm, t)
    t = tt(f_.rearrange("p (c t) -> p c t", c=8), mp[:, :].rearrange("p (c o) -> p c o", o=1).to_broadcast([4, 8, 128]),
           i8, ALU.subtract, t)
    t_si = act(f_, f_, ACT.Exp, t)
    t = tt(w_, a_, i_, ALU.add, tm)
    t = ts(w_, w_, -1.0, 87.0, ALU.mult, ALU.min, t)
    t_em = act(w_, w_, ACT.Exp, t)
    t_nm = ts(i_, i_, -1.0, None, ALU.mult, None, t)
    def gate_columns():
        nonlocal t_uT, t_eT, h3_free
        x = aux.take()
        PE.after(x.free, t_em)
        for c in range(8):
            nc.tensor.transpose(x.ap[:, 4 * c:4 * c + 4], u_[:, c * 128:(c + 1) * 128], ident[0:4, 0:4])
            ins = nc.tensor.transpose(x.ap[:, 64 + 4 * c:68 + 4 * c], w_[:, c * 128:(c + 1) * 128], ident[0:4, 0:4])
        d = PE.mark(ins)
        t_uT = copy(flat(uT[:, :, :]), x.ap[:, 0:32], d, b2_done)
        t_eT = copy(flat(eT[:, :, :]), x.ap[:, 64:96], d, b2_done)
        x.free = [t_eT]
        h3_free = [t_eT]

    t_uT = t_eT = h3_free = None
    selB4r = selB8[0:4, :, :]

    p_free = [[z1], [z1]]
    hd3_free = [[b2_done], [b2_done]]
    Pm_free, kd_free, C_free, den_free = [b2_done], [tm], [z4], [b2_done]
    y_ready = [None] * 8

    def conv4(src, dst, m, free, dfree, scale=None):
        c = ts(dst, src[:, 0:T], V("cw3", m), None, ALU.mult, None, *free, *dfree)
        for w in range(1, 4):
            c = stt(dst, src[:, w:w + T], V("cw3", 8 * w + m), dst, ALU.mult, ALU.add, c)
        a = act(dst, dst, ACT.Silu, c)
        return c, a

    def mlstm(h, s, tq, tk, tv, to):
        nonlocal Pm_free, kd_free, C_free, h3_free
        q, k, v, o = q3[:, s, :], k3[:, s, :], v3[:, s, :, :], o3[:, s, :]
        tv = [tv, turn(v[:, :, 0:128], 0, tv), turn(v[:, :, 0:128], 1, tv)]
        yield
        for g in range(2):
            x = aux.take()
            d = PE.mark(PE.after(x.free, t_nm).matmul(x.ap, selB4r[:, h, :], i_[:, g * 512:(g + 1) * 512],
                                                      start=True, stop=True))
            for c in range(4 * g, 4 * g + 4):
                t = stt(Pm[:, c * 128:(c + 1) * 128], x.ap[:, (c % 4) * 128:(c % 4 + 1) * 128], uT[:, c, h:h + 1],
                        C("tril_neg"), ALU.add, ALU.add, d, t_uT, Pm_free)
            x.free = [t]
            yield
        tp = act(Pm[:, :], Pm[:, :], ACT.Exp, t)
        yield
        for g in range(2):
            x = aux.take()
            PE.after(x.free, tk)
            for c in range(4):
                ins = nc.tensor.transpose(x.ap[:, c * 128:(c + 1) * 128],
                                          k[:, (4 * g + c) * 128:(4 * g + c + 1) * 128], ident)
            d = PE.mark(ins)
            for c in range(4):
                cc = 4 * g + c
                tkd = ts(kd3[:, cc * 128:(cc + 1) * 128], x.ap[:, c * 128:(c + 1) * 128],
                         Pm[:, cc * 128 + 127:cc * 128 + 128], None, ALU.mult, None, d, tp, kd_free)
            x.free = [tkd]
            yield
        for g in range(2):
            x = aux.take()
            PE.after(x.free, tk, tq)
            for c in range(4):
                cc = slice((4 * g + c) * 128, (4 * g + c + 1) * 128)
                ins = nc.tensor.matmul(x.ap[:, c * 128:(c + 1) * 128], k[:, cc], q[:, cc], start=True, stop=True)
            d = PE.mark(ins)
            tw = tt(Pm[:, g * 512:(g + 1) * 512], x.ap, Pm[:, g * 512:(g + 1) * 512], ALU.mult, d, tkd)
            x.free = [tw]
            yield
        for g in range(2):
            x = aux.take()
            d = PE.mark(PE.after(x.free, t_si).matmul(x.ap, selB4r[:, h, :], f_[:, g * 512:(g + 1) * 512],
                                                      start=True, stop=True))
            t = tt(q[:, g * 512:(g + 1) * 512], q[:, g * 512:(g + 1) * 512], x.ap, ALU.mult, d, tw)
            tqs = t
            t2_ = copy(den[:, 0, 4 * g:4 * g + 4].rearrange("p (c o) -> p c o", o=1),
                       x.ap.rearrange("p (c t) -> p c t", c=4)[:, :, 127:128], d, den_free)
            x.free = [t2_]
            yield
        ts_ = t2_
        tc = z4
        tcs = [z4]
        for c in range(7):
            x = aux.take()
            d = PE.mark(PE.after(x.free, tkd, tv).matmul(x.ap[:, 0:129], kd3[:, c * 128:(c + 1) * 128], v[:, c, :],
                                                         start=True, stop=True))
            tc = stt(C3[:, c + 1, :], C3[:, c, :], den[:, 0, c:c + 1], x.ap[:, 0:129], ALU.mult, ALU.add,
                     tc, d, ts_, C_free)
            x.free = [tc]
            tcs.append(tc)
            if c < 6:
                yield
        kd_free = [d]
        for c in range(8):
            x = aux.take()
            cc = slice(c * 128, (c + 1) * 128)
            PE.after(x.free, tw, tqs, tcs[c], tv)
            nc.tensor.matmul(x.ap[:, 0:129], Pm[:, cc], v[:, c, :], start=True, stop=False)
            d = PE.mark(nc.tensor.matmul(x.ap[:, 0:129], q[:, cc], C3[:, c, :], start=False, stop=True))
            dn = den[:, 1, c:c + 1]
            t = ts(dn, x.ap[:, 128:129], -1.0, None, ALU.mult, None, d)
            t = tt(dn, x.ap[:, 128:129], dn, ALU.max, t)
            t = tt(dn, dn, eT[:, c, h:h + 1], ALU.max, t, t_eT)
            t = recip(dn, dn, t)
            t = ts(h3[:, cc], x.ap[:, 0:128], dn, None, ALU.mult, None, t, h3_free)
            x.free = [t]
            t = VE.mark(VE.after(t).bn_stats(bs3[:, c, :], h3[:, cc]))
            t2 = VE.mark(VE.after(t).bn_aggr(ba3[:, c, :], bs3[:, c, :]))
            if c < 7:
                yield
        Pm_free, C_free = [d], [d]
        a = act(ba3[:, :, 1:2], ba3[:, :, 1:2], ACT.Sqrt, t2, scale=1.0, bias=LN_EPS)
        r = recip(ba3[:, :, 1:2], ba3[:, :, 1:2], a)
        for c in range(8):
            cc = slice(c * 128, (c + 1) * 128)
            t = ts(h3[:, cc], h3[:, cc], ba3[:, c, 0:1], ba3[:, c, 1:2], ALU.subtract, ALU.mult, r)
        yield
        yield
        yield
        yield
        for g in range(2):
            x = aux.take()
            PE.after(x.free, t)
            for c in range(4):
                ins = nc.tensor.transpose(x.ap[:, c * 128:(c + 1) * 128],
                                          h3[:, (4 * g + c) * 128:(4 * g + c + 1) * 128], ident)
            d = PE.mark(ins)
            ty = stt(Y[:, h, g * 512:(g + 1) * 512], x.ap, V("hn_g", h), o[:, g * 512:(g + 1) * 512],
                     ALU.mult, ALU.mult, d, to, xs_kept[h], split3[h])
            x.free = [ty]
            yield
        h3_free = [d]
        hd3_free[s] = [d, ty, tqs, tc]
        y_ready[h] = ty

    prev = None
    pn = 0
    for h in range(4):
        s = h % 2
        out = []
        for m, dst in ((h, q3[:, s, :]), (4 + h, k3[:, s, :])):
            pz = pre[:, pn % 2, :]
            pr, d, _ = gemm_fm()
            a = act(pz[:, 3:], flat(pr.ap), ACT.Copy, d, p_free[pn % 2])
            pr.free = [a]
            c, a = conv4(pz, dst, m, [a, z1], hd3_free[s])
            p_free[pn % 2] = [c]
            pn += 1
            out.append(a)
        tq = out[0]
        tk = ts(k3[:, s, :], k3[:, s, :], 128.0 ** -0.5, None, ALU.mult, None, out[1])
        pr, d, _ = gemm_fm()
        tv = act(v3[:, s, :, 0:128], flat(pr.ap).rearrange("p (t c) -> p t c", t=8), ACT.Copy, d, hd3_free[s], z2)
        pr.free = [tv]
        if h == 0:
            gate_columns()
        pr, d, _ = gemm_fm()
        to = act(o3[:, s, :], flat(pr.ap), ACT.Sigmoid, d, hd3_free[s])
        pr.free = [to]
        if prev is not None:
            finish(prev)
        prev = mlstm(h, s, tq, tk, tv, to)
        jobs.append(prev)

    pbs = [Slot(pb[:, 0, :]), Slot(pb[:, 1, :])]
    for q in pbs:
        q.free = [t_uT, t_eT]
    for g in range(4):
        pr, d, _ = gemm_fm(last=(g == 3))
        y = Y[:, 4 + g, :]
        t0 = act(y, flat(pr.ap), ACT.Copy, d, xs_kept[4 + g], split3[4 + g])
        pr.free = [t0]
        src, ts0 = y, [t0]
        for w in range(g + 1):
            n = 2 ** w
            q = pbs[w % 2]
            t1 = copy(q.ap[:, 0:n], src[:, 0:n], ts0, q.free)
            t2 = tt(q.ap[:, n:], src[:, n:], src[:, 0:T - n], ALU.add, ts0, q.free)
            ts0 = [t1, t2]
            if w:
                pbs[(w - 1) % 2].free = [t1, t2]
            src = q.ap
        win = 2 ** (g + 1)
        t3 = tt(src[:, 0:win], src[:, 0:win], C("inv")[:, 0:win], ALU.mult, ts0)
        t4 = stt(y[:, 0:win], y[:, 0:win], -1.0, src[:, 0:win], ALU.mult, ALU.add, t3)
        t5_ = stt(y[:, win:], src[:, win:], 1.0 / win, y[:, win:], ALU.mult, ALU.subtract, ts0)
        q.free = [t4, t5_]
        y_ready[4 + g] = [t4, t5_]
    finish(prev)
    for g in range(4):
        for j in range(2):
            x = aux.take()
            yj = Y[:, 4 + g, j * 512:(j + 1) * 512]
            d = PE.mark(PE.after(x.free, y_ready[4 + g], t_wp).matmul(x.ap, wp[:, g, :], yj, start=True, stop=True))
            t = act(yj, x.ap, ACT.Copy, d, scale=V("pscale", g))
            x.free = [t]
        y_ready[4 + g] = t
    for k in range(8):
        h_ready[k] = put_h(k, Y[:, k, :], y_ready[k])
    split_y = [list(t) for t in h_ready]
    mix_done = [y_ready, split_y, hd3_free, Pm_free, kd_free, h3_free, p_free, t_uT, t_eT, t_si,
                [q.free for q in pbs], [q.free for q in aux.slots]]
    s6.close()

    s7 = ExitStack()
    hdh = sb("hdh3", [P, 4, T], FR, s7)
    hdl = sb("hdl3", [P, 4, T], FR, s7)
    t7 = sb("t7", [P, 6, T], F, s7)
    R7 = sb("R7", [P, T], F, s7)[:, :]
    acc7 = sb("acc7", [P, T], F, s7)[:, :]
    sqr = Ring([Slot(t7[:, i, :]) for i in range(3)])
    tr = Ring([Slot(t7[:, 3 + i, :]) for i in range(3)])
    for q in sqr.slots + tr.slots:
        q.free = [mix_done]
    hd_free4 = [[mix_done] for _ in range(4)]

    def layer_norm(sm, g, b, use):
        _, t = sm.by_token(ACT.Copy, scale=1.0 / 1024)
        r = spread(R7, 0, t, mix_done)
        st = Stats(acc7, sqr, 1, free=[sm.d])
        for k in range(8):
            x_ready[k] = tt(X[:, k, :], X[:, k, :], R7, ALU.subtract, r, x_ready[k], sm.t)
            st.add(X[:, k, :], x_ready[k], lane=GP if k in (1, 3, 5) else VE)
        r = st.inverse_root(R7, LN_EPS, x_ready)

        def make(k):
            t = stt(X[:, k, :], X[:, k, :], V(g, k), R7, ALU.mult, ALU.mult, r, x_ready[k])
            x_ready[k] = act(X[:, k, :], X[:, k, :], ACT.Identity, t, bias=V(b, k))
            return X[:, k, :], [x_ready[k]], lambda t: None

        if use is None:
            put_all(make)
        else:
            for k in range(8):
                make(k)
                use(k)
        return st

    sm = Stats(acc7, None, 0, raw=True, free=[mix_done])
    nxt = fetch_xs(0)
    duo()
    for m in range(8):
        q, ld = nxt
        if m < 7:
            nxt = fetch_xs(m + 1)
        pr, d, _ = gemm_fm(last=(m == 7))
        x_ready[m] = stt(X[:, m, :], q.ap, ALPHA, flat(pr.ap), ALU.mult, ALU.add, d, ld, split_y[m])
        pr.free, q.free = [x_ready[m]], [x_ready[m]]
        sm.add(X[:, m, :], x_ready[m], lane=GP if m < 7 else VE)

    st = layer_norm(sm, "ln1_g", "ln1_b", None)
    for k in range(8):
        x_ready[k] = ts(X[:, k, :], X[:, k, :], ALPHA, None, ALU.mult, None, h_ready[k])
    duo()
    sm2 = Stats(acc7, None, 0, raw=True, free=[st.d])
    mlp(lambda m: sm2.add(X[:, m, :], x_ready[m], lane=VE))
    layer_norm(sm2, "ln2_g", "ln2_b", lambda k: store(A["out"][k], X[:, k, :], x_ready[k]))
    SP.after(*stores)


def slabs(I):
    def cut(w, cols):
        return [w[:, c:c + 128].reshape(8, 128, 128).transpose(1, 0, 2).reshape(128, 1024) for c in cols]

    def mlp(up, down):
        out = []
        for g in range(8):
            out += cut(up, [512 * g + 128 * k for k in range(4)])
            d = down[512 * g:512 * (g + 1)].reshape(4, 128, 4, 2, 128).transpose(2, 1, 3, 0, 4)
            out += [d[m].reshape(128, 1024) for m in range(4)]
        return out

    out = []
    w = I["w_in"][0]
    for h in range(8):
        out += cut(w, [4096 + 128 * h, 3072 + 128 * h, 5120 + 128 * h])
    out += cut(w, [8192 + 128 * m for m in range(8)])
    for m in range(8):
        out += cut(w, [128 * m, 1024 + 128 * m, 6144 + 128 * m, 2048 + 128 * m])
    out += cut(w, [7168 + 128 * m for m in range(8)])
    for name in ("w_rec_out", "w_conv_out", "w_out"):
        out += cut(I[name][0], [128 * m for m in range(8)])
    w = I["w_in_2"][0]
    out += cut(w, [2560, 2688, 2304, 2432])
    for j in range(4):
        out += cut(w, [128 * j, 512 + 128 * j, 1024 + 128 * j])
    for m in range(2):
        out += cut(w, [1792 + 128 * m, 2048 + 128 * m, 1536 + 128 * m])
    out += cut(I["w_out_2"][0], [128 * m for m in range(8)])
    out += mlp(I["w_up_2"][0], I["w_down_2"][0])
    w = I["w_in_3"][0]
    g = np.zeros((1024, 128), np.float32)
    g[:, 0:4] = w[:, 1536:1540]
    g[:, 32:36] = w[:, 1540:1544]
    out += cut(g, [0])
    for h in range(4):
        out += cut(w, [128 * h, 512 + 128 * h, 1024 + 128 * h, 1544 + 128 * h])
    out += cut(w, [2056 + 128 * g for g in range(4)])
    out += cut(I["w_out_3"][0], [128 * m for m in range(8)])
    out += mlp(I["w_ff1_3"][0], I["w_ff2_3"][0])
    return out


def consts():
    cst = np.zeros((128, NCONST), np.float32)

    def put(name, a):
        c0, w = CONSTS[name]
        cst[:a.shape[0], c0:c0 + w] = a.reshape(a.shape[0], -1)

    put("ident", np.eye(128, dtype=np.float32))
    put("ones", np.ones((128, 128), np.float32))
    a = np.zeros((128, 8, 8), np.float32)
    b = np.zeros((8, 8, 128), np.float32)
    for h in range(8):
        a[:, h, h] = 1
        b[h, h, :] = 1
    put("selA8", a)
    put("selB8", b)
    a = np.zeros((128, 4, 8), np.float32)
    b = np.zeros((8, 4, 128), np.float32)
    for t in range(4):
        a[:64, t, 2 * t] = 1
        a[64:, t, 2 * t + 1] = 1
        b[2 * t, t, :64] = 1
        b[2 * t + 1, t, 64:] = 1
    put("selA4", a)
    put("selB4", b)
    s, t = np.arange(128)[:, None], np.arange(128)[None, :]
    put("inv", np.broadcast_to((1.0 / np.arange(1, 17)).astype(np.float32), (128, 16)))
    put("tri", (s <= t).astype(np.float32))
    put("tril_neg", np.where(s <= t, 0, NEG).astype(np.float32))
    masks = np.stack([((s // (2 * h) == t // (2 * h)) & (s % (2 * h) < h) & (t % (2 * h) >= h))
                      for h in HALVES], 1).astype(np.float32)
    return cst, np.ascontiguousarray(masks.reshape(128, -1))


def vectors(I):
    v = np.zeros((128, NVEC), np.float32)

    def put(name, a):
        c0, w = VECS[name]
        v[:, c0:c0 + w] = a.reshape(w, 128).T

    put("norm_g", I["norm_g"])
    put("conv_w", I["conv_w"])
    put("conv_b", I["conv_b"])
    put("ln_g", I["ln_g"])
    put("ln_b", I["ln_b"])
    put("lb0", I["lb_logits"][0])
    put("lb1", I["lb_logits"][1])
    put("gnorm_g", I["gnorm_g"])
    put("final_g", I["final_g"])
    put("mix_g", I["mix_norm_g_2"])
    put("cw2", I["conv_w_2"])
    put("gg2", I["group_norm_g_2"])
    put("mlp_g2", I["mlp_norm_g_2"])
    put("fin_g2", I["final_norm_g_2"])
    put("cw3", I["w_conv_3"])
    put("hn_g", I["hn_g_3"])
    put("pscale", I["pool_scale_3"])
    put("ln1_g", I["ln1_g_3"])
    put("ln1_b", I["ln1_b_3"])
    put("ln2_g", I["ln2_g_3"])
    put("ln2_b", I["ln2_b_3"])
    v[0:4, VECS["b_i"][0]] = I["b_gate_3"][0, 0:4]
    v[0:4, VECS["b_f"][0]] = I["b_gate_3"][0, 4:8]
    return v


def layout(I):
    x = np.concatenate([I["meta_tokens"], I["x"][0]], 0)
    cst, masks = consts()
    rel = np.clip(np.arange(128)[:, None] + 512 - np.arange(BAND)[None, :], -128, 128) + 128
    bias = I["rel_bias_2"][0][:, rel]
    bias[:, 0:64, BAND - 64:] = NEG
    bias[:, 64:, 0:64] = NEG
    sgc = np.empty((128, 3, 256), np.float32)
    sgc[:, 0, :] = I["sg_ln_g_2"][0]
    sgc[:, 1, :] = I["sg_ln_b_2"][0]
    sgc[:, 2, :] = np.repeat(I["sg_b_2"][0].reshape(2, 2, 128).transpose(1, 0, 2), 64, 0).reshape(128, 256)
    return {
        "w_pool": np.ascontiguousarray(I["w_pool_3"][0].transpose(1, 0, 2).reshape(128, 512)),
        "bias": bias,
        "sgw": np.ascontiguousarray(I["sg_w_2"][0].transpose(2, 0, 1).reshape(128, 512)),
        "sgc": sgc.reshape(128, 768),
        "xin": np.ascontiguousarray(x.T.reshape(8, 128, TM)),
        "wts": np.stack(slabs(I)),
        "vec": vectors(I),
        "cst": cst,
        "masks": masks,
    }


_INS = ("xin", "wts", "vec", "cst", "masks", "bias", "sgw", "sgc", "w_pool")


def kernel(**inputs):
    import concourse.bacc as bacc
    from concourse.bass_utils import run_bass_kernel_spmd

    laid = layout({k: np.asarray(v) for k, v in inputs.items()})
    nc = bacc.Bacc("TRN2", target_bir_lowering=False, num_devices=1)
    arrays, A = {}, {}
    for name in _INS:
        a = np.ascontiguousarray(laid[name])
        arrays["in_" + name] = a
        A[name] = nc.dram_tensor("in_" + name, a.shape, F, kind="ExternalInput").ap()
    A["out"] = nc.dram_tensor("out_y", [KT, P, T], F, kind="ExternalOutput").ap()
    program(nc, A)
    r = run_bass_kernel_spmd(nc, [arrays], core_ids=[0])
    y = np.asarray(r.results[0]["out_y"])
    return np.ascontiguousarray(y.reshape(D_MODEL, T).T)[None]
```
